# Optimizing a Trainium2 kernel written in Bass

```python
import math
import jax, jax.numpy as jnp
from jax import lax
import numpy as np

D_MODEL = 1024
BATCH = 1
SEQ = 256
DEPTH = 1

N_META = 16
S5_WIDTH = D_MODEL // 2
S5_GROUP = 16
S5_GROUPS = S5_WIDTH // S5_GROUP
S5_STATE = 64
DT_MIN = 1e-3
DT_MAX = 1e-1
M_HEADS = 4
M_DK = D_MODEL // 8
M_DV = D_MODEL // 4
M_QK_WIDTH = M_HEADS * M_DK
M_V_WIDTH = M_HEADS * M_DV
M_CHUNK = 64
CONV_WIDTH = 4
D_FF = 4 * D_MODEL
ALPHA = (2.0 * DEPTH) ** 0.25
BETA = (8.0 * DEPTH) ** -0.25
LN_EPS = 1e-5
IN_SIZES = (S5_WIDTH, M_QK_WIDTH, M_QK_WIDTH, M_V_WIDTH, M_V_WIDTH, M_HEADS, M_HEADS, D_MODEL, D_MODEL)
IN_WIDTH = sum(IN_SIZES)
F_GATE_OFFSET = S5_WIDTH + 2 * M_QK_WIDTH + 2 * M_V_WIDTH + M_HEADS


def _layer_norm(x, g, b):
    xf = x.astype(jnp.float32)
    mu = jnp.mean(xf, axis=-1, keepdims=True)
    var = jnp.mean(jnp.square(xf - mu), axis=-1, keepdims=True)
    y = (xf - mu) * lax.rsqrt(var + LN_EPS)
    return (y * g.astype(jnp.float32) + b.astype(jnp.float32)).astype(x.dtype)

def _head_norm(h, g):
    hf = h.astype(jnp.float32)
    mu = jnp.mean(hf, axis=-1, keepdims=True)
    var = jnp.mean(jnp.square(hf - mu), axis=-1, keepdims=True)
    return (hf - mu) * lax.rsqrt(var + LN_EPS) * g.astype(jnp.float32).reshape(M_HEADS, M_DV)

def _split_columns(p):
    parts, start = [], 0
    for size in IN_SIZES:
        parts.append(p[..., start:start + size])
        start += size
    return parts

def _causal_depthwise_conv(x, w, b):
    c = x.shape[-1]
    y = lax.conv_general_dilated(
        x, w[:, None, :].astype(x.dtype), window_strides=(1,),
        padding=((CONV_WIDTH - 1, 0),), dimension_numbers=("NWC", "WIO", "NWC"),
        feature_group_count=c)
    return y + b

def _linear_recurrence_combine(left, right):
    a_l, b_l = left
    a_r, b_r = right
    return a_l * a_r, a_r * b_l + b_r

def _s5_mixer(u, lam_re, lam_im, log_dt, b_re, b_im, c_re, c_im, d_skip):
    f32 = jnp.float32
    bsz, length, _ = u.shape
    uf = u.astype(f32).reshape(bsz, length, S5_GROUPS, S5_GROUP)
    lam = lax.complex(lam_re.astype(f32), lam_im.astype(f32))
    dt = jnp.exp(log_dt.astype(f32))[:, None]
    lam_bar = jnp.exp(lam * dt)
    b_mat = lax.complex(b_re.astype(f32), b_im.astype(f32))
    b_bar = ((lam_bar - 1.0) / lam)[..., None] * b_mat
    bu = jnp.einsum("gph,blgh->blgp", b_bar, uf.astype(jnp.complex64))
    a = jnp.broadcast_to(lam_bar, (1, length, S5_GROUPS, S5_STATE))
    _, state = lax.associative_scan(_linear_recurrence_combine, (a, bu), axis=1)
    c_mat = lax.complex(c_re.astype(f32), c_im.astype(f32))
    y = jnp.real(jnp.einsum("ghp,blgp->blgh", c_mat, state))
    y = y + d_skip.astype(f32).reshape(S5_GROUPS, S5_GROUP) * uf
    return y.reshape(bsz, length, S5_WIDTH)

def _mlstm_mixer(q, k, v, i_pre, f_pre):
    f32 = jnp.float32
    bsz, length = q.shape[:2]
    n_pad = M_CHUNK - N_META
    n_chunks = (length + n_pad) // M_CHUNK

    def to_chunks(t, fill):
        t = t.astype(f32)
        t = jnp.pad(t, ((0, 0), (n_pad, 0)) + ((0, 0),) * (t.ndim - 2), constant_values=fill)
        t = t.reshape((bsz, n_chunks, M_CHUNK) + t.shape[2:])
        return jnp.moveaxis(t, (1, 3), (0, 2))

    qc = to_chunks(q, 0.0)
    kc = to_chunks(k * (M_DK ** -0.5), 0.0)
    vc = to_chunks(v, 0.0)
    log_i = to_chunks(i_pre, -jnp.inf)
    log_f = to_chunks(jax.nn.log_sigmoid(f_pre.astype(f32)), 0.0)
    causal = jnp.tril(jnp.ones((M_CHUNK, M_CHUNK), dtype=bool))

    def chunk_step(carry, inp):
        c_st, n_st, m_st = carry
        q_c, k_c, v_c, li_c, lf_c = inp
        b = jnp.cumsum(lf_c, axis=-1)
        d_mat = jnp.where(causal, b[..., :, None] - b[..., None, :] + li_c[..., None, :], -jnp.inf)
        m_inter = b + m_st[..., None]
        m_row = jnp.maximum(m_inter, jnp.max(d_mat, axis=-1))
        w_intra = jnp.exp(d_mat - m_row[..., None])
        w_inter = jnp.exp(m_inter - m_row)
        s = jnp.einsum("bhsd,bhjd->bhsj", q_c, k_c) * w_intra
        num = (jnp.einsum("bhsj,bhje->bhse", s, v_c)
               + w_inter[..., None] * jnp.einsum("bhsd,bhde->bhse", q_c, c_st))
        den = jnp.sum(s, axis=-1) + w_inter * jnp.einsum("bhsd,bhd->bhs", q_c, n_st)
        h_c = num / jnp.maximum(jnp.abs(den), jnp.exp(-m_row))[..., None]
        b_last = b[..., -1]
        g_log = b_last[..., None] - b + li_c
        m_new = jnp.maximum(b_last + m_st, jnp.max(g_log, axis=-1))
        w_k = jnp.exp(g_log - m_new[..., None])
        decay = jnp.exp(b_last + m_st - m_new)
        c_new = decay[..., None, None] * c_st + jnp.einsum("bhj,bhjd,bhje->bhde", w_k, k_c, v_c)
        n_new = decay[..., None] * n_st + jnp.einsum("bhj,bhjd->bhd", w_k, k_c)
        return (c_new, n_new, m_new), h_c

    init = (jnp.zeros((bsz, M_HEADS, M_DK, M_DV), f32),
            jnp.zeros((bsz, M_HEADS, M_DK), f32),
            jnp.zeros((bsz, M_HEADS), f32))
    _, h = lax.scan(chunk_step, init, (qc, kc, vc, log_i, log_f))
    h = jnp.moveaxis(h, (0, 2), (1, 3)).reshape(bsz, n_chunks * M_CHUNK, M_HEADS, M_DV)
    return h[:, n_pad:]

def first_inputs(seed: int = 0) -> dict:
    key = jax.random.key(seed)
    ks = jax.random.split(key, 27)
    f32 = jnp.float32

    def nrm(k, shape, scale):
        return scale * jax.random.normal(k, shape, f32)

    b_in = nrm(ks[5], (DEPTH, IN_WIDTH), 0.02)
    b_in = b_in.at[:, F_GATE_OFFSET:F_GATE_OFFSET + M_HEADS].add(jnp.linspace(3.0, 6.0, M_HEADS))
    s5_lambda_re = -0.5 + nrm(ks[8], (DEPTH, S5_GROUPS, S5_STATE), 0.01)
    s5_lambda_im = jnp.pi * jnp.arange(S5_STATE, dtype=f32) + nrm(ks[9], (DEPTH, S5_GROUPS, S5_STATE), 0.01)
    s5_log_dt = jax.random.uniform(ks[10], (DEPTH, S5_GROUPS), f32, math.log(DT_MIN), math.log(DT_MAX))
    return {
        "x": nrm(ks[0], (BATCH, SEQ, D_MODEL), 1.0),
        "meta_tokens": nrm(ks[1], (N_META, D_MODEL), 1.0),
        "ln0_g": 1.0 + nrm(ks[2], (D_MODEL,), 0.05),
        "ln0_b": nrm(ks[3], (D_MODEL,), 0.02),
        "w_in": nrm(ks[4], (DEPTH, D_MODEL, IN_WIDTH), D_MODEL ** -0.5),
        "b_in": b_in,
        "qk_conv_w": nrm(ks[6], (DEPTH, CONV_WIDTH, 2 * M_QK_WIDTH), CONV_WIDTH ** -0.5),
        "qk_conv_b": nrm(ks[7], (DEPTH, 2 * M_QK_WIDTH), 0.02),
        "s5_lambda_re": s5_lambda_re,
        "s5_lambda_im": s5_lambda_im,
        "s5_log_dt": s5_log_dt,
        "s5_b_re": nrm(ks[11], (DEPTH, S5_GROUPS, S5_STATE, S5_GROUP), (2.0 * S5_GROUP) ** -0.5),
        "s5_b_im": nrm(ks[12], (DEPTH, S5_GROUPS, S5_STATE, S5_GROUP), (2.0 * S5_GROUP) ** -0.5),
        "s5_c_re": nrm(ks[13], (DEPTH, S5_GROUPS, S5_GROUP, S5_STATE), S5_STATE ** -0.5),
        "s5_c_im": nrm(ks[14], (DEPTH, S5_GROUPS, S5_GROUP, S5_STATE), S5_STATE ** -0.5),
        "s5_d": nrm(ks[15], (DEPTH, S5_WIDTH), 1.0),
        "s5_w_glu": nrm(ks[16], (DEPTH, S5_WIDTH, 2 * D_MODEL), S5_WIDTH ** -0.5),
        "m_norm_g": 1.0 + nrm(ks[17], (DEPTH, M_V_WIDTH), 0.05),
        "m_w_out": nrm(ks[18], (DEPTH, M_V_WIDTH, D_MODEL), M_V_WIDTH ** -0.5),
        "w_o": nrm(ks[19], (DEPTH, D_MODEL, D_MODEL), BETA * D_MODEL ** -0.5),
        "ln1_g": 1.0 + nrm(ks[20], (DEPTH, D_MODEL), 0.05),
        "ln1_b": nrm(ks[21], (DEPTH, D_MODEL), 0.02),
        "w_up": nrm(ks[22], (DEPTH, D_MODEL, D_FF), D_MODEL ** -0.5),
        "b_up": nrm(ks[23], (DEPTH, D_FF), 0.02),
        "w_down": nrm(ks[24], (DEPTH, D_FF, D_MODEL), BETA * D_FF ** -0.5),
        "ln2_g": 1.0 + nrm(ks[25], (DEPTH, D_MODEL), 0.05),
        "ln2_b": nrm(ks[26], (DEPTH, D_MODEL), 0.02),
    }

def first_block(x, meta_tokens, ln0_g, ln0_b, w_in, b_in, qk_conv_w, qk_conv_b,
              s5_lambda_re, s5_lambda_im, s5_log_dt, s5_b_re, s5_b_im, s5_c_re, s5_c_im,
              s5_d, s5_w_glu, m_norm_g, m_w_out, w_o, ln1_g, ln1_b, w_up, b_up, w_down,
              ln2_g, ln2_b):
    bsz = x.shape[0]
    meta = jnp.broadcast_to(meta_tokens[None].astype(x.dtype), (bsz, N_META, D_MODEL))
    h = _layer_norm(jnp.concatenate([meta, x], axis=1), ln0_g, ln0_b)
    length = h.shape[1]
    for layer in range(DEPTH):
        p = h @ w_in[layer] + b_in[layer]
        u_s5, q, k, v, o_pre, i_pre, f_pre, g_s5, g_m = _split_columns(p)
        y_s5 = _s5_mixer(u_s5, s5_lambda_re[layer], s5_lambda_im[layer], s5_log_dt[layer],
                         s5_b_re[layer], s5_b_im[layer], s5_c_re[layer], s5_c_im[layer], s5_d[layer])
        z = jax.nn.gelu(y_s5).astype(h.dtype) @ s5_w_glu[layer]
        y_s5 = z[..., :D_MODEL] * jax.nn.sigmoid(z[..., D_MODEL:])
        qk = jax.nn.silu(_causal_depthwise_conv(jnp.concatenate([q, k], axis=-1),
                                                qk_conv_w[layer], qk_conv_b[layer]))
        q_h = qk[..., :M_QK_WIDTH].reshape(bsz, length, M_HEADS, M_DK)
        k_h = qk[..., M_QK_WIDTH:].reshape(bsz, length, M_HEADS, M_DK)
        v_h = v.reshape(bsz, length, M_HEADS, M_DV)
        hm = _mlstm_mixer(q_h, k_h, v_h, i_pre, f_pre)
        hm = _head_norm(hm, m_norm_g[layer]).reshape(bsz, length, M_V_WIDTH).astype(h.dtype)
        y_m = (jax.nn.sigmoid(o_pre) * hm) @ m_w_out[layer]
        mix = jax.nn.sigmoid(g_s5) * y_s5 + jax.nn.sigmoid(g_m) * y_m
        h = _layer_norm(ALPHA * h + mix @ w_o[layer], ln1_g[layer], ln1_b[layer])
        ff = jnp.square(jax.nn.relu(h @ w_up[layer] + b_up[layer])) @ w_down[layer]
        h = _layer_norm(ALPHA * h + ff, ln2_g[layer], ln2_b[layer])
    return h[:, N_META:]


MIX_WIDTH = D_MODEL
MOBA_HEAD_DIM = 64
MOBA_WIDTH = MIX_WIDTH // 2
MOBA_HEADS = MOBA_WIDTH // MOBA_HEAD_DIM
MOBA_BLOCK = 256
MOBA_TOPK = 3
MOBA_Q_CHUNK = 64
GDN_HEAD_DIM = 128
GDN_WIDTH = MIX_WIDTH - MOBA_WIDTH
GDN_HEADS = GDN_WIDTH // GDN_HEAD_DIM
GDN_CONV = 4
GDN_CHUNK = 64
N_GROUPS = 4
EXPERTS_PER_GROUP = 8
EXPERT_TOPK = 2
EXPERT_FF = D_MODEL // 4
RMS_EPS = 1e-6
IN_SPLITS = (MOBA_WIDTH, MOBA_WIDTH, MOBA_WIDTH, 3 * GDN_WIDTH, GDN_WIDTH, GDN_HEADS, GDN_HEADS)
IN_PROJ_WIDTH = 3 * MOBA_WIDTH + 4 * GDN_WIDTH + 2 * GDN_HEADS


def rmsnorm(x, gain):
    x32 = x.astype(jnp.float32)
    y = x32 * lax.rsqrt(jnp.mean(x32 * x32, axis=-1, keepdims=True) + RMS_EPS)
    return (y * gain.astype(jnp.float32)).astype(x.dtype)

def l2norm(x):
    return x * lax.rsqrt(jnp.sum(x * x, axis=-1, keepdims=True) + 1e-6)

def moba_attention(q, k, v):
    B, S, H, Dh = q.shape
    nb = -(-S // MOBA_BLOCK)
    pad = nb * MOBA_BLOCK - S
    topk = min(MOBA_TOPK, nb)
    scale = Dh ** -0.5
    q = q.transpose(0, 2, 1, 3)
    kp = jnp.pad(k.transpose(0, 2, 1, 3), ((0, 0), (0, 0), (0, pad), (0, 0)))
    vp = jnp.pad(v.transpose(0, 2, 1, 3), ((0, 0), (0, 0), (0, pad), (0, 0)))
    kb = kp.reshape(B, H, nb, MOBA_BLOCK, Dh)
    vb = vp.reshape(B, H, nb, MOBA_BLOCK, Dh)
    k_mean = jnp.mean(kb.astype(jnp.float32), axis=3)
    b_idx = jnp.arange(B)[:, None, None, None]
    h_idx = jnp.arange(H)[None, :, None, None]
    blk_ids = jnp.arange(nb)
    n_chunks = S // MOBA_Q_CHUNK

    def chunk(c):
        start = c * MOBA_Q_CHUNK
        qc = lax.dynamic_slice_in_dim(q, start, MOBA_Q_CHUNK, axis=2)
        qpos = start + jnp.arange(MOBA_Q_CHUNK)
        own = start // MOBA_BLOCK
        gate = jnp.einsum('bhqd,bhnd->bhqn', qc.astype(jnp.float32), k_mean)
        gate = jnp.where(blk_ids < own, gate, -jnp.inf)
        _, gidx = lax.top_k(gate, topk)
        sel_ok = jnp.arange(topk) < own
        k_sel = kb[b_idx, h_idx, gidx]
        v_sel = vb[b_idx, h_idx, gidx]
        s_sel = jnp.einsum('bhqd,bhqkld->bhqkl', qc, k_sel).astype(jnp.float32) * scale
        s_sel = jnp.where(sel_ok[:, None], s_sel, -jnp.inf)
        k_own = lax.dynamic_slice_in_dim(kb, own, 1, axis=2)[:, :, 0]
        v_own = lax.dynamic_slice_in_dim(vb, own, 1, axis=2)[:, :, 0]
        s_own = jnp.einsum('bhqd,bhld->bhql', qc, k_own).astype(jnp.float32) * scale
        kpos = own * MOBA_BLOCK + jnp.arange(MOBA_BLOCK)
        s_own = jnp.where(kpos[None, :] <= qpos[:, None], s_own, -jnp.inf)
        s = jnp.concatenate([s_sel.reshape(B, H, MOBA_Q_CHUNK, topk * MOBA_BLOCK), s_own], axis=-1)
        p = jax.nn.softmax(s, axis=-1).astype(v.dtype)
        p_sel = p[..., :topk * MOBA_BLOCK].reshape(B, H, MOBA_Q_CHUNK, topk, MOBA_BLOCK)
        p_own = p[..., topk * MOBA_BLOCK:]
        return (jnp.einsum('bhqkl,bhqkld->bhqd', p_sel, v_sel)
                + jnp.einsum('bhql,bhld->bhqd', p_own, v_own))

    out = lax.map(chunk, jnp.arange(n_chunks))
    return out.transpose(1, 0, 3, 2, 4).reshape(B, S, H, Dh)

def causal_depthwise_conv(x, w):
    C = x.shape[-1]
    return lax.conv_general_dilated(
        x, w[:, None, :].astype(x.dtype), window_strides=(1,),
        padding=((GDN_CONV - 1, 0),), dimension_numbers=('NWC', 'WIO', 'NWC'),
        feature_group_count=C)

def gated_delta_rule(q, k, v, g, beta):
    B, S, H, Dk = q.shape
    Dv = v.shape[-1]
    C = GDN_CHUNK
    N = S // C

    def to_chunks(t):
        return t.reshape(B, N, C, H, *t.shape[3:]).swapaxes(2, 3)

    q, k, v, g, beta = (to_chunks(t) for t in (q, k, v, g, beta))
    G = jnp.cumsum(g, axis=-1)
    incl = jnp.tril(jnp.ones((C, C), dtype=bool))
    strict = jnp.tril(jnp.ones((C, C), dtype=bool), k=-1)
    decay = jnp.exp(jnp.where(incl, G[..., :, None] - G[..., None, :], -jnp.inf))
    kk = jnp.einsum('bnhid,bnhjd->bnhij', k, k)
    A = jnp.where(strict, beta[..., :, None] * kk * decay, 0.0)
    eye = jnp.eye(C, dtype=A.dtype)
    gam = jnp.exp(G)
    rhs = jnp.concatenate([beta[..., None] * v, (beta * gam)[..., None] * k], axis=-1)
    sol = lax.linalg.triangular_solve(eye + A, rhs, left_side=True, lower=True, unit_diagonal=True)
    u_v, w = sol[..., :Dv], sol[..., Dv:]
    qk = jnp.einsum('bnhid,bnhjd->bnhij', q, k) * decay
    q_dec = q * gam[..., None]
    k_dec = k * jnp.exp(G[..., -1:] - G)[..., None]
    g_last = jnp.exp(G[..., -1])

    def step(state, xs):
        u_v_c, w_c, qk_c, q_dec_c, k_dec_c, g_last_c = xs
        u = u_v_c - jnp.einsum('bhck,bhkv->bhcv', w_c, state)
        o = jnp.einsum('bhck,bhkv->bhcv', q_dec_c, state) + jnp.einsum('bhij,bhjv->bhiv', qk_c, u)
        new_state = g_last_c[..., None, None] * state + jnp.einsum('bhck,bhcv->bhkv', k_dec_c, u)
        return new_state, o

    xs = tuple(t.swapaxes(0, 1) for t in (u_v, w, qk, q_dec, k_dec, g_last))
    state0 = jnp.zeros((B, H, Dk, Dv), dtype=q.dtype)
    _, o = lax.scan(step, state0, xs)
    return o.transpose(1, 0, 3, 2, 4).reshape(B, S, H, Dv)

def hierarchical_moe(h, w_group, w_router, w_gate, w_up, w_down):
    T = h.shape[0]
    group_logits = jnp.einsum('td,dg->tg', h, w_group).astype(jnp.float32)
    group_prob = jax.nn.softmax(group_logits, axis=-1)
    g_sel = jnp.argmax(group_logits, axis=-1)
    p_group = jnp.take_along_axis(group_prob, g_sel[:, None], axis=-1)
    expert_logits = jnp.einsum('td,de->te', h, w_router).astype(jnp.float32)
    expert_logits = expert_logits.reshape(T, N_GROUPS, EXPERTS_PER_GROUP)
    in_group = jnp.take_along_axis(expert_logits, g_sel[:, None, None], axis=1)[:, 0]
    in_prob = jax.nn.softmax(in_group, axis=-1)
    top_p, top_i = lax.top_k(in_prob, EXPERT_TOPK)
    top_p = top_p / jnp.sum(top_p, axis=-1, keepdims=True)
    within = jnp.sum(jax.nn.one_hot(top_i, EXPERTS_PER_GROUP, dtype=jnp.float32) * top_p[..., None], axis=1)
    combine = (jax.nn.one_hot(g_sel, N_GROUPS, dtype=jnp.float32)[:, :, None]
               * p_group[:, :, None] * within[:, None, :]).astype(h.dtype)
    y = jnp.zeros_like(h)
    for grp in range(N_GROUPS):
        hid = (jax.nn.silu(jnp.einsum('td,edf->tef', h, w_gate[grp]))
               * jnp.einsum('td,edf->tef', h, w_up[grp])) * combine[:, grp, :, None]
        y = y + jnp.einsum('tef,efd->td', hid, w_down[grp])
    return y

def second_inputs(seed: int = 0) -> dict:
    key = jax.random.key(seed)
    ks = jax.random.split(key, 16)
    f32 = jnp.float32
    D = D_MODEL
    x = jax.random.normal(ks[0], (BATCH, SEQ, D), f32)
    attn_norm = 1.0 + 0.02 * jax.random.normal(ks[1], (DEPTH, D), f32)
    w_in = jax.random.normal(ks[2], (DEPTH, D, IN_PROJ_WIDTH), f32) * D ** -0.5
    conv_w = jax.random.normal(ks[3], (DEPTH, GDN_CONV, 3 * GDN_WIDTH), f32) * GDN_CONV ** -0.5
    A_log = jnp.log(jax.random.uniform(ks[4], (DEPTH, GDN_HEADS), f32, 1.0, 16.0))
    dt = jnp.exp(jax.random.uniform(ks[5], (DEPTH, GDN_HEADS), f32, np.log(1e-3), np.log(1e-1)))
    dt_bias = dt + jnp.log(-jnp.expm1(-dt))
    gdn_norm = 1.0 + 0.02 * jax.random.normal(ks[6], (DEPTH, GDN_HEAD_DIM), f32)
    w_out = jax.random.normal(ks[7], (DEPTH, MIX_WIDTH, D), f32) * MIX_WIDTH ** -0.5
    ffn_norm = 1.0 + 0.02 * jax.random.normal(ks[8], (DEPTH, D), f32)
    w_group = jax.random.normal(ks[9], (DEPTH, D, N_GROUPS), f32) * D ** -0.5
    w_router = jax.random.normal(ks[10], (DEPTH, D, N_GROUPS * EXPERTS_PER_GROUP), f32) * D ** -0.5
    w_gate = jax.random.normal(ks[11], (DEPTH, N_GROUPS, EXPERTS_PER_GROUP, D, EXPERT_FF), f32) * D ** -0.5
    w_up = jax.random.normal(ks[12], (DEPTH, N_GROUPS, EXPERTS_PER_GROUP, D, EXPERT_FF), f32) * D ** -0.5
    w_down = jax.random.normal(ks[13], (DEPTH, N_GROUPS, EXPERTS_PER_GROUP, EXPERT_FF, D), f32) * EXPERT_FF ** -0.5
    final_norm = 1.0 + 0.02 * jax.random.normal(ks[14], (D,), f32)
    return {'x': x, 'attn_norm': attn_norm, 'w_in': w_in, 'conv_w': conv_w, 'A_log': A_log,
            'dt_bias': dt_bias, 'gdn_norm': gdn_norm, 'w_out': w_out, 'ffn_norm': ffn_norm,
            'w_group': w_group, 'w_router': w_router, 'w_gate': w_gate, 'w_up': w_up,
            'w_down': w_down, 'final_norm': final_norm}

def second_block(x, attn_norm, w_in, conv_w, A_log, dt_bias, gdn_norm, w_out, ffn_norm,
              w_group, w_router, w_gate, w_up, w_down, final_norm):
    B, S, D = x.shape
    offsets = np.cumsum(IN_SPLITS)[:-1].tolist()
    f32 = jnp.float32
    for l in range(DEPTH):
        h = rmsnorm(x, attn_norm[l])
        proj = jnp.einsum('bsd,de->bse', h, w_in[l])
        mq, mk, mv, gqkv, gz, ga, gb = jnp.split(proj, offsets, axis=-1)
        to_a = lambda t: t.reshape(B, S, MOBA_HEADS, MOBA_HEAD_DIM)
        y_a = moba_attention(to_a(mq), to_a(mk), to_a(mv)).reshape(B, S, MOBA_WIDTH)
        gqkv = jax.nn.silu(causal_depthwise_conv(gqkv, conv_w[l]))
        gq, gk, gv = jnp.split(gqkv, 3, axis=-1)
        to_b = lambda t: t.reshape(B, S, GDN_HEADS, GDN_HEAD_DIM).astype(f32)
        gq = l2norm(to_b(gq)) * GDN_HEAD_DIM ** -0.5
        gk = l2norm(to_b(gk))
        log_decay = -jnp.exp(A_log[l].astype(f32)) * jax.nn.softplus(ga.astype(f32) + dt_bias[l].astype(f32))
        beta = jax.nn.sigmoid(gb.astype(f32))
        o_b = gated_delta_rule(gq, gk, to_b(gv), log_decay, beta)
        o_b = rmsnorm(o_b, gdn_norm[l]) * jax.nn.silu(to_b(gz))
        y_b = o_b.reshape(B, S, GDN_WIDTH).astype(x.dtype)
        mix = jnp.concatenate([y_a, y_b], axis=-1)
        x = x + jnp.einsum('bse,ed->bsd', mix, w_out[l])
        h = rmsnorm(x, ffn_norm[l]).reshape(B * S, D)
        y = hierarchical_moe(h, w_group[l], w_router[l], w_gate[l], w_up[l], w_down[l])
        x = x + y.reshape(B, S, D)
    return rmsnorm(x, final_norm)


def setup_inputs(seed=0):
    out = dict(first_inputs(seed))
    for name, value in second_inputs(seed + 1).items():
        if name != "x":
            out[name + "_2"] = value
    return out


def reference(
    x, meta_tokens, ln0_g, ln0_b, w_in, b_in, qk_conv_w, qk_conv_b, s5_lambda_re, s5_lambda_im,
    s5_log_dt, s5_b_re, s5_b_im, s5_c_re, s5_c_im, s5_d, s5_w_glu, m_norm_g, m_w_out, w_o,
    ln1_g, ln1_b, w_up, b_up, w_down, ln2_g, ln2_b, attn_norm_2, w_in_2, conv_w_2, A_log_2,
    dt_bias_2, gdn_norm_2, w_out_2, ffn_norm_2, w_group_2, w_router_2, w_gate_2, w_up_2,
    w_down_2, final_norm_2,
):
    x = first_block(
        x, meta_tokens, ln0_g, ln0_b, w_in, b_in, qk_conv_w, qk_conv_b, s5_lambda_re,
        s5_lambda_im, s5_log_dt, s5_b_re, s5_b_im, s5_c_re, s5_c_im, s5_d, s5_w_glu, m_norm_g,
        m_w_out, w_o, ln1_g, ln1_b, w_up, b_up, w_down, ln2_g, ln2_b,
    )
    return second_block(
        x, attn_norm_2, w_in_2, conv_w_2, A_log_2, dt_bias_2, gdn_norm_2, w_out_2, ffn_norm_2,
        w_group_2, w_router_2, w_gate_2, w_up_2, w_down_2, final_norm_2,
    )


_drawn_inputs = setup_inputs


def setup_inputs(seed=0):
    import zlib

    import numpy as np

    out = dict(_drawn_inputs(seed))
    spreads = {}
    factors = {'qk_conv_b': 4.526,
     's5_lambda_re': 8.0,
     's5_lambda_im': 5.262,
     's5_b_re': 3.906,
     's5_b_im': 4.082,
     's5_c_re': 3.799,
     's5_c_im': 3.537,
     'm_norm_g': 2.924,
     'final_norm_2': 2.859}
    for name, (base, spread) in spreads.items():
        noise = np.random.default_rng([zlib.crc32(name.encode()), seed]).standard_normal(out[name].shape)
        drawn = base * np.exp(spread * noise) if base else spread * noise
        out[name] = __import__('jax').numpy.asarray(drawn.astype(out[name].dtype))
    for name, factor in factors.items():
        out[name] = (out[name] * factor).astype(out[name].dtype)
    return out
```

```python
from contextlib import ExitStack
import math

import concourse.bass as bass
from concourse import mybir

FP32 = mybir.dt.float32
I32 = mybir.dt.int32
ALU = mybir.AluOpType
ACT = mybir.ActivationFunctionType
AX = mybir.AxisListType

P = 128
D = 1024
KT = D // P
SEQ = 256
META = 16
LEN = META + SEQ
TT = SEQ // P
CHUNK = 16
NCH = LEN // CHUNK
S5W, GRP, STATE = 512, 16, 64
NST = (S5W // GRP) * STATE // P
UT = S5W // P
HEADS, DK, DV = 4, 128, 256
FF = 4096
ALPHA = 2.0 ** 0.25
MH, MD = 8, 64
GH, GD = 4, 128
NE, EG, NG, EF = 32, 8, 4, 256
SLOTS = 4
CAP = 128
ROUNDS = SEQ // CAP
BLOCKS = NG * ROUNDS
PROW_DMAS, SMALL_DMAS = 15, 7
LEVELS = 7
NEG = -1.0e30
C_U, C_QK, C_V, C_O, C_I, C_F, C_G = 0, 512, 1536, 2560, 3584, 3588, 3592
C2_MQ, C2_MK, C2_MV, C2_GQKV, C2_GZ, C2_GA, C2_GB = 0, 512, 1024, 1536, 3072, 3584, 3588
TWO_PI_HI, TWO_PI_MID, TWO_PI_LO = 6.28125, 0.0019350051879882812, 3.0199159819567e-07
ROUND = 1.5 * 2.0 ** 23


def stream_plan():
    plan = [("u", 0, 1)]
    plan += [("qk", i, 1) for i in range(2)]
    plan += [("v", i, 1) for i in range(2)]
    plan += [("o", i, 1) for i in range(2)]
    plan += [("g", i, 1) for i in range(4)]
    plan += [("glu", i, 2) for i in range(2)]
    plan += [("mout", i, 1) for i in range(2)]
    plan += [("wo", i, 1) for i in range(2)]
    plan += [("ffn", i, 2) for i in range(FF // 256)]
    plan += [("gqkv", i, 1) for i in range(3)]
    plan += [("mqk", i, 1) for i in range(2)]
    plan += [("gz", 0, 1), ("mv", 0, 1)]
    plan += [("wout", i, 1) for i in range(2)]
    for e in range(NE):
        plan += [("gu", e, 2), ("dn", e, 1)]
    return plan


STREAM = stream_plan()
CHUNK_AT = {(n, i): at for at, (n, i, _) in enumerate(STREAM)}


def loaded_count(at):
    return 16 * sum(d for k, (_, _, d) in enumerate(STREAM[:at + 1]) if k % SLOTS == at % SLOTS)


def bank_plan():
    order = [("prow", 0), ("prow", 1)] + [("xT", t) for t in range(KT)] + [("lam", 0)]
    order += [("u", t) for t in range(UT)] + [("bT", 0), ("bT", 1), ("cT", 0), ("cT", 1)]
    order += [("bu", k) for k in range(2 * NST)]
    order += [("qk", t) for t in range(8)] + [("i", 0), ("f", 0)]
    order += [("v", k) for k in range(6)] + [("o", k) for k in range(4)]
    order += [("g", t) for t in range(16)]
    order += [("y", t) for t in range(UT)] + [("z", t) for t in range(KT)] + [("gm", 0)]
    for h in range(HEADS):
        order += [("ms", h), ("s", h)]
    order += [("h", k) for k in range(2 * HEADS)]
    order += [("oT", t) for t in range(KT)]
    order += [("ym", t) for t in range(KT)] + [("wo", k) for k in range(4)] + [("h1T", t) for t in range(KT)]
    first = plan_from(order, {})
    uses = {}
    for bank, _ in first.values():
        uses[bank] = uses.get(bank, 0) + 1
    order = [("x2T", t) for t in range(KT)] + [("ga", 0), ("gb", 0)] + [("gqkv", t) for t in range(12)]
    order += [("Gc", 0)] + [("mqk", t) for t in range(8)]
    order += [("gz", t) for t in range(2)] + [("mv", t) for t in range(2)]
    order += [("nq", t) for t in range(4)] + [("vk", t) for t in range(2)]
    for h in range(GH):
        order += [("gb_", h), ("kk", h), ("qk_", h)]
    for lv in range(LEVELS):
        order += [("X", lv, 0), ("X", lv, 1), ("sc", lv)] + ([("av", lv - 1)] if lv else [])
        order += [("Z", lv, 0), ("ZT", lv, 0), ("Z", lv, 1), ("ZT", lv, 1), ("pT", lv)]
    order += [("sc", MH - 1), ("av", MH - 2), ("pT", MH - 1), ("av", MH - 1)]
    order += [("U1", 0), ("AU", 0), ("U2", 0), ("O", 0), ("O", 1)] + [("obT", 0), ("obT", 1)]
    order += [("wout", k) for k in range(4)] + [("x3T", t) for t in range(KT)] + [("rt", 0), ("rt", 1), ("cum", 0), ("comb", 0)] + [("sT", b) for b in range(4)]
    second = plan_from(order, uses)
    return {**first, **second}


def plan_from(order, uses):
    uses, plan = dict(uses), {}
    for k, name in enumerate(order):
        bank = k % 8
        plan[name] = (bank, uses.get(bank, 0))
        uses[bank] = uses.get(bank, 0) + 1
    return plan


BANK = bank_plan()


def build(nc, a):
    ctx = ExitStack()
    with ctx:
        def sb(name, shape, dt=FP32):
            return ctx.enter_context(nc.sbuf_tensor(name, shape, dt))

        class Sems(dict):
            def __missing__(self, name):
                self[name] = ctx.enter_context(nc.semaphore(name))
                return self[name]

        S = Sems()

        ring = sb("weight_ring", [P, SLOTS, 4096])
        tokA = sb("tokA", [P, TT, D])
        tokB = sb("tokB", [P, TT, D])
        hT = sb("hT", [P, KT, LEN])
        uTp = sb("uTp", [P, UT, CHUNK, NCH])
        rawR = sb("raw_region", [P, 8 * (LEN + 3)])
        convR = sb("conv_region", [P, 8 * LEN])
        vR = sb("v_region", [P, 3 * HEADS * (DV + 1)])
        gR = sb("gate_region", [P, 16 * SEQ])
        XR = sb("state_region", [P, 2 * NST * LEN])
        scanR = sb("scan_region", [P, 3 * 2 * NST * NCH + 2 * NST * CHUNK])
        cTt = sb("cTt", [P, 2, UT, P])
        prow = sb("prow", [P, 2, P])
        pcol = sb("pcol", [P, 2, P])
        ident = sb("ident", [P, P])
        tri = sb("tri", [P, P])
        small = sb("small", [P, 640])
        rows = sb("rows", [HEADS, 6, LEN])
        rowone = sb("rowone", [HEADS, 1])
        wif = sb("wif", [P, KT, 8])
        wif2 = sb("wif2", [P, KT, 8])
        wr = sb("wr", [P, KT, NG + NE])
        bif = sb("bif", [HEADS, 2])
        ldt = sb("ldt", [NST, 2])
        p4 = sb("p4", [GH, 2])
        ones = sb("ones", [P, P])
        stri = sb("stri", [P, P])
        negm = sb("negm", [P, P])
        blk = sb("blk", [P, P])
        lvl = sb("lvl", [P, LEVELS, P])
        trips = sb("trips", [1, 1], I32)
        fgs = sb("fgs", [P, TT, NG])
        wtok = sb("wtok", [P, TT, EG])
        rig = sb("rig", [P, TT, EG])
        rcum = sb("rcum", [P, EG])
        rone = sb("rone", [P, EG])
        rmul = sb("rmul", [P, NG, EG])

        raw = rawR[:].rearrange("p (t n) -> p t n", t=8)
        conv = convR[:].rearrange("p (t n) -> p t n", t=8)
        vaug = vR[:].rearrange("p (t h n) -> p t h n", t=3, h=HEADS)
        gT = gR[:].rearrange("p (t n) -> p t n", t=16)
        X = XR[:].rearrange("p (c i s n) -> p c i s n", c=2, i=NST, s=CHUNK)
        cell = 2 * NST * NCH
        T1 = scanR[:, 0:cell].rearrange("p (c i n) -> p c i n", c=2, i=NST)
        T2 = scanR[:, cell:2 * cell].rearrange("p (c i n) -> p c i n", c=2, i=NST)
        EN = scanR[:, 2 * cell:3 * cell].rearrange("p (c i n) -> p c i n", c=2, i=NST)
        PW = scanR[:, 3 * cell:].rearrange("p (c s i) -> p c s i", c=2, s=CHUNK)
        meta = vR[0:META, 0:D]
        bTt = gR[:, 0:1024].rearrange("p (c j n) -> p c j n", c=2, j=UT)
        braw = gR[:, 1024:1536].rearrange("p (c i h) -> p c i h", c=2, i=NST)
        bexp = gR[:, 1536:2560].rearrange("p (c i h) -> p c i h", c=2, i=NST)
        craw = gR[:, 2560:3072].rearrange("p (c j n) -> p c j n", c=2, j=UT)
        cexp = gR[:, 3072:4096].rearrange("p (c j n) -> p c j n", c=2, j=UT)
        lrow = tokB[0:NST].rearrange("p t n -> p (t n)").rearrange("p (c n) -> p c n", n=P)
        sel = sb("sel", [HEADS, HEADS, P])
        hm = rawR[:, 0:TT * D].rearrange("p (t n) -> p t n", t=TT)
        omT = convR[:, 0:KT * SEQ].rearrange("p (t n) -> p t n", t=KT)
        gelT = scanR[:, 0:UT * SEQ].rearrange("p (t n) -> p t n", t=UT)
        mixT = XR[:, 0:KT * SEQ].rearrange("p (t n) -> p t n", t=KT)
        zsig = XR[:, 2048:2048 + 512].rearrange("p (b n) -> p b n", b=2)
        pt = XR[:, 4608:5888].rearrange("p (b n) -> p b n", b=2)
        wgt = XR[:, 5888:7168].rearrange("p (b n) -> p b n", b=2)
        bc0 = XR[:, 0:2 * D].rearrange("p (c n) -> p c n", c=2)
        bcvo = convR[:, 0:2 * D].rearrange("p (c n) -> p c n", c=2)
        bcL = XR[:, 4608:4608 + 2 * D].rearrange("p (c n) -> p c n", c=2)
        ffr = XR[:, 2560:2560 + 1024].rearrange("p (b n) -> p b n", b=2)
        ffh = XR[:, 3584:3584 + 1024].rearrange("p (b n) -> p b n", b=2)

        ps = [ctx.enter_context(nc.psum_tensor(f"bank{b}", [P, 512], FP32)) for b in range(8)]

        def bank(*name):
            return ps[BANK[name][0]]

        def slot(name, i, cols):
            return ring[:, CHUNK_AT[name, i] % SLOTS, :].rearrange("p (k n) -> p k n", n=cols)

        mix2T = mixT
        graw = XR[:, 2048:2048 + 12 * (SEQ + 3)].rearrange("p (t n) -> p t n", t=12)
        gsq = XR[:, 2048:2048 + 12 * SEQ].rearrange("p (t n) -> p t n", t=12)
        gconv = XR[:, 5156:5156 + 12 * SEQ].rearrange("p (t n) -> p t n", t=12)
        mq = rawR[:, 0:8 * SEQ].rearrange("p (t n) -> p t n", t=8)
        mval = vR[:, 0:1024].rearrange("p (t n) -> p t n", t=TT)
        gz = vR[:, 1024:2048].rearrange("p (t n) -> p t n", t=TT)
        vb = vR[:, 2048:3072].rearrange("p (t h n) -> p t h n", t=TT, h=GH)
        aT = gR[:, 0:1536].rearrange("p (h n) -> p h n", h=GH)
        qkT = gR[:, 1536:3072].rearrange("p (h n) -> p h n", h=GH)
        U = gR[:, 3072:4096].rearrange("p (t h n) -> p t h n", t=TT, h=GH)
        Tm = convR[:, 0:1024].rearrange("p (q n) -> p q n", q=8)
        Tt = convR[:, 1024:2048].rearrange("p (q n) -> p q n", q=8)
        Xb = scanR[:, 0:1024].rearrange("p (q n) -> p q n", q=8)
        Zm = scanR[:, 1024:2048].rearrange("p (q n) -> p q n", q=8)
        gsig = gsq
        xg = XR[:, 0:1024].rearrange("p (k n) -> p k n", k=KT)
        ptok = XR[:, 1024:1024 + TT * (BLOCKS + 1) * CAP]\
            .rearrange("p (t b n) -> p t b n", t=TT, b=BLOCKS + 1)
        pslot = gR[:, 0:BLOCKS * SEQ].rearrange("p (b n) -> p b n", b=BLOCKS)
        pcur = gR[:, 2048:2048 + SEQ]
        iota = gR[:, 2304:2304 + CAP]
        yg = vR[:, 0:D]
        sg = vR[:, 1024:1536].rearrange("p (b n) -> p b n", b=2)
        hid = rawR[:, 0:512].rearrange("p (b n) -> p b n", b=2)
        hidT = rawR[:, 512:1024].rearrange("p (b n) -> p b n", b=2)
        wslot = rawR[:, 1024:1024 + BLOCKS * EG]
        yu = scanR[:, 1088:1088 + UT * SEQ].rearrange("p (t n) -> p t n", t=UT)
        ymg = XR[:, 4096:4608].rearrange("p (b n) -> p b n", b=2)
        tokBf = tokB[:].rearrange("p t n -> p (t n)")
        pm = tokBf[:, 0:768].rearrange("p (b n) -> p b n", b=2)
        pTs = tokBf[:, 768:1536].rearrange("p (b n) -> p b n", b=2)
        dec = pTs
        ob = cTt[:].rearrange("p a b n -> p (a b n)").rearrange("p (t h n) -> p t h n", t=TT, h=GH)

        used = [0]

        def col(n):
            used[0] += n
            assert used[0] <= small.shape[1], used
            return small[:, used[0] - n:used[0]]

        eps5, eps6 = col(1), col(1)
        odd, even = col(1), col(1)
        parity = col(4)
        stats = col(36)
        mv = col(6)
        std, rstd = col(8), col(8)
        lamcol = col(64)
        gcol, em = col(20), col(8)
        den, rden = col(8), col(8)
        bst, mvh = col(48), col(16)
        ss = col(8)
        nmax, psum_, prec = col(4), col(4), col(4)
        gc = col(16)
        mv3 = mv.rearrange("p (r c) -> p r c", c=2)
        mvh3 = mvh.rearrange("p (r c) -> p r c", c=2)
        comb = col(2 * NE)
        rl = col(72)
        rt = col(80)
        rank = col(4)
        count = col(8)

        NROW1 = 81
        block = ctx.enter_context(nc.Block())

        def full(*name):
            return S[f"bank{BANK[name][0]}_full"], 1

        def filled(*name):
            return S[f"bank{BANK[name][0]}_full"], BANK[name][1] + 1

        def read(*name):
            return S[f"bank{BANK[name][0]}_read"], 1

        def drained(*name):
            return S[f"bank{BANK[name][0]}_read"], BANK[name][1] + 1

        @block.sync
        def _(sp):
            def w_rows(w, k0, nk, c0, nc_):
                return w[k0 * P:(k0 + nk) * P, c0:c0 + nc_].rearrange("(k p) n -> p k n", p=P)

            w_in, w2 = a["w_in"][0], a["w_in_2"][0]

            def dram(name, i):
                if name == "u":
                    return [w_rows(w_in, 0, KT, C_U, 512)]
                if name == "qk":
                    return [w_rows(w_in, 0, KT, C_QK + 512 * i, 512)]
                if name == "v":
                    return [w_rows(w_in, 0, KT, C_V + 512 * i, 512)]
                if name == "o":
                    return [w_rows(w_in, 0, KT, C_O + 512 * i, 512)]
                if name == "g":
                    return [w_rows(w_in, 0, KT, C_G + 512 * i, 512)]
                if name == "glu":
                    return [w_rows(a["s5_w_glu"][0], 0, UT, 512 * i, 512),
                            w_rows(a["s5_w_glu"][0], 0, UT, D + 512 * i, 512)]
                if name == "mout":
                    return [w_rows(a["m_w_out"][0], 0, KT, 512 * i, 512)]
                if name == "wo":
                    return [w_rows(a["w_o"][0], 0, KT, 512 * i, 512)]
                if name == "gqkv":
                    return [w_rows(w2, 0, KT, C2_GQKV + 512 * i, 512)]
                if name == "mqk":
                    return [w_rows(w2, 0, KT, C2_MQ + 512 * i, 512)]
                if name == "gz":
                    return [w_rows(w2, 0, KT, C2_GZ, 512)]
                if name == "mv":
                    return [w_rows(w2, 0, KT, C2_MV, 512)]
                if name == "wout":
                    return [w_rows(a["w_out_2"][0], 0, KT, 512 * i, 512)]

            def chunk_used(at):
                name, i, _ = STREAM[at]
                if name == "ffn":
                    return S["ffn_down"], i + 1
                if name == "u":
                    return filled("u", 3)
                if name in ("qk", "g", "glu", "mout", "gqkv", "mqk"):
                    return filled({"glu": "z", "mout": "ym"}.get(name, name), 4 * i + 3)
                if name == "v":
                    return filled("v", 3 * i + 2)
                if name in ("o", "wo", "wout"):
                    return filled(name, 2 * i + 1)
                return filled(name, 1)

            def load(name, i):
                at = CHUNK_AT[name, i]
                if at >= SLOTS:
                    sp.wait_ge(*chunk_used(at - SLOTS))
                srcs = dram(name, i)
                size = 4096 // len(srcs)
                for k, src in enumerate(srcs):
                    dst = ring[:, at % SLOTS, k * size:(k + 1) * size].rearrange("p (k n) -> p k n", n=512)
                    sp.dma_start(dst, src).then_inc(S[f"slot{at % SLOTS}_loaded"], 16)

            for name, i, _ in STREAM:
                if name == "ffn":
                    break
                load(name, i)
            base = CHUNK_AT["ffn", 0]
            wup = a["w_up"][0].rearrange("(k p) (j n) -> j p k n", p=P, n=256)
            wdn = a["w_down"][0].rearrange("(j k p) n -> j p k n", p=P, k=2)

            def load_ffn(j, q):
                s = (base + q) % SLOTS
                sp.dma_start(ring[:, s, 0:2048].rearrange("p (k n) -> p k n", n=256),
                             wup[bass.ds(j, 1)].squeeze(0)).then_inc(S[f"slot{s}_loaded"], 16)
                sp.dma_start(ring[:, s, 2048:4096].rearrange("p (k n) -> p k n", n=D),
                             wdn[bass.ds(j, 1)].squeeze(0)).then_inc(S[f"slot{s}_loaded"], 16)

            for q in range(SLOTS):
                sp.wait_ge(*chunk_used(base + q - SLOTS))
                load_ffn(q, q)
            with sp.Fori(1, FF // 256 // SLOTS) as it:
                for q in range(SLOTS):
                    sp.wait_ge(S["ffn_down"], it * SLOTS + (q - SLOTS + 1))
                    load_ffn(it * SLOTS + q, q)
            for name, i, _ in STREAM[CHUNK_AT["gqkv", 0]:CHUNK_AT["gu", 0]]:
                load(name, i)
            base = CHUNK_AT["gu", 0]
            wg = a["w_gate_2"][0].rearrange("g e (k p) n -> (g e) p k n", p=P)
            wu = a["w_up_2"][0].rearrange("g e (k p) n -> (g e) p k n", p=P)
            wd = a["w_down_2"][0].rearrange("g e (k p) n -> (g e) p k n", p=P)

            def load_gate_up(e, q):
                s = (base + 2 * q) % SLOTS
                for c, w in enumerate((wg, wu)):
                    sp.dma_start(ring[:, s, 2048 * c:2048 * c + 2048].rearrange("p (k n) -> p k n", n=EF),
                                 w[bass.ds(e, 1)].squeeze(0)).then_inc(S[f"slot{s}_loaded"], 16)

            def load_down(e, q):
                s = (base + 2 * q + 1) % SLOTS
                sp.dma_start(ring[:, s, 0:2048].rearrange("p (k n) -> p k n", n=D),
                             wd[bass.ds(e, 1)].squeeze(0)).then_inc(S[f"slot{s}_loaded"], 16)

            for q in range(2):
                sp.wait_ge(*chunk_used(base + 2 * q - SLOTS))
                load_gate_up(q, q)
                sp.wait_ge(*chunk_used(base + 2 * q + 1 - SLOTS))
                load_down(q, q)
            for q in range(2):
                sp.wait_ge(S["gu_full"], q + 1)
                load_gate_up(2 + q, q)
            sp.wait_ge(S["trips_ready"], 1)
            blocks = sp.value_load(trips[0:1, 0:1], min_val=NG, max_val=BLOCKS)
            with sp.Fori(1, blocks * (EG // 2) - 1) as it:
                pair, ahead = it % (NE // 2), (it + 1) % (NE // 2)
                for q in range(2):
                    sp.wait_ge(S["moe_down"], it * 2 + (q - 1 + 3))
                    load_down(pair * 2 + q, q)
                    sp.wait_ge(S["gu_full"], it * 2 + (q + 1))
                    load_gate_up(ahead * 2 + q, q)
            for q in range(2):
                sp.wait_ge(S["moe_down"], blocks * EG + q)
                load_down(NE - 2 + q, q)
            for t in range(TT):
                sp.wait_ge(S["out_ready"], t + 1)
                sp.dma_start(a["out"][0, t * P:(t + 1) * P, :], tokB[:, t, :]).then_inc(S["out_written"], 16)
            sp.wait_ge(S["out_written"], 16 * TT)

        @block.tensor
        def _(pe):
            def free(*name):
                b, n = BANK[name]
                if n:
                    pe.wait_ge(S[f"bank{b}_read"], n)
                return ps[b]

            def arrived(name, i):
                at = CHUNK_AT[name, i]
                pe.wait_ge(S[f"slot{at % SLOTS}_loaded"], loaded_count(at))

            def project_T(o, w, c0, xT, nk, n0, n1):
                for k in range(nk):
                    last = nc.tensor.matmul(o, w[:, k, c0:c0 + P], xT[:, k, n0:n1], start=(k == 0), stop=(k == nk - 1))
                return last

            def project_tok(o, w, xT, nk, n0, n1):
                for k in range(nk):
                    last = nc.tensor.matmul(o, xT[:, k, n0:n1], w[:, k, :], start=(k == 0), stop=(k == nk - 1))
                return last

            pe.wait_ge(S["const_ready"], 1)
            pe.wait_ge(S["prow_loaded"], PROW_DMAS * 16)
            for c, n in ((0, P), (1, NROW1)):
                o = free("prow", c)
                nc.tensor.transpose(o[:, 0:n], prow[0:n, c, :], ident[0:n, 0:n]).then_inc(*full("prow", c))
            pe.wait_ge(S["xn_ready"], 1)
            for t in range(KT):
                o = free("xT", t)
                nc.tensor.transpose(o[:, 0:META], meta[:, t * P:(t + 1) * P], ident[0:META, 0:META])
                for m in range(TT):
                    last = nc.tensor.transpose(o[:, META + m * P:META + (m + 1) * P], tokA[:, m, t * P:(t + 1) * P],
                                               ident[:])
                last.then_inc(*full("xT", t))
            pe.wait_ge(S["poles_ready"], 1)
            o = free("lam", 0)
            for c in range(4):
                last = nc.tensor.transpose(o[:, c * NST:(c + 1) * NST], lrow[:, 12 + c, :], ident[0:NST, 0:NST])
            last.then_inc(*full("lam", 0))
            arrived("u", 0)
            pe.wait_ge(*drained("xT", KT - 1))
            for t in range(UT):
                o = free("u", t)
                project_T(o[:, 0:LEN], slot("u", 0, 512), t * P, hT, KT, 0, LEN).then_inc(*full("u", t))
            pe.wait_ge(S["bexp_ready"], 1)
            for c in range(2):
                o = free("bT", c)
                for j in range(UT):
                    last = nc.tensor.transpose(o[:, j * P:(j + 1) * P],
                                               bexp[:, c, 4 * j:4 * j + 4, :].rearrange("p i h -> p (i h)"), ident[:])
                last.then_inc(*full("bT", c))
            pe.wait_ge(S["cexp_ready"], 1)
            for c in range(2):
                o = free("cT", c)
                for j in range(UT):
                    last = nc.tensor.transpose(o[:, j * P:(j + 1) * P], cexp[:, c, j, :], ident[:])
                last.then_inc(*full("cT", c))
            pe.wait_ge(*drained("u", UT - 1))
            pe.wait_ge(*drained("bT", 1))
            for i in range(NST):
                j, r = i // 4, 32 * (i % 4)
                for c in range(2):
                    o = free("bu", 2 * i + c)
                    nc.tensor.matmul(o[:, 0:LEN], bTt[r:r + 32, c, j, :],
                                     uTp[r:r + 32, j, :, :].rearrange("p s n -> p (s n)"), start=True, stop=True)\
                        .then_inc(*full("bu", 2 * i + c))
            for t in range(8):
                if t % 4 == 0:
                    arrived("qk", t // 4)
                o = free("qk", t)
                project_T(o[:, 0:LEN], slot("qk", t // 4, 512), (t % 4) * P, hT, KT, 0, LEN).then_inc(*full("qk", t))
            pe.wait_ge(S["small_loaded"], SMALL_DMAS * 16)
            for c, name in enumerate(("i", "f")):
                o = free(name, 0)
                for k in range(KT):
                    last = nc.tensor.matmul(o[0:HEADS, 0:LEN], wif[:, k, 4 * c:4 * c + 4], hT[:, k, :],
                                            start=(k == 0), stop=(k == KT - 1))
                last.then_inc(*full(name, 0))
            spans = [(0, META), (META, META + P), (META + P, LEN)]
            for k in range(6):
                if k % 3 == 0:
                    arrived("v", k // 3)
                n0, n1 = spans[k % 3]
                o = free("v", k)
                project_tok(o[0:n1 - n0, :], slot("v", k // 3, 512), hT, KT, n0, n1).then_inc(*full("v", k))
            for k in range(4):
                if k % 2 == 0:
                    arrived("o", k // 2)
                n0, n1 = spans[1 + k % 2]
                o = free("o", k)
                project_tok(o[:, :], slot("o", k // 2, 512), hT, KT, n0, n1).then_inc(*full("o", k))
            for t in range(16):
                if t % 4 == 0:
                    arrived("g", t // 4)
                o = free("g", t)
                project_T(o[:, 0:SEQ], slot("g", t // 4, 512), (t % 4) * P, hT, KT, META, LEN).then_inc(*full("g", t))
            pe.wait_ge(S["scan_ready"], 1)
            pe.wait_ge(*drained("cT", 1))
            for j in range(UT):
                o = free("y", j)
                for r in range(4):
                    for c in range(2):
                        last = nc.tensor.matmul(o[32 * r:32 * r + 32, 0:SEQ], cTt[:, c, j, 32 * r:32 * r + 32],
                                                X[:, c, 4 * j + r, :, 1:NCH], start=(c == 0), stop=(c == 1))
                last.then_inc(*full("y", j))
            pe.wait_ge(S["gelu_ready"], UT)
            for t in range(KT):
                if t % 4 == 0:
                    arrived("glu", t // 4)
                w = slot("glu", t // 4, 512)
                o = free("z", t)
                project_T(o[:, 0:SEQ], w[:, 0:UT, :], (t % 4) * P, gelT, UT, 0, SEQ)
                project_T(o[:, SEQ:2 * SEQ], w[:, UT:2 * UT, :], (t % 4) * P, gelT, UT, 0, SEQ)\
                    .then_inc(*full("z", t))
            pe.wait_ge(S["gate_rows_ready"], 1)
            o = free("gm", 0)
            nc.tensor.transpose(o[0:META, 0:4], rows[:, 0, 0:META], ident[0:HEADS, 0:HEADS])
            for m in range(TT):
                lo, hi = spans[1 + m]
                nc.tensor.transpose(o[:, 4 + 4 * m:8 + 4 * m], rows[:, 0, lo:hi], ident[0:HEADS, 0:HEADS])
                last = nc.tensor.transpose(o[:, 12 + 4 * m:16 + 4 * m], rows[:, 5, lo:hi], ident[0:HEADS, 0:HEADS])
            last.then_inc(*full("gm", 0))
            pe.wait_ge(S["qk_ready"], 2)
            for h in range(HEADS):
                q, kk = conv[:, h, META:LEN], conv[:, 4 + h, :]
                o = free("ms", h)
                nc.tensor.matmul(o[:, 0:SEQ], sel[:, h, :], rows[:, 4, META:LEN], start=True, stop=True)
                nc.tensor.matmul(o[0:META, SEQ:2 * SEQ], kk[:, 0:META], q, start=True, stop=True)\
                    .then_inc(*full("ms", h))
                o = free("s", h)
                nc.tensor.matmul(o[:, 0:SEQ], kk[:, META:META + P], q, start=True, stop=True)
                nc.tensor.matmul(o[:, SEQ:SEQ + P], kk[:, META + P:LEN], q[:, P:SEQ], start=True, stop=True)\
                    .then_inc(*full("s", h))
            pe.wait_ge(S["v_biased"], 6)
            for k in range(2 * HEADS):
                h, m = k // 2, k % 2
                b = h % 2
                if m == 0:
                    pe.wait_ge(S["pt_ready"], h + 1)
                o = free("h", k)
                nc.tensor.matmul(o[:, 0:DV + 1], pt[0:META, b, m * P:(m + 1) * P], vaug[0:META, 0, h, :],
                                 start=True, stop=False)
                last = nc.tensor.matmul(o[:, 0:DV + 1], pt[:, b, SEQ + m * P:SEQ + (m + 1) * P], vaug[:, 1, h, :],
                                        start=False, stop=(m == 0))
                if m == 1:
                    last = nc.tensor.matmul(o[:, 0:DV + 1], pt[:, b, 2 * SEQ:2 * SEQ + P], vaug[:, 2, h, :],
                                            start=False, stop=True)
                last.then_inc(*full("h", k))
            pe.wait_ge(S["gated_ready"], 1)
            for t in range(KT):
                o = free("oT", t)
                for m in range(TT):
                    last = nc.tensor.transpose(o[:, m * P:(m + 1) * P], hm[:, m, t * P:(t + 1) * P], ident[:])
                last.then_inc(*full("oT", t))
            pe.wait_ge(*drained("oT", KT - 1))
            for t in range(KT):
                if t % 4 == 0:
                    arrived("mout", t // 4)
                o = free("ym", t)
                project_T(o[:, 0:SEQ], slot("mout", t // 4, 512), (t % 4) * P, omT, KT, 0, SEQ)\
                    .then_inc(*full("ym", t))
            pe.wait_ge(S["mix_ready"], KT)
            for k in range(4):
                if k % 2 == 0:
                    arrived("wo", k // 2)
                o = free("wo", k)
                project_tok(o[:, :], slot("wo", k // 2, 512), mixT, KT, (k % 2) * P, (k % 2 + 1) * P)\
                    .then_inc(*full("wo", k))

            def transposed(name, ready):
                pe.wait_ge(S["xn_ready"], ready)
                for t in range(KT):
                    o = free(name, t)
                    for m in range(TT):
                        last = nc.tensor.transpose(o[:, m * P:(m + 1) * P], tokB[:, m, t * P:(t + 1) * P], ident[:])
                    last.then_inc(*full(name, t))
                pe.wait_ge(*drained(name, KT - 1))

            transposed("h1T", 2)
            base = CHUNK_AT["ffn", 0]
            first = [loaded_count(base + q) for q in range(SLOTS)]
            with pe.Fori(0, FF // 256 // SLOTS) as it:
                for q in range(SLOTS):
                    s = (base + q) % SLOTS
                    up = ring[:, s, 0:2048].rearrange("p (k n) -> p k n", n=256)
                    down = ring[:, s, 2048:4096].rearrange("p (k n) -> p k n", n=D)
                    pe.wait_ge(S[f"slot{s}_loaded"], it * 32 + first[q])
                    for m in range(2):
                        project_T(ps[2 * (q % 2) + m][:, 0:SEQ], up, m * P, hT, KT, 0, SEQ)\
                            .then_inc(S["ffn_up"], 1)
                    pe.wait_ge(S["ffn_added"], it * SLOTS + (q + 1))
                    for k in range(2):
                        pe.wait_ge(S["relu2_ready"], it * (2 * SLOTS) + (2 * q + k + 1))
                        for m in range(TT):
                            for n in range(2):
                                last = nc.tensor.matmul(ps[4 + 2 * m + n][:, :], ffh[:, q % 2, k * SEQ + m * P:k * SEQ + (m + 1) * P],
                                                        down[:, k, 512 * n:512 * n + 512], start=(k == 0), stop=(k == 1))
                    last.then_inc(S["ffn_down"], 1)

            transposed("x2T", 3)
            for c, name in enumerate(("ga", "gb")):
                o = free(name, 0)
                for k in range(KT):
                    last = nc.tensor.matmul(o[0:GH, 0:SEQ], wif2[:, k, 4 * c:4 * c + 4], hT[:, k, 0:SEQ],
                                            start=(k == 0), stop=(k == KT - 1))
                last.then_inc(*full(name, 0))
            for t in range(12):
                if t % 4 == 0:
                    arrived("gqkv", t // 4)
                o = free("gqkv", t)
                project_T(o[:, 0:SEQ], slot("gqkv", t // 4, 512), (t % 4) * P, hT, KT, 0, SEQ)\
                    .then_inc(*full("gqkv", t))
            pe.wait_ge(S["decay_rows_ready"], 1)
            o = free("Gc", 0)
            for m in range(TT):
                nc.tensor.transpose(o[:, 4 * m:4 * m + 4], rows[:, 3, m * P:(m + 1) * P], ident[0:GH, 0:GH])
                last = nc.tensor.transpose(o[:, 8 + 4 * m:12 + 4 * m], rows[:, 4, m * P:(m + 1) * P], ident[0:GH, 0:GH])
            last.then_inc(*full("Gc", 0))
            for t in range(8):
                if t % 4 == 0:
                    arrived("mqk", t // 4)
                o = free("mqk", t)
                project_T(o[:, 0:SEQ], slot("mqk", t // 4, 512), (t % 4) * P, hT, KT, 0, SEQ)\
                    .then_inc(*full("mqk", t))
            for name, dst in (("gz", 0), ("mv", 0)):
                arrived(name, 0)
                for m in range(TT):
                    o = free(name, m)
                    project_tok(o[:, :], slot(name, 0, 512), hT, KT, m * P, (m + 1) * P).then_inc(*full(name, m))
            for t in range(4):
                pe.wait_ge(S["gsq_ready"], t + 1)
                o = free("nq", t)
                nc.tensor.matmul(o[:, :], ones[:], gsq[:, 2 * t:2 * t + 2, :].rearrange("p t n -> p (t n)"),
                                 start=True, stop=True).then_inc(*full("nq", t))
            pe.wait_ge(S["gconv_ready"], 3)
            for m in range(TT):
                o = free("vk", m)
                for h in range(GH):
                    last = nc.tensor.transpose(o[:, h * P:(h + 1) * P], gconv[:, 8 + h, m * P:(m + 1) * P], ident[:])
                last.then_inc(*full("vk", m))
            pe.wait_ge(S["gnorm_ready"], 4)
            for h in range(GH):
                q, kk = gconv[:, h, :], gconv[:, 4 + h, :]
                o = free("gb_", h)
                nc.tensor.matmul(o[:, 0:SEQ], sel[:, h, :], rows[:, 3, 0:SEQ], start=True, stop=True)
                nc.tensor.matmul(o[:, SEQ:2 * SEQ], sel[:, h, :], rows[:, 4, 0:SEQ], start=True, stop=True)\
                    .then_inc(*full("gb_", h))
                for name, r in (("kk", kk), ("qk_", q)):
                    o = free(name, h)
                    nc.tensor.matmul(o[:, 0:SEQ], kk[:, 0:P], r, start=True, stop=True)
                    nc.tensor.matmul(o[:, SEQ:SEQ + P], kk[:, P:SEQ], r[:, P:SEQ], start=True, stop=True)\
                        .then_inc(*full(name, h))

            def scores(h):
                b = MD * (h % 2)
                qh, kh = mq[b:b + MD, h // 2, :], mq[b:b + MD, 4 + h // 2, :]
                o = free("sc", h)
                nc.tensor.matmul(o[:, 0:P], qh[:, 0:P], kh[:, 0:P], start=True, stop=True)
                nc.tensor.matmul(o[:, P:P + SEQ], qh[:, P:SEQ], kh, start=True, stop=True).then_inc(*full("sc", h))

            def probs_T(h):
                pe.wait_ge(S["probs_ready"], h + 1)
                o = free("pT", h)
                for c in range(3):
                    last = nc.tensor.transpose(o[:, c * P:(c + 1) * P], pm[:, h % 2, c * P:(c + 1) * P], ident[:])
                last.then_inc(*full("pT", h))

            def attend(h):
                b = MD * (h % 2)
                pe.wait_ge(*drained("pT", h))
                o = free("av", h)
                w = pTs[:, h % 2, :]
                nc.tensor.matmul(o[b:b + MD, 0:SEQ], mval[:, 0, h * MD:(h + 1) * MD], w[:, 0:SEQ], start=True, stop=False)
                nc.tensor.matmul(o[b:b + MD, P:SEQ], mval[:, 1, h * MD:(h + 1) * MD], w[:, SEQ:SEQ + P],
                                 start=False, stop=True).then_inc(*full("av", h))

            def diag(h, m):
                return aT[:, h, 0:P] if m == 0 else aT[:, h, SEQ:SEQ + P]

            pe.wait_ge(S["aT_ready"], GH)
            pe.wait_ge(*drained("mv", 1))
            for lv in range(LEVELS):
                for half in range(2):
                    if lv:
                        pe.wait_ge(S["T_ready"], 2 * lv - 1 + half)
                    else:
                        pe.wait_ge(S["T_init"], 1)
                    o = free("X", lv, half)
                    for q in range(4):
                        h, m = 2 * half + q // 2, q % 2
                        last = nc.tensor.matmul(o[:, q * P:(q + 1) * P], diag(h, m), Tm[:, 4 * half + q, :],
                                                start=True, stop=True)
                    last.then_inc(*full("X", lv, half))
                scores(lv)
                if lv:
                    attend(lv - 1)
                for half in range(2):
                    pe.wait_ge(*drained("X", lv, half))
                    o = free("Z", lv, half)
                    for q in range(4):
                        g = 4 * half + q
                        last = nc.tensor.matmul(o[:, q * P:(q + 1) * P], Tt[:, g, :], Xb[:, g, :], start=True, stop=True)
                    last.then_inc(*full("Z", lv, half))
                    o = free("ZT", lv, half)
                    for q in range(4):
                        g = 4 * half + q
                        last = nc.tensor.matmul(o[:, q * P:(q + 1) * P], Xb[:, g, :], Tt[:, g, :], start=True, stop=True)
                    last.then_inc(*full("ZT", lv, half))
                probs_T(lv)
            scores(MH - 1)
            attend(MH - 2)
            probs_T(MH - 1)
            attend(MH - 1)
            pe.wait_ge(S["T_ready"], 2 * LEVELS)
            pe.wait_ge(*drained("vk", 1))
            o = free("U1", 0)
            for h in range(GH):
                last = nc.tensor.matmul(o[:, h * P:(h + 1) * P], Tt[:, 2 * h, :], vb[:, 0, h, :], start=True, stop=True)
            last.then_inc(*full("U1", 0))
            pe.wait_ge(*drained("U1", 0))
            o = free("AU", 0)
            for h in range(GH):
                last = nc.tensor.matmul(o[:, h * P:(h + 1) * P], aT[:, h, P:SEQ], U[:, 0, h, :], start=True, stop=True)
            last.then_inc(*full("AU", 0))
            pe.wait_ge(*drained("AU", 0))
            o = free("U2", 0)
            for h in range(GH):
                last = nc.tensor.matmul(o[:, h * P:(h + 1) * P], Tt[:, 2 * h + 1, :], vb[:, 1, h, :], start=True, stop=True)
            last.then_inc(*full("U2", 0))
            o = free("O", 0)
            for h in range(GH):
                last = nc.tensor.matmul(o[:, h * P:(h + 1) * P], qkT[:, h, 0:P], U[:, 0, h, :], start=True, stop=True)
            last.then_inc(*full("O", 0))
            pe.wait_ge(*drained("U2", 0))
            o = free("O", 1)
            for h in range(GH):
                nc.tensor.matmul(o[:, h * P:(h + 1) * P], qkT[:, h, P:SEQ], U[:, 0, h, :], start=True, stop=False)
                last = nc.tensor.matmul(o[:, h * P:(h + 1) * P], qkT[:, h, SEQ:SEQ + P], U[:, 1, h, :],
                                        start=False, stop=True)
            last.then_inc(*full("O", 1))
            pe.wait_ge(S["ob_ready"], 1)
            for b in range(2):
                o = free("obT", b)
                for q in range(4):
                    h, m = 2 * b + q // 2, q % 2
                    last = nc.tensor.transpose(o[:, q * P:(q + 1) * P], ob[:, m, h, :], ident[:])
                last.then_inc(*full("obT", b))
            pe.wait_ge(*drained("obT", 1))
            for k in range(4):
                if k % 2 == 0:
                    arrived("wout", k // 2)
                o = free("wout", k)
                project_tok(o[:, :], slot("wout", k // 2, 512), mix2T, KT, (k % 2) * P, (k % 2 + 1) * P)\
                    .then_inc(*full("wout", k))
            transposed("x3T", 4)
            for m in range(TT):
                o = free("rt", m)
                project_tok(o[:, 0:NG + NE], wr, hT, KT, m * P, (m + 1) * P).then_inc(*full("rt", m))
            pe.wait_ge(S["group_ready"], TT)
            o = free("cum", 0)
            nc.tensor.matmul(o[:, 0:NG], tri[:], fgs[:, 0, :], start=True, stop=True)
            nc.tensor.matmul(o[:, NG:2 * NG], tri[:], fgs[:, 1, :], start=True, stop=False)
            nc.tensor.matmul(o[:, NG:2 * NG], ones[:], fgs[:, 0, :], start=False, stop=True)
            nc.tensor.matmul(o[:, 2 * NG:3 * NG], ones[:], fgs[:, 0, :], start=True, stop=False)
            nc.tensor.matmul(o[:, 2 * NG:3 * NG], ones[:], fgs[:, 1, :], start=False, stop=True)\
                .then_inc(*full("cum", 0))
            pe.wait_ge(S["ptok_ready"], 1)
            o = free("comb", 0)
            for b in range(BLOCKS):
                for m in range(TT):
                    last = nc.tensor.matmul(o[:, b * EG:(b + 1) * EG], ptok[:, m, b, :], wtok[:, m, :],
                                            start=(m == 0), stop=(m == TT - 1))
            last.then_inc(*full("comb", 0))
            for c in range(BLOCKS // 2):
                o = free("sT", c)
                for q in range(4):
                    last = nc.tensor.transpose(o[:, q * P:(q + 1) * P], ptok[:, q % 2, 2 * c + q // 2, :], ident[:])
                last.then_inc(*full("sT", c))
            pe.wait_ge(*drained("sT", BLOCKS // 2 - 1))

            def gather(b):
                for k in range(KT):
                    for m in range(TT):
                        last = nc.tensor.matmul(ps[6 + k // 4][:, (k % 4) * CAP:(k % 4 + 1) * CAP],
                                                tokB[:, m, k * P:(k + 1) * P], ptok[:, m, b, :],
                                                start=(m == 0), stop=(m == TT - 1))
                last.then_inc(S["gathered"], 1)

            def gate_up(s, q):
                w = ring[:, s, :].rearrange("p (c k n) -> p k c n", c=2, n=EF)
                for k in range(KT):
                    last = nc.tensor.matmul(ps[q][:], xg[:, k, :], w[:, k, :, :], start=(k == 0), stop=(k == KT - 1))
                last.then_inc(S["gu_full"], 1)

            def hidden_T(q):
                for k in range(2):
                    last = nc.tensor.transpose(ps[2 + q][:, k * CAP:(k + 1) * CAP], hid[:, q, k * P:(k + 1) * P],
                                               ident[:])
                last.then_inc(S["hidT_full"], 1)

            def down(s, q, first, last_one):
                w = ring[:, s, 0:2048].rearrange("p (k n) -> p k n", n=D)
                for k in range(2):
                    for n in range(2):
                        last = nc.tensor.matmul(ps[4 + n][:], hidT[:, q, k * CAP:(k + 1) * CAP],
                                                w[:, k, 512 * n:512 * n + 512], start=(first and k == 0),
                                                stop=(last_one and k == 1))
                last.then_inc(S["moe_down"], 1)

            def put_back(m):
                for n in range(2):
                    last = nc.tensor.matmul(ps[6 + n][:], pcur[:, m * P:(m + 1) * P], yg[:, 512 * n:512 * n + 512],
                                            start=True, stop=True)
                last.then_inc(S["put_back"], 1)

            base = CHUNK_AT["gu", 0]
            first = [loaded_count(base + q) for q in range(SLOTS)]
            gather(0)
            pe.sem_inc(S["moe_down"], 3)
            pe.wait_ge(S["trips_ready"], 1)
            blocks = pe.value_load(trips[0:1, 0:1], min_val=NG, max_val=BLOCKS)
            with pe.Fori(0, blocks) as it:
                def do_down(e):
                    s = (base + 2 * e + 1) % SLOTS
                    pe.wait_ge(S[f"slot{s}_loaded"], it * 64 + (first[2 * (e % 2) + 1] + 16 * (e // 2)))
                    pe.wait_ge(S["hidT_ready"], it * EG + (e + 1))
                    if e == 0:
                        pe.wait_ge(S["yg_ready"], it + 1)
                    down(s, e % 2, e == 0, e == EG - 1)

                pe.wait_ge(S["xg_ready"], it + 1)
                for e in range(EG):
                    s = (base + 2 * e) % SLOTS
                    pe.wait_ge(S[f"slot{s}_loaded"], it * 128 + (first[2 * (e % 2)] + 32 * (e // 2)))
                    gate_up(s, e % 2)
                    if e >= 1:
                        pe.wait_ge(S["hidden_ready"], it * EG + e)
                        hidden_T((e - 1) % 2)
                    if e >= 2:
                        do_down(e - 2)
                    if e == 1:
                        pe.wait_ge(S["yg_ready"], it + 1)
                        pe.wait_ge(S["pcur_ready"], it + 1)
                        put_back(0)
                    if e == 3:
                        pe.wait_ge(S["added_back"], it * 2 + 2)
                        put_back(1)
                pe.wait_ge(S["added_back"], it * 2 + 3)
                gather(it + 1)
                pe.wait_ge(S["hidden_ready"], it * EG + EG)
                hidden_T((EG - 1) % 2)
                do_down(EG - 2)
                do_down(EG - 1)
            pe.wait_ge(S["yg_ready"], blocks + 1)
            pe.wait_ge(S["pcur_ready"], blocks + 1)
            pe.wait_ge(S["xg_ready"], blocks + 1)
            put_back(0)
            pe.wait_ge(S["added_back"], blocks * 2 + 2)
            put_back(1)

        @block.scalar
        def _(act):
            n_act = [0]

            def link(ins):
                n_act[0] += 1
                ins.then_inc(S["act_chain"], 1)
                act.wait_ge(S["act_chain"], n_act[0])

            A = nc.scalar.activation

            def root(out, in_, eps, scale, k):
                act.wait_ge(S["var_ready"], k)
                A(out, in_, ACT.Sqrt, bias=eps, scale=scale).then_inc(S["std_ready"], 1)

            for t in range(TT):
                act.dma_start(tokA[:, t, :], a["x"][0, t * P:(t + 1) * P, :]).then_inc(S["x_loaded"], 16)
            act.dma_start(meta, a["meta_tokens"]).then_inc(S["x_loaded"], 16)
            for c, name in ((0, "s5_lambda_re"), (1, "s5_lambda_im")):
                act.dma_start(lrow[:, c, :], a[name][0].rearrange("(i two) p -> i (two p)", two=2))\
                    .then_inc(S["poles_loaded"], 16)
            act.dma_start(ldt[:], a["s5_log_dt"][0].rearrange("(i two) -> i two", two=2)).then_inc(S["poles_loaded"], 16)
            for c, (bn, cn) in enumerate((("s5_b_re", "s5_c_re"), ("s5_b_im", "s5_c_im"))):
                act.dma_start(braw[:, c, :, :], a[bn][0].rearrange("(i two) p h -> (two p) i h", two=2))\
                    .then_inc(S["bc_loaded"], 16)
                act.dma_start(craw[:, c, :, :], a[cn][0].rearrange("(j g) h n -> (g h) j n", g=8))\
                    .then_inc(S["bc_loaded"], 16)
            act.wait_ge(S["poles_loaded"], 48)
            A(ldt[:], ldt[:], ACT.Exp).then_inc(S["dt_ready"], 1)
            act.wait_ge(S["eps_ready"], 2)
            root(std[:, 0:3], mv3[:, :, 1], eps5, 1.0, 1)
            act.wait_ge(S["zr_ready"], 1)
            A(lrow[:, 7, :], lrow[:, 3, :], ACT.Exp).then_inc(S["er_ready"], 1)
            act.wait_ge(S["angle_ready"], 1)
            A(lrow[:, 8, :], lrow[:, 6, :], ACT.Sin).then_inc(S["sin_ready"], 1)
            A(lrow[:, 9, :], lrow[:, 6, :], ACT.Sin, scale=0.5).then_inc(S["sin_ready"], 1)
            act.wait_ge(*drained("prow", 1))
            for t in range(KT):
                act.wait_ge(*filled("xT", t))
                A(hT[:, t, :], bank("xT", t)[:, 0:LEN], ACT.Identity, bias=pcol[:, 0, 112 + t:113 + t],
                  scale=pcol[:, 0, 104 + t:105 + t]).then_inc(*read("xT", t))
            for t in range(UT):
                act.wait_ge(*filled("u", t))
                A(uTp[:, t, :, :].rearrange("p s n -> p n s"),
                  bank("u", t)[:, 0:LEN].rearrange("p (n s) -> p n s", s=CHUNK), ACT.Identity,
                  bias=pcol[:, 0, 40 + t:41 + t]).then_inc(*read("u", t))
            for c in range(2):
                act.wait_ge(*filled("bT", c))
                A(bTt[:, c, :, :].rearrange("p j n -> p (j n)"), bank("bT", c)[:], ACT.Copy).then_inc(*read("bT", c))
            for c in range(2):
                act.wait_ge(*filled("cT", c))
                A(cTt[:, c, :, :].rearrange("p j n -> p (j n)"), bank("cT", c)[:], ACT.Copy).then_inc(*read("cT", c))
            act.wait_ge(S["h0_ready"], 1)
            for k in range(2 * NST):
                act.wait_ge(*filled("bu", k))
                A(X[:, k % 2, k // 2, :, :].rearrange("p s n -> p (s n)"), bank("bu", k)[:, 0:LEN], ACT.Copy)\
                    .then_inc(*read("bu", k))
            act.wait_ge(S["pads_ready"], 1)
            for t in range(8):
                act.wait_ge(*filled("qk", t))
                A(raw[:, t, 3:3 + LEN], bank("qk", t)[:, 0:LEN], ACT.Identity, bias=pcol[:, 0, 44 + t:45 + t])\
                    .then_inc(*read("qk", t))
            act.wait_ge(S["small_loaded"], SMALL_DMAS * 16)
            for c, name in enumerate(("i", "f")):
                act.wait_ge(*filled(name, 0))
                A(rows[:, c, :], bank(name, 0)[0:HEADS, 0:LEN], ACT.Identity, bias=bif[:, c:c + 1])\
                    .then_inc(*read(name, 0))
            act.wait_ge(S["ones_column_ready"], 1)
            for k in range(6):
                n = META if k % 3 == 0 else P
                act.wait_ge(*filled("v", k))
                A(vaug[0:n, k % 3, 2 * (k // 3):2 * (k // 3) + 2, 0:DV],
                  bank("v", k)[0:n, :].rearrange("p (h n) -> p h n", h=2), ACT.Copy).then_inc(*read("v", k))
            for k in range(4):
                act.wait_ge(*filled("o", k))
                A(tokB[:, k % 2, 512 * (k // 2):512 * (k // 2) + 512], bank("o", k)[:], ACT.Copy)\
                    .then_inc(*read("o", k))
            for t in range(16):
                act.wait_ge(*filled("g", t))
                A(gT[:, t, :], bank("g", t)[:, 0:SEQ], ACT.Sigmoid, bias=pcol[:, 0, 52 + t:53 + t])\
                    .then_inc(*read("g", t))
            act.wait_ge(S["o_biased"], 4)
            A(tokB[:], tokB[:], ACT.Sigmoid).then_inc(S["osig_ready"], 1)
            act.wait_ge(S["conv_ready"], 1)
            sig = rawR[:, 0:8 * LEN]
            A(sig, convR[:], ACT.Sigmoid).then_inc(S["silu_ready"], 1)
            for t in range(UT):
                act.wait_ge(*drained("y", t))
                A(gelT[:, t, :].rearrange("p (n s) -> p s n", s=CHUNK),
                  yu[:, t, :].rearrange("p (s n) -> p s n", s=CHUNK), ACT.Gelu_apprx_tanh).then_inc(S["gelu_ready"], 1)
            for t in range(KT):
                act.wait_ge(*filled("z", t))
                if t >= 2:
                    act.wait_ge(*drained("z", t - 2))
                A(zsig[:, t % 2, :], bank("z", t)[:, SEQ:2 * SEQ], ACT.Sigmoid).then_inc(S["zsig_ready"], 1)
            link(A(rows[:, 2, :], rows[:, 1, :], ACT.Abs))
            link(A(rows[:, 2, :], rows[:, 2, :], ACT.Exp, scale=-1.0))
            A(rows[:, 2, :], rows[:, 2, :], ACT.Ln, bias=1.0).then_inc(S["softplus_ready"], 1)
            act.wait_ge(*filled("gm", 0))
            A(em, bank("gm", 0)[:, 12:20], ACT.Exp, scale=-1.0).then_inc(S["em_ready"], 1)
            for h in range(HEADS):
                act.wait_ge(S["wlog_ready"], h + 1)
                A(wgt[0:META, h % 2, 0:SEQ], wgt[0:META, h % 2, 0:SEQ], ACT.Exp, scale=-1.0)
                A(wgt[:, h % 2, SEQ:640], wgt[:, h % 2, SEQ:640], ACT.Exp, scale=-1.0).then_inc(S["w_ready"], 1)
            root(std, mvh3[:, :, 1], eps5, 1.0, 2)
            for t in range(KT):
                act.wait_ge(*filled("oT", t))
                A(omT[:, t, :], bank("oT", t)[:, 0:SEQ], ACT.Copy, scale=pcol[:, 0, 120 + t:121 + t])\
                    .then_inc(*read("oT", t))
            root(std[:, 0:2], mv3[:, 0:2, 1], eps5, 1.0, 3)
            for t in range(KT):
                act.wait_ge(*filled("h1T", t))
                A(hT[:, t, 0:SEQ], bank("h1T", t)[:, 0:SEQ], ACT.Identity, bias=pcol[:, 1, 56 + t:57 + t],
                  scale=pcol[:, 1, 48 + t:49 + t]).then_inc(*read("h1T", t))
            with act.Fori(0, FF // 256 // SLOTS) as it:
                for q in range(SLOTS):
                    for m in range(2):
                        act.wait_ge(S["ffn_up"], it * (2 * SLOTS) + (2 * q + m + 1))
                        A(ffr[:, q % 2, m * SEQ:(m + 1) * SEQ], ps[2 * (q % 2) + m][:, 0:SEQ], ACT.Relu,
                          bias=pcol[:, 0, bass.ds(it * (2 * SLOTS) + (72 + 2 * q + m), 1)]).then_inc(S["relu_ready"], 1)

            root(std[:, 0:2], mv3[:, 0:2, 1], eps5, 1.0, 4)

            def mean_square(k):
                act.wait_ge(S["res_ready"], k)
                for m in range(TT):
                    A(tokB[:, m, :], tokA[:, m, :], ACT.Square, accum_out=ss[:, m:m + 1]).then_inc(S["act_sq"], 1)
                act.wait_ge(S["act_sq"], TT * k)
                A(std[:, 0:TT], ss[:, 0:TT], ACT.Sqrt, bias=eps6, scale=1.0 / D).then_inc(S["std_ready"], 1)

            def normed_T(name, c0):
                for t in range(KT):
                    act.wait_ge(*filled(name, t))
                    A(hT[:, t, 0:SEQ], bank(name, t)[:, 0:SEQ], ACT.Copy, scale=pcol[:, 1, c0 + t:c0 + t + 1])\
                        .then_inc(*read(name, t))

            mean_square(1)
            normed_T("x2T", 64)
            act.wait_ge(*filled("ga", 0))
            A(rows[:, 0, 0:SEQ], bank("ga", 0)[0:GH, 0:SEQ], ACT.Identity, bias=p4[:, 1:2]).then_inc(*read("ga", 0))
            act.wait_ge(*filled("gb", 0))
            A(rows[:, 4, 0:SEQ], bank("gb", 0)[0:GH, 0:SEQ], ACT.Sigmoid).then_inc(*read("gb", 0))
            act.wait_ge(*drained("ga", 0))
            link(A(rows[:, 2, 0:SEQ], rows[:, 0, 0:SEQ], ACT.Abs))
            link(A(rows[:, 2, 0:SEQ], rows[:, 2, 0:SEQ], ACT.Exp, scale=-1.0))
            A(p4[:, 0:1], p4[:, 0:1], ACT.Exp)
            A(rows[:, 2, 0:SEQ], rows[:, 2, 0:SEQ], ACT.Ln, bias=1.0).then_inc(S["softplus_ready"], 1)
            act.wait_ge(S["pads_ready"], 2)
            for t in range(12):
                act.wait_ge(*filled("gqkv", t))
                A(graw[:, t, 3:3 + SEQ], bank("gqkv", t)[:, 0:SEQ], ACT.Copy).then_inc(*read("gqkv", t))
            for t in range(8):
                act.wait_ge(*filled("mqk", t))
                A(mq[:, t, :], bank("mqk", t)[:, 0:SEQ], ACT.Copy).then_inc(*read("mqk", t))
            for m in range(TT):
                act.wait_ge(*filled("gz", m))
                A(gz[:, m, :], bank("gz", m)[:], ACT.Sigmoid).then_inc(S["gzsig_ready"], 1)
            for m in range(TT):
                act.wait_ge(*filled("mv", m))
                A(mval[:, m, :], bank("mv", m)[:], ACT.Copy).then_inc(*read("mv", m))
            for g in range(3):
                act.wait_ge(S["gpre_ready"], g + 1)
                A(gsig[:, 4 * g:4 * g + 4, :], gconv[:, 4 * g:4 * g + 4, :], ACT.Sigmoid).then_inc(S["gsilu_ready"], 1)
            for t in range(4):
                act.wait_ge(S["gconv_ready"], t // 2 + 1)
                A(gsq[:, 2 * t:2 * t + 2, :], gconv[:, 2 * t:2 * t + 2, :], ACT.Square).then_inc(S["gsq_ready"], 1)
            for t in range(4):
                act.wait_ge(*filled("nq", t))
                A(gsq[:, 2 * t:2 * t + 2, :].rearrange("p t n -> p (t n)"), bank("nq", t)[:], ACT.Sqrt, bias=eps6)\
                    .then_inc(*read("nq", t))
            for h in range(GH):
                act.wait_ge(S["dlog_ready"], h + 1)
                A(dec[:, h % 2, 0:384], dec[:, h % 2, 0:384], ACT.Exp).then_inc(S["dec_ready"], 1)

            def copy_X(lv, half):
                act.wait_ge(*filled("X", lv, half))
                A(Xb[:, 4 * half:4 * half + 4, :].rearrange("p q n -> p (q n)"), bank("X", lv, half)[:], ACT.Copy)\
                    .then_inc(*read("X", lv, half))

            def softmax(h):
                act.wait_ge(S["logits_ready"], h + 1)
                w = pm[:, h % 2, :]
                A(w[:, 0:P], w[:, 0:P], ACT.Exp, bias=nmax[:, 2 * (h % 2):2 * (h % 2) + 1],
                  accum_out=psum_[:, 2 * (h % 2):2 * (h % 2) + 1])
                A(w[:, P:P + SEQ], w[:, P:P + SEQ], ACT.Exp, bias=nmax[:, 2 * (h % 2) + 1:2 * (h % 2) + 2],
                  accum_out=psum_[:, 2 * (h % 2) + 1:2 * (h % 2) + 2]).then_inc(S["exp_ready"], 1)

            def copy_pT(h):
                act.wait_ge(*filled("pT", h))
                A(pTs[:, h % 2, :], bank("pT", h)[:, 0:384], ACT.Copy).then_inc(*read("pT", h))

            def copy_av(h):
                b = MD * (h % 2)
                act.wait_ge(*filled("av", h))
                A(mix2T[b:b + MD, h // 2, :], bank("av", h)[b:b + MD, 0:SEQ], ACT.Copy).then_inc(*read("av", h))

            for lv in range(LEVELS):
                copy_X(lv, 0)
                copy_X(lv, 1)
                if lv:
                    copy_av(lv - 1)
                softmax(lv)
                copy_pT(lv)
            softmax(MH - 1)
            copy_av(MH - 2)
            copy_pT(MH - 1)
            copy_av(MH - 1)
            act.wait_ge(*filled("U1", 0))
            A(U[:, 0, :, :].rearrange("p h n -> p (h n)"), bank("U1", 0)[:], ACT.Copy).then_inc(*read("U1", 0))
            act.wait_ge(*filled("U2", 0))
            A(U[:, 1, :, :].rearrange("p h n -> p (h n)"), bank("U2", 0)[:], ACT.Copy).then_inc(*read("U2", 0))
            act.wait_ge(S["var_ready"], 5)
            A(std, ss, ACT.Sqrt, bias=eps6, scale=1.0 / GD).then_inc(S["std_ready"], 1)
            for b in range(2):
                act.wait_ge(*filled("obT", b))
                A(mix2T[:, 4 + 2 * b:6 + 2 * b, :].rearrange("p t n -> p (t n)"), bank("obT", b)[:], ACT.Copy,
                  scale=pcol[:, 1, 80:81]).then_inc(*read("obT", b))
            mean_square(2)
            normed_T("x3T", 72)
            for m in range(TT):
                act.wait_ge(S["gmax_ready"], m + 1)
                A(rt[:, 40 * m + 36:40 * m + 40], rl[:, 36 * m:36 * m + 4], ACT.Exp, bias=rt[:, 40 * m:40 * m + 1],
                  accum_out=rt[:, 40 * m + 1:40 * m + 2]).then_inc(S["gexp_ready"], 1)
                act.wait_ge(S["e2_ready"], m + 1)
                A(rt[:, 40 * m + 2:40 * m + 3], rt[:, 40 * m + 2:40 * m + 3], ACT.Exp).then_inc(S["e2exp_ready"], 1)
            for c in range(BLOCKS // 2):
                act.wait_ge(*filled("sT", c))
                A(pslot[:, 2 * c:2 * c + 2, :].rearrange("p b n -> p (b n)"), bank("sT", c)[:], ACT.Copy)\
                    .then_inc(*read("sT", c))

            def copy_gathered():
                for k in range(KT):
                    ins = A(xg[:, k, :], ps[6 + k // 4][:, (k % 4) * CAP:(k % 4 + 1) * CAP], ACT.Copy,
                            scale=pcol[:, 1, 72 + k:73 + k])
                ins.then_inc(S["xg_ready"], 1)

            act.wait_ge(S["gathered"], 1)
            copy_gathered()
            act.wait_ge(S["trips_ready"], 1)
            blocks = act.value_load(trips[0:1, 0:1], min_val=NG, max_val=BLOCKS)
            with act.Fori(0, blocks) as it:
                def copy_hidden(e):
                    act.wait_ge(S["hidT_full"], it * EG + (e + 1))
                    A(hidT[:, e % 2, :], ps[2 + e % 2][:, 0:2 * CAP], ACT.Copy).then_inc(S["hidT_ready"], 1)

                for e in range(EG):
                    act.wait_ge(S["gu_full"], it * EG + (e + 1))
                    A(sg[:, e % 2, :], ps[e % 2][:, 0:EF], ACT.Sigmoid).then_inc(S["sg_ready"], 1)
                    if e >= 1:
                        copy_hidden(e - 1)
                act.wait_ge(S["gathered"], it + 2)
                copy_gathered()
                copy_hidden(EG - 1)
                act.wait_ge(S["moe_down"], it * EG + (EG + 3))
                A(yg[:, 0:512], ps[4][:], ACT.Copy)
                A(yg[:, 512:D], ps[5][:], ACT.Copy).then_inc(S["yg_ready"], 1)
            mean_square(3)

        @block.vector
        def _(dve):
            V = nc.vector
            n_dve = [0]

            def step(ins):
                n_dve[0] += 1
                ins.then_inc(S["dve_chain"], 1)

            def settle():
                dve.wait_ge(S["dve_chain"], n_dve[0])

            def link(ins):
                step(ins)
                settle()

            def stt(out, in0, scalar, in1, op0, op1):
                return V.scalar_tensor_tensor(out=out, in0=in0, scalar=scalar, in1=in1, op0=op0, op1=op1)

            def layer_stats(rows_, k):
                for r, (x, n) in enumerate(rows_):
                    for c in range(2):
                        step(V.bn_stats(stats[0:n, 12 * r + 6 * c:12 * r + 6 * c + 6], x[:, 512 * c:512 * c + 512]))
                settle()
                for r, (x, n) in enumerate(rows_):
                    ins = V.bn_aggr(mv3[0:n, r, :], stats[0:n, 12 * r:12 * r + 12])
                    if r == len(rows_) - 1:
                        ins.then_inc(S["var_ready"], 1)
                    else:
                        step(ins)
                dve.wait_ge(S["std_ready"], k)
                settle()
                link(V.reciprocal(rstd[:, 0:3] if len(rows_) == 3 else rstd[:, 0:2],
                                  std[:, 0:3] if len(rows_) == 3 else std[:, 0:2]))

            link(V.memset(mv, 1.0))
            V.memset(eps5, 1e-5).then_inc(S["eps_ready"], 1)
            V.memset(eps6, 1e-6).then_inc(S["eps_ready"], 1)
            dve.wait_ge(S["x_loaded"], 48)
            layer_stats([(tokA[:, 0, :], P), (tokA[:, 1, :], P), (meta, META)], 1)
            for m in range(TT):
                step(V.tensor_scalar(tokA[:, m, :], tokA[:, m, :], mv3[:, m, 0:1], rstd[:, m:m + 1],
                                     ALU.subtract, ALU.mult))
            settle()
            V.tensor_scalar(meta, meta, mv3[0:META, 2, 0:1], rstd[0:META, 2:3], ALU.subtract, ALU.mult)\
                .then_inc(S["xn_ready"], 1)
            for c, n in ((0, P), (1, NROW1)):
                dve.wait_ge(*filled("prow", c))
                V.tensor_copy(pcol[:, c, 0:n], bank("prow", c)[:, 0:n]).then_inc(*read("prow", c))
            L = [lrow[:, c, :] for c in range(16)]
            lre, lim, dt, zr, th, kk, r, er, sn, sh, t1, t2, lbr, lbi, cr, ci = L
            dve.wait_ge(S["dt_ready"], 1)
            V.tensor_tensor(zr.rearrange("p (a b) -> p a b", a=2), lre.rearrange("p (a b) -> p a b", a=2),
                            ldt[:].unsqueeze(2).broadcast_to([NST, 2, STATE]), ALU.mult).then_inc(S["zr_ready"], 1)
            link(V.tensor_tensor(th.rearrange("p (a b) -> p a b", a=2), lim.rearrange("p (a b) -> p a b", a=2),
                                 ldt[:].unsqueeze(2).broadcast_to([NST, 2, STATE]), ALU.mult))
            link(V.tensor_scalar(kk, th, 1.0 / (2.0 * math.pi), ROUND, ALU.mult, ALU.add))
            link(V.tensor_scalar(kk, kk, -ROUND, None, ALU.add))
            link(stt(r, kk, -TWO_PI_HI, th, ALU.mult, ALU.add))
            link(stt(r, kk, -TWO_PI_MID, r, ALU.mult, ALU.add))
            link(stt(r, kk, -TWO_PI_LO, r, ALU.mult, ALU.add))
            V.tensor_scalar(r, r, 3.1415925, -3.1415925, ALU.min, ALU.max).then_inc(S["angle_ready"], 1)
            step(V.tensor_tensor(t1, lre, lre, ALU.mult))
            step(V.tensor_tensor(t2, lim, lim, ALU.mult))
            settle()
            link(V.tensor_tensor(t1, t1, t2, ALU.add))
            link(V.reciprocal(kk, t1))
            dve.wait_ge(S["er_ready"], 1)
            dve.wait_ge(S["sin_ready"], 2)
            link(V.tensor_tensor(sh, sh, sh, ALU.mult))
            step(V.tensor_tensor(lbi, er, sn, ALU.mult))
            link(V.tensor_scalar(sh, sh, -2.0, 1.0, ALU.mult, ALU.add))
            link(V.tensor_tensor(lbr, er, sh, ALU.mult))
            link(V.tensor_scalar(sh, lbr, -1.0, None, ALU.add))
            step(V.tensor_tensor(t1, sh, lre, ALU.mult))
            step(V.tensor_tensor(t2, lbi, lim, ALU.mult))
            step(V.tensor_tensor(sn, lbi, lre, ALU.mult))
            step(V.tensor_tensor(er, sh, lim, ALU.mult))
            settle()
            step(V.tensor_tensor(t1, t1, t2, ALU.add))
            step(V.tensor_tensor(sn, sn, er, ALU.subtract))
            settle()
            step(V.tensor_tensor(cr, t1, kk, ALU.mult))
            settle()
            V.tensor_tensor(ci, sn, kk, ALU.mult).then_inc(S["poles_ready"], 1)
            dve.wait_ge(S["const_ready"], 2)
            dve.wait_ge(S["bc_loaded"], 64)
            for c in range(2):
                sign = 1.0 - 2.0 * c
                step(V.tensor_scalar(cexp[:, c, :, 0:STATE], craw[:, c, :, :], even, sign, ALU.mult, ALU.mult))
                ins = V.tensor_scalar(cexp[:, c, :, STATE:P], craw[:, c, :, :], odd, sign, ALU.mult, ALU.mult)
                if c:
                    ins.then_inc(S["cexp_ready"], 1)
                else:
                    step(ins)
            dve.wait_ge(*filled("lam", 0))
            V.tensor_copy(lamcol, bank("lam", 0)[:, 0:64]).then_inc(*read("lam", 0))
            dve.wait_ge(*drained("lam", 0))
            ar, ai = lamcol[:, 0:16], lamcol[:, 16:32]
            crc = lamcol[:, 32:48].unsqueeze(2).broadcast_to([P, NST, GRP])
            cic = lamcol[:, 48:64].unsqueeze(2).broadcast_to([P, NST, GRP])
            tmp = [scanR[:, 256 * k:256 * k + 256].rearrange("p (i h) -> p i h", i=NST) for k in range(4)]
            step(V.tensor_tensor(tmp[0], crc, braw[:, 0, :, :], ALU.mult))
            step(V.tensor_tensor(tmp[1], cic, braw[:, 1, :, :], ALU.mult))
            step(V.tensor_tensor(tmp[2], crc, braw[:, 1, :, :], ALU.mult))
            step(V.tensor_tensor(tmp[3], cic, braw[:, 0, :, :], ALU.mult))
            settle()
            dve.wait_ge(S["bexp_zero"], 1)
            for g in range(2):
                p0 = g * STATE
                step(V.tensor_tensor(bexp[p0:p0 + STATE, 0, :, g * GRP:(g + 1) * GRP], tmp[0][p0:p0 + STATE],
                                     tmp[1][p0:p0 + STATE], ALU.subtract))
                ins = V.tensor_tensor(bexp[p0:p0 + STATE, 1, :, g * GRP:(g + 1) * GRP], tmp[2][p0:p0 + STATE],
                                      tmp[3][p0:p0 + STATE], ALU.add)
                step(ins) if g == 0 else ins.then_inc(S["bexp_ready"], 1)
            settle()
            arn = ar.unsqueeze(1)
            ain = ai.unsqueeze(1)
            step(V.tensor_copy(PW[:, 0, 0, :], ar))
            step(V.tensor_copy(PW[:, 1, 0, :], ai))
            settle()
            n = 1
            while n < CHUNK:
                hi = [PW[:, c, n - 1:n, :].broadcast_to([P, n, NST]) for c in range(2)]
                lo = [PW[:, c, 0:n, :] for c in range(2)]
                q = [scanR[:, 128 * k:128 * k + n * NST].rearrange("p (s i) -> p s i", i=NST) for k in range(4)]
                step(V.tensor_tensor(q[0], hi[0], lo[0], ALU.mult))
                step(V.tensor_tensor(q[1], hi[1], lo[1], ALU.mult))
                step(V.tensor_tensor(q[2], hi[0], lo[1], ALU.mult))
                step(V.tensor_tensor(q[3], hi[1], lo[0], ALU.mult))
                settle()
                step(V.tensor_tensor(PW[:, 0, n:2 * n, :], q[0], q[1], ALU.subtract))
                step(V.tensor_tensor(PW[:, 1, n:2 * n, :], q[2], q[3], ALU.add))
                settle()
                n *= 2
            dve.wait_ge(*drained("bu", 2 * NST - 1))

            def times(v, s):
                n = NCH - (s is not None)
                src = (ar, ai)[v] if s is None else PW[:, v, s, :]
                return src.unsqueeze(1).unsqueeze(3).broadcast_to([P, 2, NST, n])

            for s in range(1, CHUNK):
                prev, here = X[:, :, :, s - 1, :], X[:, :, :, s, :]
                step(V.tensor_tensor(T1, prev, times(0, None), ALU.mult))
                step(V.tensor_tensor(T2, prev, times(1, None), ALU.mult))
                settle()
                link(V.tensor_tensor(here, here, T1, ALU.add))
                step(V.tensor_tensor(here[:, 0], here[:, 0], T2[:, 1], ALU.subtract))
                step(V.tensor_tensor(here[:, 1], here[:, 1], T2[:, 0], ALU.add))
                settle()
            link(V.tensor_copy(EN, X[:, :, :, CHUNK - 1, :]))
            a16 = [PW[:, v, CHUNK - 1, :].unsqueeze(1).broadcast_to([P, 2, NST]) for v in range(2)]
            for c in range(1, NCH - 1):
                step(V.tensor_tensor(T1[:, :, :, 0], EN[:, :, :, c - 1], a16[0], ALU.mult))
                step(V.tensor_tensor(T2[:, :, :, 0], EN[:, :, :, c - 1], a16[1], ALU.mult))
                settle()
                link(V.tensor_tensor(EN[:, :, :, c], EN[:, :, :, c], T1[:, :, :, 0], ALU.add))
                step(V.tensor_tensor(EN[:, 0, :, c], EN[:, 0, :, c], T2[:, 1, :, 0], ALU.subtract))
                step(V.tensor_tensor(EN[:, 1, :, c], EN[:, 1, :, c], T2[:, 0, :, 0], ALU.add))
                settle()
            prev = EN[:, :, :, 0:NCH - 1]
            for s in range(CHUNK):
                here = X[:, :, :, s, 1:NCH]
                step(V.tensor_tensor(T1[:, :, :, 1:NCH], prev, times(0, s), ALU.mult))
                step(V.tensor_tensor(T2[:, :, :, 1:NCH], prev, times(1, s), ALU.mult))
                settle()
                link(V.tensor_tensor(here, here, T1[:, :, :, 1:NCH], ALU.add))
                step(V.tensor_tensor(here[:, 0], here[:, 0], T2[:, 1, :, 1:NCH], ALU.subtract))
                ins = V.tensor_tensor(here[:, 1], here[:, 1], T2[:, 0, :, 1:NCH], ALU.add)
                ins.then_inc(S["scan_ready"], 1) if s == CHUNK - 1 else step(ins)
                settle()
            dve.wait_ge(S["v_biased"], 6)
            dve.wait_ge(S["o_biased"], 4)
            dve.wait_ge(*drained("qk", 7))
            for tap in range(4):
                for t in range(8):
                    w = pcol[:, 0, 8 * tap + t:8 * tap + t + 1]
                    if tap == 0:
                        ins = V.tensor_scalar(conv[:, t, :], raw[:, t, 0:LEN], w, pcol[:, 0, 32 + t:33 + t],
                                              ALU.mult, ALU.add)
                    else:
                        ins = stt(conv[:, t, :], raw[:, t, tap:tap + LEN], w, conv[:, t, :], ALU.mult, ALU.add)
                    ins.then_inc(S["conv_ready"], 1) if (tap, t) == (3, 7) else step(ins)
                settle()
            dve.wait_ge(S["silu_ready"], 1)
            half = 4 * LEN
            V.tensor_tensor(convR[:, 0:half], convR[:, 0:half], rawR[:, 0:half], ALU.mult).then_inc(S["qk_ready"], 1)
            stt(convR[:, half:2 * half], convR[:, half:2 * half], DK ** -0.5, rawR[:, half:2 * half],
                ALU.mult, ALU.mult).then_inc(S["qk_ready"], 1)
            for t in range(UT):
                dve.wait_ge(*filled("y", t))
                stt(yu[:, t, :].rearrange("p (s n) -> p s n", s=CHUNK), uTp[:, t, :, 1:NCH], pcol[:, 0, 68 + t:69 + t],
                    bank("y", t)[:, 0:SEQ].rearrange("p (s n) -> p s n", s=CHUNK), ALU.mult, ALU.add)\
                    .then_inc(*read("y", t))
            for t in range(KT):
                dve.wait_ge(S["zsig_ready"], t + 1)
                V.tensor_tensor(mixT[:, t, :], bank("z", t)[:, 0:SEQ], zsig[:, t % 2, :], ALU.mult)\
                    .then_inc(*read("z", t))
                dve.wait_ge(*drained("z", t))
                step(V.tensor_tensor(mixT[:, t, :], mixT[:, t, :], gT[:, t, :], ALU.mult))
            dve.wait_ge(S["softplus_ready"], 1)
            dve.wait_ge(S["rowone_ready"], 1)
            rowones = rowone[:].broadcast_to([HEADS, LEN])
            link(stt(rows[:, 2, :], rows[:, 1, :], 0.0, rows[:, 2, :], ALU.min, ALU.subtract))
            link(V.tensor_tensor_scan(rows[:, 3, :], rowones, rows[:, 2, :], 0.0, ALU.mult, ALU.add))
            link(V.tensor_tensor(rows[:, 0, :], rows[:, 0, :], rows[:, 3, :], ALU.subtract))
            link(V.tensor_tensor_scan(rows[:, 4, :], rows[:, 0, :], rows[:, 0, :], 0.0, ALU.max, ALU.max))
            V.tensor_tensor(rows[:, 5, :], rows[:, 3, :], rows[:, 4, :], ALU.add).then_inc(S["gate_rows_ready"], 1)
            dve.wait_ge(*filled("gm", 0))
            dve.wait_ge(S["em_ready"], 1)
            link(V.tensor_copy(gcol[0:META, 0:4], bank("gm", 0)[0:META, 0:4]))
            V.tensor_copy(gcol[:, 4:12], bank("gm", 0)[:, 4:12]).then_inc(*read("gm", 0))
            dve.wait_ge(*drained("gm", 0))
            for h in range(HEADS):
                b = h % 2
                dve.wait_ge(*filled("ms", h))
                M = bank("ms", h)[:, 0:SEQ]
                V.tensor_scalar(wgt[0:META, b, 0:SEQ], M[0:META], gcol[0:META, h:h + 1], 0.0, ALU.subtract, ALU.max)
                V.tensor_scalar(wgt[:, b, SEQ:2 * SEQ], M, gcol[:, 4 + h:5 + h], 0.0, ALU.subtract, ALU.max)
                V.tensor_scalar(wgt[:, b, 2 * SEQ:640], M[:, P:SEQ], gcol[:, 8 + h:9 + h], 0.0, ALU.subtract, ALU.max)\
                    .then_inc(S["wlog_ready"], 1)
                dve.wait_ge(S["w_ready"], h + 1)
                if h >= 2:
                    dve.wait_ge(*filled("h", 2 * (h - 2) + 1))
                V.tensor_tensor(pt[0:META, b, 0:SEQ], wgt[0:META, b, 0:SEQ], bank("ms", h)[0:META, SEQ:2 * SEQ],
                                ALU.mult).then_inc(*read("ms", h))
                dve.wait_ge(*filled("s", h))
                V.tensor_tensor(pt[:, b, SEQ:640], wgt[:, b, SEQ:640], bank("s", h)[:, 0:384], ALU.mult)\
                    .then_inc(*read("s", h))
                dve.wait_ge(*drained("s", h))
                step(V.tensor_tensor(pt[:, b, SEQ:SEQ + P], pt[:, b, SEQ:SEQ + P], tri[:], ALU.mult))
                V.tensor_tensor(pt[:, b, 2 * SEQ:640], pt[:, b, 2 * SEQ:640], tri[:], ALU.mult)\
                    .then_inc(S["pt_ready"], 1)
                settle()
            for k in range(2 * HEADS):
                h, m = k // 2, k % 2
                dve.wait_ge(*filled("h", k))
                o = bank("h", k)
                link(V.tensor_scalar(rden[:, k:k + 1], o[:, DV:DV + 1], -1.0, None, ALU.mult))
                link(stt(den[:, k:k + 1], o[:, DV:DV + 1], em[:, 4 * m + h:4 * m + h + 1], rden[:, k:k + 1],
                         ALU.max, ALU.max))
                link(V.reciprocal(rden[:, k:k + 1], den[:, k:k + 1]))
                V.tensor_scalar(hm[:, m, h * DV:(h + 1) * DV], o[:, 0:DV], rden[:, k:k + 1], None, ALU.mult)\
                    .then_inc(*read("h", k))
                dve.wait_ge(*drained("h", k))
                step(V.bn_stats(bst[:, 6 * k:6 * k + 6], hm[:, m, h * DV:(h + 1) * DV]))
            settle()
            for k in range(2 * HEADS):
                ins = V.bn_aggr(mvh3[:, k, :], bst[:, 6 * k:6 * k + 6])
                ins.then_inc(S["var_ready"], 1) if k == 2 * HEADS - 1 else step(ins)
            dve.wait_ge(S["std_ready"], 2)
            link(V.reciprocal(rstd, std))
            for k in range(2 * HEADS):
                h, m = k // 2, k % 2
                part = hm[:, m, h * DV:(h + 1) * DV]
                step(V.tensor_scalar(part, part, mvh3[:, k, 0:1], rstd[:, k:k + 1], ALU.subtract, ALU.mult))
            settle()
            dve.wait_ge(S["osig_ready"], 1)
            V.tensor_tensor(hm, hm, tokB[:], ALU.mult).then_inc(S["gated_ready"], 1)
            for t in range(KT):
                dve.wait_ge(*filled("ym", t))
                V.tensor_tensor(ymg[:, t % 2, :], bank("ym", t)[:, 0:SEQ], gT[:, 8 + t, :], ALU.mult)\
                    .then_inc(*read("ym", t))
                dve.wait_ge(*drained("ym", t))
                settle()
                V.tensor_tensor(mixT[:, t, :], mixT[:, t, :], ymg[:, t % 2, :], ALU.add).then_inc(S["mix_ready"], 1)
            dve.wait_ge(S["h0_ready"], 1)
            for k in range(4):
                m, n = k % 2, k // 2
                dve.wait_ge(*filled("wo", k))
                part = tokA[:, m, 512 * n:512 * n + 512]
                stt(part, part, ALPHA, bank("wo", k)[:], ALU.mult, ALU.add).then_inc(*read("wo", k))
            for k in range(4):
                dve.wait_ge(*drained("wo", k))

            def normalised(count, k):
                layer_stats([(tokA[:, m, :], P) for m in range(TT)], k)
                for m in range(TT):
                    ins = V.tensor_scalar(tokB[:, m, :], tokA[:, m, :], mv3[:, m, 0:1], rstd[:, m:m + 1],
                                          ALU.subtract, ALU.mult)
                    if m == TT - 1 and count:
                        ins.then_inc(S["xn_ready"], 1)
                    else:
                        step(ins)
                if count:
                    dve.wait_ge(S["xn_ready"], count)
                settle()

            normalised(2, 3)
            dve.wait_ge(S["h1_ready"], 1)
            dve.sem_inc(S["ffn_added"], 1)
            with dve.Fori(0, FF // 256 // SLOTS) as it:
                for q in range(SLOTS):
                    for m in range(2):
                        dve.wait_ge(S["relu_ready"], it * (2 * SLOTS) + (2 * q + m + 1))
                        half = ffr[:, q % 2, m * SEQ:(m + 1) * SEQ]
                        V.tensor_tensor(ffh[:, q % 2, m * SEQ:(m + 1) * SEQ], half, half, ALU.mult)\
                            .then_inc(S["relu2_ready"], 1)
                    dve.wait_ge(S["ffn_down"], it * SLOTS + (q + 1))
                    for m in range(TT):
                        for n in range(2):
                            part = tokA[:, m, 512 * n:512 * n + 512]
                            last = V.tensor_tensor(part, part, ps[4 + 2 * m + n][:], ALU.add)
                            if (m, n) == (1, 1):
                                last.then_inc(S["ffn_added"], 1)
                            else:
                                last.then_inc(S["ffn_part_added"], 1)
                    dve.wait_ge(S["ffn_added"], it * SLOTS + (q + 2))
            normalised(0, 4)
            dve.wait_ge(S["bc_rows_loaded"], 96)
            for m in range(TT):
                step(V.tensor_tensor(tokA[:, m, :], tokB[:, m, :], bcL[:, 0, :], ALU.mult))
            settle()
            for m in range(TT):
                ins = V.tensor_tensor(tokA[:, m, :], tokA[:, m, :], bcL[:, 1, :], ALU.add)
                ins.then_inc(S["res_ready"], 1) if m else step(ins)

            def rms(count, k):
                dve.wait_ge(S["std_ready"], k)
                link(V.reciprocal(rstd[:, 0:2], std[:, 0:2]))
                for m in range(TT):
                    ins = V.tensor_scalar(tokB[:, m, :], tokA[:, m, :], rstd[:, m:m + 1], None, ALU.mult)
                    ins.then_inc(S["xn_ready"], 1) if m and count else step(ins)

            rms(3, 5)
            dve.wait_ge(S["softplus_ready"], 2)
            link(stt(rows[:, 1, 0:SEQ], rows[:, 0, 0:SEQ], 0.0, rows[:, 2, 0:SEQ], ALU.max, ALU.add))
            link(V.tensor_scalar(rows[:, 1, 0:SEQ], rows[:, 1, 0:SEQ], p4[:, 0:1], -1.0, ALU.mult, ALU.mult))
            V.tensor_tensor_scan(rows[:, 3, 0:SEQ], rowone[:].broadcast_to([GH, SEQ]), rows[:, 1, 0:SEQ], 0.0, ALU.mult, ALU.add)\
                .then_inc(S["decay_rows_ready"], 1)
            for g in range(3):
                dve.wait_ge(*drained("gqkv", 4 * g + 3))
                for tap in range(4):
                    for t in range(4 * g, 4 * g + 4):
                        w = pcol[:, 1, 12 * tap + t:12 * tap + t + 1]
                        if tap == 0:
                            ins = V.tensor_scalar(gconv[:, t, :], graw[:, t, 0:SEQ], w, None, ALU.mult)
                        else:
                            ins = stt(gconv[:, t, :], graw[:, t, tap:tap + SEQ], w, gconv[:, t, :], ALU.mult, ALU.add)
                        ins.then_inc(S["gpre_ready"], 1) if (tap, t) == (3, 4 * g + 3) else step(ins)
                    settle()
            dve.wait_ge(*filled("Gc", 0))
            V.tensor_copy(gc, bank("Gc", 0)[:, 0:16]).then_inc(*read("Gc", 0))
            for m in range(TT):
                dve.wait_ge(S["gzsig_ready"], m + 1)
                V.tensor_tensor(gz[:, m, :], gz[:, m, :], bank("gz", m)[:], ALU.mult).then_inc(*read("gz", m))
            for g in range(3):
                dve.wait_ge(S["gsilu_ready"], g + 1)
                V.tensor_tensor(gconv[:, 4 * g:4 * g + 4, :], gconv[:, 4 * g:4 * g + 4, :], gsig[:, 4 * g:4 * g + 4, :],
                                ALU.mult).then_inc(S["gconv_ready"], 1)
            for t in range(4):
                dve.wait_ge(*drained("nq", t))
                n2 = gsq[:, 2 * t:2 * t + 2, :]
                link(V.reciprocal(n2, n2))
                stt(gconv[:, 2 * t:2 * t + 2, :], gconv[:, 2 * t:2 * t + 2, :], GD ** -0.5 if t < 2 else 1.0, n2,
                    ALU.mult, ALU.mult).then_inc(S["gnorm_ready"], 1)
            dve.wait_ge(*drained("Gc", 0))
            for m in range(TT):
                dve.wait_ge(*filled("vk", m))
                for h in range(GH):
                    ins = V.tensor_scalar(vb[:, m, h, :], bank("vk", m)[:, h * P:(h + 1) * P],
                                          gc[:, 8 + 4 * m + h:9 + 4 * m + h], None, ALU.mult)
                    if h == GH - 1:
                        ins.then_inc(*read("vk", m))
                    else:
                        step(ins)
            for q in range(8):
                step(V.tensor_copy(Tm[:, q, :], ident[:]))
                ins = V.tensor_copy(Tt[:, q, :], ident[:])
                ins.then_inc(S["T_init"], 1) if q == 7 else step(ins)
            for h in range(GH):
                b = h % 2
                dve.wait_ge(*filled("gb_", h))
                G, beta = bank("gb_", h)[:, 0:SEQ], bank("gb_", h)[:, SEQ:2 * SEQ]
                V.tensor_scalar(dec[:, b, 0:SEQ], G, gc[:, h:h + 1], 0.0, ALU.subtract, ALU.min)
                V.tensor_scalar(dec[:, b, SEQ:384], G[:, P:SEQ], gc[:, 4 + h:5 + h], 0.0, ALU.subtract, ALU.min)\
                    .then_inc(S["dlog_ready"], 1)
                dve.wait_ge(S["dec_ready"], h + 1)
                dve.wait_ge(*filled("kk", h))
                V.tensor_tensor(aT[:, h, :], dec[:, b, 0:384], bank("kk", h)[:, 0:384], ALU.mult).then_inc(*read("kk", h))
                dve.wait_ge(*filled("qk_", h))
                V.tensor_tensor(qkT[:, h, :], dec[:, b, 0:384], bank("qk_", h)[:, 0:384], ALU.mult)\
                    .then_inc(*read("qk_", h))
                dve.wait_ge(*drained("kk", h))
                step(V.tensor_tensor(aT[:, h, SEQ:384], aT[:, h, SEQ:384], beta[:, P:SEQ], ALU.mult))
                V.tensor_tensor(aT[:, h, 0:SEQ], aT[:, h, 0:SEQ], beta, ALU.mult).then_inc(*read("gb_", h))
                dve.wait_ge(*drained("gb_", h))
                dve.wait_ge(*drained("qk_", h))
                settle()
                step(V.tensor_tensor(qkT[:, h, 0:P], qkT[:, h, 0:P], tri[:], ALU.mult))
                step(V.tensor_tensor(qkT[:, h, SEQ:384], qkT[:, h, SEQ:384], tri[:], ALU.mult))
                step(V.tensor_tensor(aT[:, h, 0:P], aT[:, h, 0:P], stri[:], ALU.mult))
                settle()
                V.tensor_tensor(aT[:, h, SEQ:384], aT[:, h, SEQ:384], stri[:], ALU.mult).then_inc(S["aT_ready"], 1)

            def logits(h):
                w, o, nm = pm[:, h % 2, :], bank("sc", h), nmax[:, 2 * (h % 2):2 * (h % 2) + 2]
                if h >= 2:
                    dve.wait_ge(*filled("pT", h - 2))
                dve.wait_ge(*filled("sc", h))
                step(stt(w[:, 0:P], o[:, 0:P], MD ** -0.5, negm[:], ALU.mult, ALU.add))
                step(V.tensor_scalar(w[:, P:SEQ], o[:, P:SEQ], MD ** -0.5, None, ALU.mult))
                stt(w[:, SEQ:384], o[:, SEQ:384], MD ** -0.5, negm[:], ALU.mult, ALU.add).then_inc(*read("sc", h))
                settle()
                dve.wait_ge(*drained("sc", h))
                step(V.tensor_reduce(nm[:, 0:1], w[:, 0:P], AX.X, ALU.max, negate=True))
                settle()
                V.tensor_reduce(nm[:, 1:2], w[:, P:384], AX.X, ALU.max, negate=True).then_inc(S["logits_ready"], 1)

            def probs(h):
                w, c = pm[:, h % 2, :], 2 * (h % 2)
                dve.wait_ge(S["exp_ready"], h + 1)
                link(V.reciprocal(prec[:, c:c + 2], psum_[:, c:c + 2]))
                step(V.tensor_scalar(w[:, 0:P], w[:, 0:P], prec[:, c:c + 1], None, ALU.mult))
                settle()
                V.tensor_scalar(w[:, P:384], w[:, P:384], prec[:, c + 1:c + 2], None, ALU.mult)\
                    .then_inc(S["probs_ready"], 1)

            dve.wait_ge(S["masks_ready"], 1)
            for lv in range(LEVELS):
                logits(lv)
                for half in range(2):
                    m4 = lvl[:, lv, :].unsqueeze(1).broadcast_to([P, 4, P])
                    for name, M in (("Z", Tm), ("ZT", Tt)):
                        part = M[:, 4 * half:4 * half + 4, :]
                        dve.wait_ge(*filled(name, lv, half))
                        V.tensor_tensor(Zm[:, 0:4, :] if name == "Z" else Zm[:, 4:8, :],
                                        bank(name, lv, half)[:].rearrange("p (q n) -> p q n", q=4), m4, ALU.mult)\
                            .then_inc(*read(name, lv, half))
                    dve.wait_ge(*drained("Z", lv, half))
                    dve.wait_ge(*drained("ZT", lv, half))
                    step(V.tensor_tensor(Tm[:, 4 * half:4 * half + 4, :], Tm[:, 4 * half:4 * half + 4, :],
                                         Zm[:, 0:4, :], ALU.subtract))
                    settle()
                    V.tensor_tensor(Tt[:, 4 * half:4 * half + 4, :], Tt[:, 4 * half:4 * half + 4, :],
                                    Zm[:, 4:8, :], ALU.subtract).then_inc(S["T_ready"], 1)
                    if half == 0:
                        probs(lv)
                    dve.wait_ge(S["T_ready"], 2 * lv + half + 1)
            logits(MH - 1)
            probs(MH - 1)
            dve.wait_ge(*filled("AU", 0))
            V.tensor_tensor(vb[:, 1, :, :].rearrange("p h n -> p (h n)"), vb[:, 1, :, :].rearrange("p h n -> p (h n)"),
                            bank("AU", 0)[:], ALU.subtract).then_inc(*read("AU", 0))
            for m in range(TT):
                dve.wait_ge(*filled("O", m))
                V.tensor_copy(ob[:, m, :, :].rearrange("p h n -> p (h n)"), bank("O", m)[:]).then_inc(*read("O", m))
                dve.wait_ge(*drained("O", m))
                link(V.tensor_tensor(Zm[:, 0:4, :], ob[:, m, :, :], ob[:, m, :, :], ALU.mult))
                ins = V.tensor_reduce(ss[:, 4 * m:4 * m + 4], Zm[:, 0:4, :], AX.X, ALU.add)
                ins.then_inc(S["var_ready"], 1) if m else link(ins)
            dve.wait_ge(S["std_ready"], 6)
            link(V.reciprocal(rstd, std))
            for m in range(TT):
                link(V.tensor_tensor(ob[:, m, :, :], ob[:, m, :, :],
                                     rstd[:, 4 * m:4 * m + 4].unsqueeze(2).broadcast_to([P, GH, GD]), ALU.mult))
                ins = V.tensor_tensor(ob[:, m, :, :].rearrange("p h n -> p (h n)"),
                                      ob[:, m, :, :].rearrange("p h n -> p (h n)"), gz[:, m, :], ALU.mult)
                ins.then_inc(S["ob_ready"], 1) if m else step(ins)
            for k in range(4):
                m, n = k % 2, k // 2
                dve.wait_ge(*filled("wout", k))
                part = tokA[:, m, 512 * n:512 * n + 512]
                V.tensor_tensor(part, part, bank("wout", k)[:], ALU.add).then_inc(*read("wout", k))
            for k in range(4):
                dve.wait_ge(*drained("wout", k))
            link(V.memset(rt, 0.0))
            dve.sem_inc(S["res_ready"], 1)
            rms(4, 7)
            for m in range(TT):
                R = rt[:, 40 * m:40 * m + 40]
                lg = rl[:, 36 * m:36 * m + 36]
                dve.wait_ge(*filled("rt", m))
                V.tensor_copy(lg, bank("rt", m)[:, 0:36]).then_inc(*read("rt", m))
                dve.wait_ge(*drained("rt", m))
                groups, experts = lg[:, 0:NG], lg[:, NG:36].rearrange("p (g e) -> p g e", g=NG)
                ngmax, gsum, e2, top1, top2, w0, fg = (R[:, 0:1], R[:, 1:2], R[:, 2:3], R[:, 3:4], R[:, 4:5], R[:, 5:6],
                                                      R[:, 6:10])
                eq, f1, f2, ig = R[:, 10:18], R[:, 18:26], R[:, 26:34], rig[:, m, :]

                def first_max(out, x, top, n):
                    link(V.tensor_scalar(eq[:, 0:n], x, top, None, ALU.is_equal))
                    link(V.tensor_tensor_scan(rcum[:, 0:n], rone[:, 0:n], eq[:, 0:n], 0.0, ALU.mult, ALU.add))
                    link(stt(out, rcum[:, 0:n], 1.0, eq[:, 0:n], ALU.is_equal, ALU.mult))

                fg = fgs[:, m, :]
                V.tensor_reduce(ngmax, groups, AX.X, ALU.max, negate=True).then_inc(S["gmax_ready"], 1)
                link(V.tensor_reduce(top1, groups, AX.X, ALU.max))
                first_max(fg, groups, top1, NG)
                link(V.tensor_tensor(rmul[:], experts, fg.unsqueeze(2).broadcast_to([P, NG, EG]), ALU.mult))
                link(V.tensor_reduce(ig, rmul[:].rearrange("p g e -> p e g"), AX.X, ALU.add))
                link(V.tensor_reduce(top1, ig, AX.X, ALU.max))
                first_max(f1, ig, top1, EG)
                link(stt(ig, f1, 2.0 * NEG, ig, ALU.mult, ALU.add))
                link(V.tensor_reduce(top2, ig, AX.X, ALU.max))
                first_max(f2, ig, top2, EG)
                V.tensor_tensor(e2, top2, top1, ALU.subtract).then_inc(S["e2_ready"], 1)
                dve.wait_ge(S["gexp_ready"], m + 1)
                dve.wait_ge(S["e2exp_ready"], m + 1)
                link(V.tensor_scalar(w0, e2, 1.0, gsum, ALU.add, ALU.mult))
                link(V.reciprocal(w0, w0))
                link(V.tensor_scalar(f2, f2, e2, None, ALU.mult))
                link(V.tensor_tensor(f1, f1, f2, ALU.add))
                V.tensor_scalar(wtok[:, m, :], f1, w0, None, ALU.mult).then_inc(S["group_ready"], 1)
            dve.wait_ge(*filled("cum", 0))
            o = bank("cum", 0)
            for m in range(TT):
                link(V.tensor_tensor(rmul[:, 0, 0:NG], fgs[:, m, :], o[:, NG * m:NG * (m + 1)], ALU.mult))
                link(V.tensor_reduce(rank[:, m:m + 1], rmul[:, 0, 0:NG], AX.X, ALU.add))
                link(V.tensor_scalar(rank[:, m:m + 1], rank[:, m:m + 1], -1.0, None, ALU.add))
                step(V.tensor_scalar(rank[:, 2 + m:3 + m], rank[:, m:m + 1], -float(CAP), None, ALU.add))
            V.tensor_reduce(count[:, 0:1], o[:, 2 * NG:3 * NG], AX.X, ALU.max).then_inc(*read("cum", 0))
            dve.wait_ge(*drained("cum", 0))
            settle()
            link(V.tensor_scalar(count[:, 1:2], count[:, 0:1], CAP + 0.5, float(NG), ALU.is_gt, ALU.mult))
            V.tensor_scalar(trips[:], count[0:1, 1:2], float(NG), None, ALU.add).then_inc(S["trips_ready"], 1)
            dve.wait_ge(S["iota_ready"], 1)
            for m in range(TT):
                for b in range(BLOCKS):
                    r, g = b // NG, b % NG
                    ins = V.tensor_scalar(ptok[:, m, b, :], iota, rank[:, 2 * r + m:2 * r + m + 1],
                                          fgs[:, m, g:g + 1], ALU.is_equal, ALU.mult)
                    step(ins)
            settle()
            V.memset(ptok[:, :, BLOCKS, :], 0.0).then_inc(S["ptok_ready"], 1)
            dve.wait_ge(*filled("comb", 0))
            V.tensor_copy(wslot, bank("comb", 0)[:, 0:BLOCKS * EG]).then_inc(*read("comb", 0))
            dve.wait_ge(*drained("comb", 0))

            def add_back(m, at):
                dve.wait_ge(S["put_back"], at + (m + 1))
                for n in range(2):
                    part = tokA[:, m, 512 * n:512 * n + 512]
                    ins = V.tensor_tensor(part, part, ps[6 + n][:], ALU.add)
                    ins.then_inc(S["added_back"] if n else S["half_added_back"], 1)

            dve.wait_ge(*drained("sT", BLOCKS // 2 - 1))
            dve.sem_inc(S["added_back"], 1)
            blocks = dve.value_load(trips[0:1, 0:1], min_val=NG, max_val=BLOCKS)
            with dve.Fori(0, blocks) as it:
                for e in range(EG):
                    o, q = ps[e % 2], e % 2
                    dve.wait_ge(S["sg_ready"], it * EG + (e + 1))
                    V.tensor_tensor(sg[:, q, :], sg[:, q, :], o[:, 0:EF], ALU.mult).then_inc(S["silu_gate"], 1)
                    dve.wait_ge(S["silu_gate"], it * EG + (e + 1))
                    stt(hid[:, q, :], o[:, EF:2 * EF], wslot[:, bass.ds(it * EG + e, 1)], sg[:, q, :],
                        ALU.mult, ALU.mult).then_inc(S["hidden_ready"], 1)
                    if e == 2:
                        add_back(0, it * 2)
                    if e == 4:
                        add_back(1, it * 2)
                V.tensor_copy(pcur, pslot[:, bass.ds(it, 1), :].rearrange("p b n -> p (b n)"))\
                    .then_inc(S["pcur_ready"], 1)
            for m in range(TT):
                add_back(m, blocks * 2)
            dve.wait_ge(S["added_back"], blocks * 2 + 3)
            dve.sem_inc(S["res_ready"], 1)
            rms(0, 8)
            settle()
            dve.wait_ge(S["bc_rows_loaded"], 112)
            for m in range(TT):
                V.tensor_tensor(tokB[:, m, :], tokB[:, m, :], bcL[:, 0, :], ALU.mult).then_inc(S["out_ready"], 1)

        @block.gpsimd
        def _(pool):
            G = nc.gpsimd
            n_pool = [0]

            def link(ins):
                n_pool[0] += 1
                ins.then_inc(S["pool_chain"], 1)
                pool.wait_ge(S["pool_chain"], n_pool[0])

            def rows_of(t, r0, src, n):
                pool.dma_start(prow[r0:r0 + n, t, :], src).then_inc(S["prow_loaded"], 16)

            def lane(v):
                return v.rearrange("(t p) -> t p", p=P)

            b_in = a["b_in"][0]
            rows_of(0, 0, a["qk_conv_w"][0].rearrange("i (t p) -> (i t) p", p=P), 32)
            rows_of(0, 32, lane(a["qk_conv_b"][0]), 8)
            rows_of(0, 40, lane(b_in[C_U:C_V]), 12)
            rows_of(0, 52, lane(b_in[C_G:C_G + 2 * D]), 16)
            rows_of(0, 68, lane(a["s5_d"][0]), 4)
            rows_of(0, 72, lane(a["b_up"][0]), 32)
            rows_of(0, 104, lane(a["ln0_g"]), 8)
            rows_of(0, 112, lane(a["ln0_b"]), 8)
            rows_of(0, 120, lane(a["m_norm_g"][0]), 8)
            rows_of(1, 0, a["conv_w_2"][0].rearrange("i (t p) -> (i t) p", p=P), 48)
            rows_of(1, 48, lane(a["ln1_g"][0]), 8)
            rows_of(1, 56, lane(a["ln1_b"][0]), 8)
            rows_of(1, 64, lane(a["attn_norm_2"][0]), 8)
            rows_of(1, 72, lane(a["ffn_norm_2"][0]), 8)
            rows_of(1, 80, lane(a["gdn_norm_2"][0]), 1)
            link(G.memset(ident[:], 0.0))
            G.affine_select(out=ident[:], in_=ident[:], compare_op=ALU.not_equal, fill=1.0, base=0,
                            pattern=[[-1, P]], channel_multiplier=1).then_inc(S["const_ready"], 1)
            link(G.memset(parity, 1.0))
            link(G.affine_select(out=parity, in_=parity, compare_op=ALU.is_ge, fill=0.0, base=-GRP,
                                 pattern=[[-2 * GRP, 4]], channel_multiplier=1))
            link(G.affine_select(out=parity, in_=parity, compare_op=ALU.is_ge, fill=0.0, base=2 * GRP - 1,
                                 pattern=[[2 * GRP, 4]], channel_multiplier=-1))
            link(G.tensor_tensor(parity[:, 0:2], parity[:, 0:2], parity[:, 2:4], ALU.add))
            link(G.tensor_tensor(odd, parity[:, 0:1], parity[:, 1:2], ALU.add))
            G.tensor_scalar(even, odd, -1.0, 1.0, ALU.mult, ALU.add).then_inc(S["const_ready"], 1)
            G.memset(bexp, 0.0).then_inc(S["bexp_zero"], 1)
            pool.dma_start(wif[:], a["w_in"][0, :, C_I:C_G].rearrange("(k p) n -> p k n", p=P),
                           allow_slow_non_contiguous=True).then_inc(S["small_loaded"], 16)
            pool.dma_start(wif2[:], a["w_in_2"][0, :, C2_GA:C2_GA + 8].rearrange("(k p) n -> p k n", p=P),
                           allow_slow_non_contiguous=True).then_inc(S["small_loaded"], 16)
            pool.dma_start(bif[:], b_in[C_I:C_G].rearrange("(c h) -> h c", c=2),
                           allow_slow_non_contiguous=True).then_inc(S["small_loaded"], 16)
            pool.dma_start(wr[:, :, 0:NG], a["w_group_2"][0].rearrange("(k p) n -> p k n", p=P),
                           allow_slow_non_contiguous=True).then_inc(S["small_loaded"], 16)
            pool.dma_start(wr[:, :, NG:NG + NE], a["w_router_2"][0].rearrange("(k p) n -> p k n", p=P),
                           allow_slow_non_contiguous=True).then_inc(S["small_loaded"], 16)
            pool.dma_start(p4[:, 0:1], a["A_log_2"][0].rearrange("(h a) -> h a", a=1),
                           allow_slow_non_contiguous=True).then_inc(S["small_loaded"], 16)
            pool.dma_start(p4[:, 1:2], a["dt_bias_2"][0].rearrange("(h a) -> h a", a=1),
                           allow_slow_non_contiguous=True).then_inc(S["small_loaded"], 16)
            for c, v in enumerate((a["ln0_g"], a["ln0_b"])):
                pool.dma_start(bc0[:, c, :], v.partition_broadcast(P)).then_inc(S["bc_rows_loaded"], 16)
            pool.dma_start(convR[:, 0:2 * D], b_in[C_V:C_I].partition_broadcast(P))\
                .then_inc(S["bcvo_loaded"], 16)
            G.memset(rowone[:], 1.0).then_inc(S["rowone_ready"], 1)
            G.memset(raw[:, :, 0:3], 0.0).then_inc(S["pads_ready"], 1)
            link(G.memset(sel[:], 1.0))
            link(G.affine_select(out=sel[:], in_=sel[:], compare_op=ALU.is_equal, fill=0.0, base=0,
                                 pattern=[[-1, HEADS], [0, P]], channel_multiplier=1))
            for m, base, op, fill in ((tri, 0, ALU.is_ge, 0.0), (stri, 0, ALU.is_gt, 0.0)):
                link(G.memset(m[:], 1.0))
                link(G.affine_select(out=m[:], in_=m[:], compare_op=op, fill=fill, base=base,
                                     pattern=[[1, P]], channel_multiplier=-1))
            link(G.memset(negm[:], 0.0))
            link(G.affine_select(out=negm[:], in_=negm[:], compare_op=ALU.is_ge, fill=NEG, base=0,
                                 pattern=[[-1, P]], channel_multiplier=1))
            link(G.memset(ones[:], 1.0))
            link(G.memset(rone[:], 1.0))
            pool.wait_ge(*drained("xT", KT - 1))
            G.memset(vaug[:, :, :, DV:DV + 1], 1.0).then_inc(S["ones_column_ready"], 1)
            pool.wait_ge(S["bc_rows_loaded"], 32)
            for m in range(TT):
                link(G.tensor_tensor(tokA[:, m, :], tokA[:, m, :], bc0[:, 0, :], ALU.mult))
                link(G.tensor_tensor(tokA[:, m, :], tokA[:, m, :], bc0[:, 1, :], ALU.add))
            pool.sem_inc(S["h0_ready"], 1)
            for lv in range(LEVELS + 1):
                s = 1 << lv
                nb = P // s
                m = blk[:].rearrange("p (b n) -> p b n", n=s)
                link(G.memset(blk[:], 1.0))
                link(G.affine_select(out=m, in_=m, compare_op=ALU.is_ge, fill=0.0, base=0,
                                     pattern=[[-s, nb], [0, s]], channel_multiplier=1))
                link(G.affine_select(out=m, in_=m, compare_op=ALU.is_ge, fill=0.0, base=s - 1,
                                     pattern=[[s, nb], [0, s]], channel_multiplier=-1))
                if lv < LEVELS:
                    link(G.tensor_scalar(lvl[:, lv, :], blk[:], -1.0, None, ALU.mult))
                if lv:
                    link(G.tensor_tensor(lvl[:, lv - 1, :], lvl[:, lv - 1, :], blk[:], ALU.add))
            pool.sem_inc(S["masks_ready"], 1)
            pool.wait_ge(S["bcvo_loaded"], 16)
            for k in range(6):
                n = META if k % 3 == 0 else P
                c = k // 3
                pool.wait_ge(*drained("v", k))
                part = vaug[0:n, k % 3, 2 * c:2 * c + 2, 0:DV]
                G.tensor_tensor(part, part, bcvo[0:n, 0, 512 * c:512 * c + 512].rearrange("p (h n) -> p h n", h=2),
                                ALU.add).then_inc(S["v_biased"], 1)
            for k in range(4):
                c = k // 2
                pool.wait_ge(*drained("o", k))
                part = tokB[:, k % 2, 512 * c:512 * c + 512]
                G.tensor_tensor(part, part, bcvo[:, 1, 512 * c:512 * c + 512], ALU.add).then_inc(S["o_biased"], 1)
            pool.wait_ge(S["gated_ready"], 1)
            for c, v in enumerate((a["ln1_g"][0], a["ln1_b"][0])):
                pool.dma_start(bcL[:, c, :], v.partition_broadcast(P)).then_inc(S["bc_rows_loaded"], 16)
            pool.wait_ge(S["bc_rows_loaded"], 64)
            pool.wait_ge(S["xn_ready"], 2)
            for m in range(TT):
                link(G.tensor_tensor(tokA[:, m, :], tokB[:, m, :], bcL[:, 0, :], ALU.mult))
                link(G.tensor_tensor(tokA[:, m, :], tokA[:, m, :], bcL[:, 1, :], ALU.add))
                link(G.tensor_scalar(tokA[:, m, :], tokA[:, m, :], ALPHA, None, ALU.mult))
            pool.sem_inc(S["h1_ready"], 1)
            for c, v in enumerate((a["ln2_g"][0], a["ln2_b"][0])):
                pool.dma_start(bcL[:, c, :], v.partition_broadcast(P)).then_inc(S["bc_rows_loaded"], 16)
            pool.wait_ge(S["xn_ready"], 3)
            G.memset(graw[:, :, 0:3], 0.0).then_inc(S["pads_ready"], 1)
            pool.wait_ge(S["xn_ready"], 4)
            G.iota(iota, pattern=[[1, CAP]], base=0, channel_multiplier=0, allow_small_or_imprecise_dtypes=True)\
                .then_inc(S["iota_ready"], 1)
            G.memset(yg, 0.0).then_inc(S["yg_ready"], 1)
            G.memset(pcur, 0.0).then_inc(S["pcur_ready"], 1)
            pool.dma_start(bcL[:, 0, :], a["final_norm_2"].partition_broadcast(P)).then_inc(S["bc_rows_loaded"], 16)


_INS = ["x", "meta_tokens", "ln0_g", "ln0_b", "w_in", "b_in", "qk_conv_w", "qk_conv_b", "s5_lambda_re",
        "s5_lambda_im", "s5_log_dt", "s5_b_re", "s5_b_im", "s5_c_re", "s5_c_im", "s5_d", "s5_w_glu", "m_norm_g",
        "m_w_out", "w_o", "ln1_g", "ln1_b", "w_up", "b_up", "w_down", "ln2_g", "ln2_b", "attn_norm_2", "w_in_2",
        "conv_w_2", "A_log_2", "dt_bias_2", "gdn_norm_2", "w_out_2", "ffn_norm_2", "w_group_2", "w_router_2",
        "w_gate_2", "w_up_2", "w_down_2", "final_norm_2"]


def kernel(**inputs):
    import numpy as np
    import concourse.bacc as bacc
    from concourse.bass_utils import run_bass_kernel_spmd

    nc = bacc.Bacc("TRN2", target_bir_lowering=False, num_devices=1)
    arrays, args = {}, {}
    for name in _INS:
        v = np.ascontiguousarray(inputs[name])
        arrays[f"in_{name}"] = v
        args[name] = nc.dram_tensor(f"in_{name}", v.shape, mybir.dt.from_np(v.dtype), kind="ExternalInput").ap()
    args["out"] = nc.dram_tensor("out", (1, SEQ, D), FP32, kind="ExternalOutput").ap()
    build(nc, args)
    r = run_bass_kernel_spmd(nc, [arrays], core_ids=[0])
    return r.results[0]["out"]
```

```python
from contextlib import ExitStack
import math

import concourse.bass as bass
from concourse import mybir

FP32 = mybir.dt.float32
FP32R = mybir.dt.float32r
I32 = mybir.dt.int32
ALU = mybir.AluOpType
ACT = mybir.ActivationFunctionType
AX = mybir.AxisListType

P = 128
D = 1024
KT = D // P
SEQ = 256
META = 16
LEN = META + SEQ
TT = SEQ // P
CHUNK = 16
NCH = LEN // CHUNK
S5W, GRP, STATE = 512, 16, 64
NST = (S5W // GRP) * STATE // P
UT = S5W // P
HEADS, DK, DV = 4, 128, 256
FF = 4096
ALPHA = 2.0 ** 0.25
MH, MD = 8, 64
GH, GD = 4, 128
NE, EG, NG, EF = 32, 8, 4, 256
SLOTS = 4
CAP = 128
ROUNDS = SEQ // CAP
BLOCKS = NG * ROUNDS
PROW_DMAS, SMALL_DMAS = 15, 7
LEVELS = 7
NEG = -1.0e30
C_U, C_QK, C_V, C_O, C_I, C_F, C_G = 0, 512, 1536, 2560, 3584, 3588, 3592
C2_MQ, C2_MK, C2_MV, C2_GQKV, C2_GZ, C2_GA, C2_GB = 0, 512, 1024, 1536, 3072, 3584, 3588
TWO_PI_HI, TWO_PI_MID, TWO_PI_LO = 6.28125, 0.0019350051879882812, 3.0199159819567e-07
ROUND = 1.5 * 2.0 ** 23


def stream_plan():
    plan = [("u", 0, 1)]
    plan += [("qk", i, 1) for i in range(2)]
    plan += [("v", i, 1) for i in range(2)]
    plan += [("o", i, 1) for i in range(2)]
    plan += [("g", i, 1) for i in range(3)]
    plan += [("glu", i, 2) for i in range(2)]
    plan += [("g", 3, 1)]
    plan += [("mout", i, 1) for i in range(2)]
    plan += [("wo", i, 1) for i in range(2)]
    plan += [("ffn", i, 2) for i in range(FF // 256)]
    plan += [("gqkv", i, 1) for i in range(3)]
    plan += [("mqk", i, 1) for i in range(2)]
    plan += [("mv", 0, 1), ("gz", 0, 1)]
    plan += [("wout", i, 1) for i in range(2)]
    for e in range(NE):
        plan += [("gu", e, 2), ("dn", e, 1)]
    return plan


STREAM = stream_plan()
CHUNK_AT = {(n, i): at for at, (n, i, _) in enumerate(STREAM)}


def loaded_count(at):
    return 16 * sum(d for k, (_, _, d) in enumerate(STREAM[:at + 1]) if k % SLOTS == at % SLOTS)


def bank_plan():
    order = [("prow", 0), ("prow", 1)] + [("xT", t) for t in range(KT)] + [("lam", 0)]
    order += [("u", t) for t in range(UT)] + [("bT", 0), ("bT", 1), ("cT", 0), ("cT", 1)]
    order += [("bu", k) for k in range(2 * NST)]
    order += [("qk", t) for t in range(8)] + [("i", 0), ("f", 0)]
    order += [("v", k) for k in range(6)] + [("o", k) for k in range(4)]
    order += [("g", t) for t in range(8)]
    order += [("y", t) for t in range(UT)] + [("g", t) for t in range(8, 12)] + [("gm", 0)] + [("z", t) for t in range(KT)]
    for h in range(HEADS):
        order += [("ms", h), ("s", h)]
    order += [("h", k) for k in range(2 * HEADS)] + [("g", t) for t in range(12, 16)]
    order += [("oT", t) for t in range(KT)]
    order += [("ym", t) for t in range(KT)] + [("wo", k) for k in range(4)] + [("h1T", t) for t in range(KT)]
    first = plan_from(order, {})
    uses = {}
    for bank, _ in first.values():
        uses[bank] = uses.get(bank, 0) + 1
    order = [("x2T", t) for t in range(KT)] + [("ga", 0), ("gb", 0)] + [("gqkv", t) for t in range(12)]
    order += [("Gc", 0)] + [("mqk", t) for t in range(5)]
    order += [("nq", t) for t in range(4)] + [("mqk", t) for t in range(5, 8)]
    order += [("mv", 0)] + [("vk", t) for t in range(2)]
    for h in range(GH):
        order += [("gb_", h), ("kk", h), ("qk_", h)]
    order += [("mv", 1)]
    for lv in range(LEVELS):
        order += [("X", lv, 0), ("X", lv, 1), ("sc", lv)] + ([("av", lv - 1)] if lv else []) + ([("gz", lv)] if lv < 4 else [])
        order += [("Z", lv, 0), ("ZT", lv, 0), ("Z", lv, 1), ("ZT", lv, 1), ("pT", lv)]
    order += [("sc", MH - 1), ("av", MH - 2), ("pT", MH - 1), ("av", MH - 1)]
    order += [("U1", 0), ("AU", 0), ("U2", 0), ("O", 0), ("O", 1)]
    order += [("wout", k) for k in range(4)] + [("obT", 0), ("obT", 1)] + [("x3T", t) for t in range(KT)]
    order += [None] * ((6 - len(order)) % 8) + [("rt", 0), ("rt", 1), ("cum", 0), ("comb", 0)]
    order += [("sT", b) for b in range(BLOCKS // 2)]
    second = plan_from(order, uses)
    return {**first, **second}


def plan_from(order, uses):
    uses, plan = dict(uses), {}
    for k, name in enumerate(order):
        if name is None:
            continue
        bank = k % 8
        plan[name] = (bank, uses.get(bank, 0))
        uses[bank] = uses.get(bank, 0) + 1
    return plan


BANK = bank_plan()


def build(nc, a):
    ctx = ExitStack()
    with ctx:
        def sb(name, shape, dt=FP32):
            return ctx.enter_context(nc.sbuf_tensor(name, shape, dt))

        class Sems(dict):
            def __missing__(self, name):
                self[name] = ctx.enter_context(nc.semaphore(name))
                return self[name]

        S = Sems()

        ring = sb("weight_ring", [P, SLOTS, 4096])
        tokA = sb("tokA", [P, TT, D])
        tokB = sb("tokB", [P, TT, D])
        with nc.sbuf_tensor("split", [P, 15360], FP32R) as split:
            pass
        hT = sb("hT", [P, KT, LEN])
        uTp = sb("uTp", [P, UT, CHUNK, NCH])
        rawR = sb("raw_region", [P, 8 * (LEN + 3)])
        convR = sb("conv_region", [P, 8 * LEN])
        vR = sb("v_region", [P, 3 * HEADS * (DV + 1)])
        gR = sb("gate_region", [P, 16 * SEQ])
        XR = sb("state_region", [P, 2 * NST * LEN])
        scanR = sb("scan_region", [P, 3 * 2 * NST * NCH + 2 * NST * CHUNK])
        cTt = sb("cTt", [P, 2, UT, P])
        prow = sb("prow", [P, 2, P])
        pcol = sb("pcol", [P, 2, P])
        ident = sb("ident", [P, P])
        tri = sb("tri", [P, P])
        small = sb("small", [P, 640])
        rows = sb("rows", [HEADS, 6, LEN])
        rowone = sb("rowone", [HEADS, 1])
        wif = sb("wif", [P, KT, 8])
        wif2 = sb("wif2", [P, KT, 8])
        wr = sb("wr", [P, KT, NG + NE])
        bif = sb("bif", [HEADS, 2])
        ldt = sb("ldt", [NST, 2])
        p4 = sb("p4", [GH, 2])
        ones = sb("ones", [P, P])
        stri = sb("stri", [P, P])
        negm = sb("negm", [P, P])
        blk = sb("blk", [P, P])
        lvl = sb("lvl", [P, LEVELS, P])
        turns_ = sb("turns", [1, 1], I32)
        fgs = sb("fgs", [P, TT, NG])
        wtok = sb("wtok", [P, TT, EG])
        rig = sb("rig", [P, TT, EG])
        rcum = sb("rcum", [P, TT * EG])
        req = sb("req", [P, TT * EG])
        rkeep = sb("rkeep", [P, TT * (NG + EG)])
        rmul = sb("rmul", [P, TT, NG, EG])

        raw = rawR[:].rearrange("p (t n) -> p t n", t=8)
        conv = convR[:].rearrange("p (t n) -> p t n", t=8)
        vaug = vR[:].rearrange("p (t h n) -> p t h n", t=3, h=HEADS)
        gT = gR[:].rearrange("p (t n) -> p t n", t=16)
        X = XR[:].rearrange("p (c i s n) -> p c i s n", c=2, i=NST, s=CHUNK)
        cell = 2 * NST * NCH
        T1 = scanR[:, 0:cell].rearrange("p (c i n) -> p c i n", c=2, i=NST)
        T2 = scanR[:, cell:2 * cell].rearrange("p (c i n) -> p c i n", c=2, i=NST)
        EN = scanR[:, 2 * cell:3 * cell].rearrange("p (c i n) -> p c i n", c=2, i=NST)
        PW = scanR[:, 3 * cell:].rearrange("p (c s i) -> p c s i", c=2, s=CHUNK)
        meta = vR[0:META, 0:D]
        bTt = gR[:, 0:1024].rearrange("p (c j n) -> p c j n", c=2, j=UT)
        braw = gR[:, 1024:1536].rearrange("p (c i h) -> p c i h", c=2, i=NST)
        bexp = gR[:, 1536:2560].rearrange("p (c i h) -> p c i h", c=2, i=NST)
        craw = gR[:, 2560:3072].rearrange("p (c j n) -> p c j n", c=2, j=UT)
        cexp = gR[:, 3072:4096].rearrange("p (c j n) -> p c j n", c=2, j=UT)
        lrow = tokB[0:NST].rearrange("p t n -> p (t n)").rearrange("p (c n) -> p c n", n=P)
        sel = sb("sel", [HEADS, HEADS, P])
        hm = rawR[:, 0:TT * D].rearrange("p (t n) -> p t n", t=TT)
        omT = convR[:, 0:KT * SEQ].rearrange("p (t n) -> p t n", t=KT)
        gelT = scanR[:, 0:UT * SEQ].rearrange("p (t n) -> p t n", t=UT)
        mixT = XR[:, 0:KT * SEQ].rearrange("p (t n) -> p t n", t=KT)
        zsig = XR[:, 2048:2048 + 512].rearrange("p (b n) -> p b n", b=2)
        pt = XR[:, 4608:5888].rearrange("p (b n) -> p b n", b=2)
        wgt = XR[:, 5888:7168].rearrange("p (b n) -> p b n", b=2)
        bc0 = XR[:, 0:2 * D].rearrange("p (c n) -> p c n", c=2)
        bcvo = convR[:, 0:2 * D].rearrange("p (c n) -> p c n", c=2)
        bcL = XR[:, 4608:4608 + 2 * D].rearrange("p (c n) -> p c n", c=2)
        ffr = XR[:, 2560:2560 + 1024].rearrange("p (b n) -> p b n", b=2)
        ffh = XR[:, 3584:3584 + 1024].rearrange("p (b n) -> p b n", b=2)

        zeros = XR[:, 7168:7680]
        HI, LO = 0, 1
        xs = split[:, 8192:12288].rearrange("p (h k n) -> p h k n", h=2, k=KT)
        ups = split[:, 4096:8192].rearrange("p (i h k n) -> p i h k n", i=2, h=2, k=4)
        dns = split[:, 0:4096].rearrange("p (i h n) -> p i h n", i=2, h=2)
        ffs = split[:, 12288:14336].rearrange("p (q h n) -> p q h n", q=2, h=2)
        gus = split[:, 0:8192].rearrange("p (i h c k n) -> p i h c k n", i=4, h=2, c=2, k=2)
        dns2 = split[:, 8192:12288].rearrange("p (i h n) -> p i h n", i=2, h=2)
        xgs = split[:, 12288:14336].rearrange("p (h k n) -> p h k n", h=2, k=KT)
        hidTs = split[:, 14336:15360].rearrange("p (q h n) -> p q h n", q=2, h=2)

        ps = [ctx.enter_context(nc.psum_tensor(f"bank{b}", [P, 512], FP32)) for b in range(8)]

        def bank(*name):
            return ps[BANK[name][0]]

        def slot(name, i, cols):
            return ring[:, CHUNK_AT[name, i] % SLOTS, :].rearrange("p (k n) -> p k n", n=cols)

        mix2T = mixT
        graw = XR[:, 2048:2048 + 12 * (SEQ + 3)].rearrange("p (t n) -> p t n", t=12)
        gsq = XR[:, 2048:2048 + 12 * SEQ].rearrange("p (t n) -> p t n", t=12)
        gconv = XR[:, 5156:5156 + 12 * SEQ].rearrange("p (t n) -> p t n", t=12)
        mq = rawR[:, 0:8 * SEQ].rearrange("p (t n) -> p t n", t=8)
        mval = vR[:, 0:1024].rearrange("p (t n) -> p t n", t=TT)
        gz = vR[:, 1024:2048].rearrange("p (t n) -> p t n", t=TT)
        vb = vR[:, 2048:3072].rearrange("p (t h n) -> p t h n", t=TT, h=GH)
        aT = gR[:, 0:1536].rearrange("p (h n) -> p h n", h=GH)
        qkT = gR[:, 1536:3072].rearrange("p (h n) -> p h n", h=GH)
        U = gR[:, 3072:4096].rearrange("p (t h n) -> p t h n", t=TT, h=GH)
        Tm = convR[:, 0:1024].rearrange("p (q n) -> p q n", q=8)
        Tt = convR[:, 1024:2048].rearrange("p (q n) -> p q n", q=8)
        Xb = scanR[:, 0:1024].rearrange("p (q n) -> p q n", q=8)
        Zm = scanR[:, 1024:2048].rearrange("p (q n) -> p q n", q=8)
        gsig = gsq
        xg = scanR[:, 1024:2048].rearrange("p (k n) -> p k n", k=KT)
        yg = scanR[:, 0:D]
        ptok = XR[:, 1024:1024 + TT * (BLOCKS + 1) * CAP]\
            .rearrange("p (t b n) -> p t b n", t=TT, b=BLOCKS + 1)
        wslot = XR[:, 3328:3328 + BLOCKS * EG]
        pcur = XR[:, 3392:3392 + SEQ]
        iota = XR[:, 3648:3648 + CAP]
        hid = XR[:, 3776:4288].rearrange("p (b n) -> p b n", b=2)
        pslot = XR[:, 6656:6656 + BLOCKS * SEQ].rearrange("p (b n) -> p b n", b=BLOCKS)
        sg = cTt[:].rearrange("p a b n -> p (a b n)")[:, 0:512].rearrange("p (b n) -> p b n", b=2)
        yu = scanR[:, 1088:1088 + UT * SEQ].rearrange("p (t n) -> p t n", t=UT)
        ymg = XR[:, 4096:4608].rearrange("p (b n) -> p b n", b=2)
        tokBf = tokB[:].rearrange("p t n -> p (t n)")
        pm = tokBf[:, 0:768].rearrange("p (b n) -> p b n", b=2)
        pTs = tokBf[:, 768:1536].rearrange("p (b n) -> p b n", b=2)
        dec = pTs
        ob = cTt[:].rearrange("p a b n -> p (a b n)").rearrange("p (t h n) -> p t h n", t=TT, h=GH)

        used = [0]

        def col(n):
            used[0] += n
            assert used[0] <= small.shape[1], used
            return small[:, used[0] - n:used[0]]

        eps5, eps6 = col(1), col(1)
        odd, even = col(1), col(1)
        parity = col(4)
        stats = col(36)
        mv = col(6)
        std, rstd = col(8), col(8)
        lamcol = col(64)
        gcol, em = col(20), col(8)
        den, rden = col(8), col(8)
        bst, mvh = col(48), col(16)
        ss = col(8)
        nmax, psum_, prec = col(4), col(4), col(4)
        gc = col(16)
        mv3 = mv.rearrange("p (r c) -> p r c", c=2)
        mvh3 = mvh.rearrange("p (r c) -> p r c", c=2)
        warm_out = col(12)
        lg2 = col(TT * (NG + NE)).rearrange("p (m n) -> p m n", m=TT)
        ngmax, gsum, e2, top1, top2, w0 = col(TT), col(TT), col(TT), col(TT), col(TT), col(TT)
        gexp = col(TT * NG).rearrange("p (m n) -> p m n", m=TT)
        f1 = col(TT * EG).rearrange("p (m n) -> p m n", m=TT)
        f2 = col(TT * EG).rearrange("p (m n) -> p m n", m=TT)
        rank = col(4)
        count = col(8)

        NROW1 = 81
        block = ctx.enter_context(nc.Block())

        def full(*name):
            return S[f"bank{BANK[name][0]}_full"], 1

        def filled(*name):
            return S[f"bank{BANK[name][0]}_full"], BANK[name][1] + 1

        def read(*name):
            return S[f"bank{BANK[name][0]}_read"], 1

        def drained(*name):
            return S[f"bank{BANK[name][0]}_read"], BANK[name][1] + 1

        @block.sync
        def _(sp):
            def w_rows(w, k0, nk, c0, nc_):
                return w[k0 * P:(k0 + nk) * P, c0:c0 + nc_].rearrange("(k p) n -> p k n", p=P)

            w_in, w2 = a["w_in"][0], a["w_in_2"][0]

            def dram(name, i):
                if name == "u":
                    return [w_rows(w_in, 0, KT, C_U, 512)]
                if name == "qk":
                    return [w_rows(w_in, 0, KT, C_QK + 512 * i, 512)]
                if name == "v":
                    return [w_rows(w_in, 0, KT, C_V + 512 * i, 512)]
                if name == "o":
                    return [w_rows(w_in, 0, KT, C_O + 512 * i, 512)]
                if name == "g":
                    return [w_rows(w_in, 0, KT, C_G + 512 * i, 512)]
                if name == "glu":
                    return [w_rows(a["s5_w_glu"][0], 0, UT, 512 * i, 512),
                            w_rows(a["s5_w_glu"][0], 0, UT, D + 512 * i, 512)]
                if name == "mout":
                    return [w_rows(a["m_w_out"][0], 0, KT, 512 * i, 512)]
                if name == "wo":
                    return [w_rows(a["w_o"][0], 0, KT, 512 * i, 512)]
                if name == "gqkv":
                    return [w_rows(w2, 0, KT, C2_GQKV + 512 * i, 512)]
                if name == "mqk":
                    return [w_rows(w2, 0, KT, C2_MQ + 512 * i, 512)]
                if name == "gz":
                    return [w_rows(w2, 0, KT, C2_GZ, 512)]
                if name == "mv":
                    return [w_rows(w2, 0, KT, C2_MV, 512)]
                if name == "wout":
                    return [w_rows(a["w_out_2"][0], 0, KT, 512 * i, 512)]

            def chunk_used(at):
                name, i, _ = STREAM[at]
                if name == "ffn":
                    return S["wdn_split"], 2 * (i + 1)
                if name == "u":
                    return filled("u", 3)
                if name in ("qk", "g", "glu", "mout", "gqkv", "mqk"):
                    return filled({"glu": "z", "mout": "ym"}.get(name, name), 4 * i + 3)
                if name == "v":
                    return filled("v", 3 * i + 2)
                if name in ("o", "wo", "wout"):
                    return filled(name, 2 * i + 1)
                return filled(name, 3 if name == "gz" else 1)

            def load(name, i):
                at = CHUNK_AT[name, i]
                if at >= SLOTS:
                    sp.wait_ge(*chunk_used(at - SLOTS))
                srcs = dram(name, i)
                size = 4096 // len(srcs)
                for k, src in enumerate(srcs):
                    dst = ring[:, at % SLOTS, k * size:(k + 1) * size].rearrange("p (k n) -> p k n", n=512)
                    sp.dma_start(dst, src).then_inc(S[f"slot{at % SLOTS}_loaded"], 16)

            def rows_of(t, r0, src, n):
                sp.dma_start(prow[r0:r0 + n, t, :], src).then_inc(S["prow_loaded"], 16)

            def lane(v):
                return v.rearrange("(t p) -> t p", p=P)

            b_in = a["b_in"][0]
            rows_of(0, 0, a["qk_conv_w"][0].rearrange("i (t p) -> (i t) p", p=P), 32)
            rows_of(0, 32, lane(a["qk_conv_b"][0]), 8)
            rows_of(0, 40, lane(b_in[C_U:C_V]), 12)
            rows_of(0, 52, lane(b_in[C_G:C_G + 2 * D]), 16)
            rows_of(0, 68, lane(a["s5_d"][0]), 4)
            rows_of(0, 72, lane(a["b_up"][0]), 32)
            rows_of(0, 104, lane(a["ln0_g"]), 8)
            rows_of(0, 112, lane(a["ln0_b"]), 8)
            rows_of(0, 120, lane(a["m_norm_g"][0]), 8)
            rows_of(1, 0, a["conv_w_2"][0].rearrange("i (t p) -> (i t) p", p=P), 48)
            rows_of(1, 48, lane(a["ln1_g"][0]), 8)
            rows_of(1, 56, lane(a["ln1_b"][0]), 8)
            rows_of(1, 64, lane(a["attn_norm_2"][0]), 8)
            rows_of(1, 72, lane(a["ffn_norm_2"][0]), 8)
            rows_of(1, 80, lane(a["gdn_norm_2"][0]), 1)
            sp.wait_ge(S["x_loaded"], 16 * (TT + 1))
            for name, i, _ in STREAM:
                if name == "ffn":
                    break
                load(name, i)
            base = CHUNK_AT["ffn", 0]
            wup = a["w_up"][0].rearrange("(k p) (j n) -> j p k n", p=P, n=256)
            wdn = a["w_down"][0].rearrange("(j k p) n -> j p k n", p=P, k=2)

            def load_ffn(j, q):
                s = (base + q) % SLOTS
                sp.dma_start(ring[:, s, 0:2048].rearrange("p (k n) -> p k n", n=256),
                             wup[bass.ds(j, 1)].squeeze(0)).then_inc(S[f"slot{s}_loaded"], 16)
                sp.dma_start(ring[:, s, 2048:4096].rearrange("p (k n) -> p k n", n=D),
                             wdn[bass.ds(j, 1)].squeeze(0)).then_inc(S[f"slot{s}_loaded"], 16)

            for q in range(SLOTS):
                sp.wait_ge(*chunk_used(base + q - SLOTS))
                load_ffn(q, q)
            with sp.Fori(1, FF // 256 // SLOTS) as it:
                for q in range(SLOTS):
                    sp.wait_ge(S["wdn_split"], it * (2 * SLOTS) + 2 * (q - SLOTS + 1))
                    load_ffn(it * SLOTS + q, q)
            for name, i, _ in STREAM[CHUNK_AT["gqkv", 0]:CHUNK_AT["gu", 0]]:
                load(name, i)
            base = CHUNK_AT["gu", 0]
            wg = a["w_gate_2"][0].rearrange("g e (k p) n -> (g e) p k n", p=P)
            wu = a["w_up_2"][0].rearrange("g e (k p) n -> (g e) p k n", p=P)

            def load_gate_up(e, q):
                s = (base + 2 * q) % SLOTS
                for c, w in enumerate((wg, wu)):
                    sp.dma_start(ring[:, s, 2048 * c:2048 * c + 2048].rearrange("p (k n) -> p k n", n=EF),
                                 w[bass.ds(e, 1)].squeeze(0)).then_inc(S[f"slot{s}_loaded"], 16)

            for q in range(2):
                sp.wait_ge(*chunk_used(base + 2 * q - SLOTS))
                load_gate_up(q, q)
            for q in range(2):
                sp.wait_ge(S["gu_split"], 4 * (q + 1))
                load_gate_up(2 + q, q)
            sp.wait_ge(S["turns_ready"], 1)
            turns = sp.value_load(turns_[0:1, 0:1], min_val=NG - 1, max_val=BLOCKS - 1)
            with sp.Fori(0, turns * (EG // 2) + (EG // 2 - 2)) as it:
                pair = (it + 2) % (NE // 2)
                for q in range(2):
                    sp.wait_ge(S["gu_split"], it * 8 + 4 * (q + 3))
                    load_gate_up(pair * 2 + q, q)
            for t in range(TT):
                sp.wait_ge(S["out_ready"], t + 1)
                sp.dma_start(a["out"][0, t * P:(t + 1) * P, :], tokB[:, t, :]).then_inc(S["out_written"], 16)
            sp.wait_ge(S["out_written"], 16 * TT)

        @block.tensor
        def _(pe):
            def free(*name):
                b, n = BANK[name]
                if n:
                    pe.wait_ge(S[f"bank{b}_read"], n)
                return ps[b]

            def arrived(name, i):
                at = CHUNK_AT[name, i]
                pe.wait_ge(S[f"slot{at % SLOTS}_loaded"], loaded_count(at))

            def project_T(o, w, c0, xT, nk, n0, n1, before=None):
                for k in range(nk):
                    if before:
                        before(k)
                    last = nc.tensor.matmul(o, w[:, k, c0:c0 + P], xT[:, k, n0:n1], start=(k == 0), stop=(k == nk - 1))
                return last

            def project_tok(o, w, xT, nk, n0, n1, before=None):
                for k in range(nk):
                    if before:
                        before(k)
                    last = nc.tensor.matmul(o, xT[:, k, n0:n1], w[:, k, :], start=(k == 0), stop=(k == nk - 1))
                return last

            pe.wait_ge(S["const_ready"], 1)
            pe.wait_ge(S["prow_loaded"], PROW_DMAS * 16)
            for c, n in ((0, P), (1, NROW1)):
                o = free("prow", c)
                nc.tensor.transpose(o[:, 0:n], prow[0:n, c, :], ident[0:n, 0:n]).then_inc(*full("prow", c))
            pe.wait_ge(S["xn_ready"], 1)
            for t in range(KT):
                o = free("xT", t)
                nc.tensor.transpose(o[:, 0:META], meta[:, t * P:(t + 1) * P], ident[0:META, 0:META])
                for m in range(TT):
                    last = nc.tensor.transpose(o[:, META + m * P:META + (m + 1) * P], tokA[:, m, t * P:(t + 1) * P],
                                               ident[:])
                last.then_inc(*full("xT", t))
            pe.wait_ge(S["poles_ready"], 1)
            o = free("lam", 0)
            for c in range(4):
                last = nc.tensor.transpose(o[:, c * NST:(c + 1) * NST], lrow[:, 12 + c, :], ident[0:NST, 0:NST])
            last.then_inc(*full("lam", 0))
            arrived("u", 0)
            for t in range(UT):
                o = free("u", t)
                project_T(o[:, 0:LEN], slot("u", 0, 512), t * P, hT, KT, 0, LEN,
                          (lambda k: pe.wait_ge(*drained("xT", k))) if t == 0 else None).then_inc(*full("u", t))
            pe.wait_ge(S["bexp_ready"], 1)
            for c in range(2):
                o = free("bT", c)
                for j in range(UT):
                    last = nc.tensor.transpose(o[:, j * P:(j + 1) * P],
                                               bexp[:, c, 4 * j:4 * j + 4, :].rearrange("p i h -> p (i h)"), ident[:])
                last.then_inc(*full("bT", c))
            pe.wait_ge(S["cexp_ready"], 1)
            for c in range(2):
                o = free("cT", c)
                for j in range(UT):
                    last = nc.tensor.transpose(o[:, j * P:(j + 1) * P], cexp[:, c, j, :], ident[:])
                last.then_inc(*full("cT", c))
            pe.wait_ge(*drained("u", UT - 1))
            pe.wait_ge(*drained("bT", 1))
            for i in range(NST):
                j, r = i // 4, 32 * (i % 4)
                for c in range(2):
                    o = free("bu", 2 * i + c)
                    nc.tensor.matmul(o[:, 0:LEN], bTt[r:r + 32, c, j, :],
                                     uTp[r:r + 32, j, :, :].rearrange("p s n -> p (s n)"), start=True, stop=True)\
                        .then_inc(*full("bu", 2 * i + c))
            for t in range(8):
                if t % 4 == 0:
                    arrived("qk", t // 4)
                o = free("qk", t)
                project_T(o[:, 0:LEN], slot("qk", t // 4, 512), (t % 4) * P, hT, KT, 0, LEN).then_inc(*full("qk", t))
            pe.wait_ge(S["small_loaded"], SMALL_DMAS * 16)
            for c, name in enumerate(("i", "f")):
                o = free(name, 0)
                for k in range(KT):
                    last = nc.tensor.matmul(o[0:HEADS, 0:LEN], wif[:, k, 4 * c:4 * c + 4], hT[:, k, :],
                                            start=(k == 0), stop=(k == KT - 1))
                last.then_inc(*full(name, 0))
            spans = [(0, META), (META, META + P), (META + P, LEN)]
            for k in range(6):
                if k % 3 == 0:
                    arrived("v", k // 3)
                n0, n1 = spans[k % 3]
                o = free("v", k)
                project_tok(o[0:n1 - n0, :], slot("v", k // 3, 512), hT, KT, n0, n1).then_inc(*full("v", k))
            for k in range(4):
                if k % 2 == 0:
                    arrived("o", k // 2)
                n0, n1 = spans[1 + k % 2]
                o = free("o", k)
                project_tok(o[:, :], slot("o", k // 2, 512), hT, KT, n0, n1).then_inc(*full("o", k))
            def gates(t0, t1):
                for t in range(t0, t1):
                    if t % 4 == 0:
                        arrived("g", t // 4)
                    o = free("g", t)
                    project_T(o[:, 0:SEQ], slot("g", t // 4, 512), (t % 4) * P, hT, KT, META, LEN)\
                        .then_inc(*full("g", t))

            gates(0, 8)
            pe.wait_ge(S["scan_ready"], 1)
            pe.wait_ge(*drained("cT", 1))
            for j in range(UT):
                o = free("y", j)
                for r in range(4):
                    for c in range(2):
                        last = nc.tensor.matmul(o[32 * r:32 * r + 32, 0:SEQ], cTt[:, c, j, 32 * r:32 * r + 32],
                                                X[:, c, 4 * j + r, :, 1:NCH], start=(c == 0), stop=(c == 1))
                last.then_inc(*full("y", j))
            gates(8, 12)
            pe.wait_ge(S["gate_rows_ready"], 1)
            o = free("gm", 0)
            nc.tensor.transpose(o[0:META, 0:4], rows[:, 0, 0:META], ident[0:HEADS, 0:HEADS])
            for m in range(TT):
                lo, hi = spans[1 + m]
                nc.tensor.transpose(o[:, 4 + 4 * m:8 + 4 * m], rows[:, 0, lo:hi], ident[0:HEADS, 0:HEADS])
                last = nc.tensor.transpose(o[:, 12 + 4 * m:16 + 4 * m], rows[:, 5, lo:hi], ident[0:HEADS, 0:HEADS])
            last.then_inc(*full("gm", 0))
            pe.wait_ge(S["gelu_ready"], UT)
            for t in range(KT):
                if t % 4 == 0:
                    arrived("glu", t // 4)
                w = slot("glu", t // 4, 512)
                o = free("z", t)
                project_T(o[:, 0:SEQ], w[:, 0:UT, :], (t % 4) * P, gelT, UT, 0, SEQ)
                project_T(o[:, SEQ:2 * SEQ], w[:, UT:2 * UT, :], (t % 4) * P, gelT, UT, 0, SEQ)\
                    .then_inc(*full("z", t))
            pe.wait_ge(S["qk_ready"], 2)
            for h in range(HEADS):
                q, kk = conv[:, h, META:LEN], conv[:, 4 + h, :]
                o = free("ms", h)
                nc.tensor.matmul(o[:, 0:SEQ], sel[:, h, :], rows[:, 4, META:LEN], start=True, stop=True)
                nc.tensor.matmul(o[0:META, SEQ:2 * SEQ], kk[:, 0:META], q, start=True, stop=True)\
                    .then_inc(*full("ms", h))
                o = free("s", h)
                nc.tensor.matmul(o[:, 0:SEQ], kk[:, META:META + P], q, start=True, stop=True)
                nc.tensor.matmul(o[:, SEQ:SEQ + P], kk[:, META + P:LEN], q[:, P:SEQ], start=True, stop=True)\
                    .then_inc(*full("s", h))
            pe.wait_ge(S["v_biased"], 6)
            for k in range(2 * HEADS):
                h, m = k // 2, k % 2
                b = h % 2
                if m == 0:
                    pe.wait_ge(S["pt_ready"], h + 1)
                o = free("h", k)
                nc.tensor.matmul(o[:, 0:DV + 1], pt[0:META, b, m * P:(m + 1) * P], vaug[0:META, 0, h, :],
                                 start=True, stop=False)
                last = nc.tensor.matmul(o[:, 0:DV + 1], pt[:, b, SEQ + m * P:SEQ + (m + 1) * P], vaug[:, 1, h, :],
                                        start=False, stop=(m == 0))
                if m == 1:
                    last = nc.tensor.matmul(o[:, 0:DV + 1], pt[:, b, 2 * SEQ:2 * SEQ + P], vaug[:, 2, h, :],
                                            start=False, stop=True)
                last.then_inc(*full("h", k))
            gates(12, 16)
            pe.wait_ge(S["gated_ready"], 1)
            for t in range(KT):
                o = free("oT", t)
                for m in range(TT):
                    last = nc.tensor.transpose(o[:, m * P:(m + 1) * P], hm[:, m, t * P:(t + 1) * P], ident[:])
                last.then_inc(*full("oT", t))
            pe.wait_ge(*drained("oT", KT - 1))
            for t in range(KT):
                if t % 4 == 0:
                    arrived("mout", t // 4)
                o = free("ym", t)
                project_T(o[:, 0:SEQ], slot("mout", t // 4, 512), (t % 4) * P, omT, KT, 0, SEQ)\
                    .then_inc(*full("ym", t))
            for k in range(4):
                if k % 2 == 0:
                    arrived("wo", k // 2)
                o = free("wo", k)
                project_tok(o[:, :], slot("wo", k // 2, 512), mixT, KT, (k % 2) * P, (k % 2 + 1) * P,
                            (lambda t: pe.wait_ge(S["mix_ready"], t + 1)) if k == 0 else None)\
                    .then_inc(*full("wo", k))

            def transposed(name, ready):
                pe.wait_ge(S["xn_ready"], ready)
                for t in range(KT):
                    o = free(name, t)
                    for m in range(TT):
                        last = nc.tensor.transpose(o[:, m * P:(m + 1) * P], tokB[:, m, t * P:(t + 1) * P], ident[:])
                    last.then_inc(*full(name, t))

            transposed("h1T", 2)
            pe.wait_ge(*drained("h1T", KT - 1))
            pe.wait_ge(S["zeros_ready"], 1)
            for b in range(4, 8):
                nc.tensor.matmul(ps[b][:], ident[:], zeros, start=True, stop=False)

            def three(o, l, r, start, stop):
                nc.tensor.matmul(o, l(HI), r(HI), start=start, stop=False)
                nc.tensor.matmul(o, l(HI), r(LO), start=False, stop=False)
                return nc.tensor.matmul(o, l(LO), r(HI), start=False, stop=stop)

            def ffn_up(it, q, before=None):
                for m in range(2):
                    for k in range(KT):
                        if m == 0 and k % 4 == 0:
                            pe.wait_ge(S["wup_split"], it * (2 * SLOTS) + (2 * q + k // 4 + 1))
                        if before and m == 0:
                            before(k)
                        last = three(ps[2 * (q % 2) + m][:, 0:SEQ],
                                     lambda h: ups[:, k // 4, h, k % 4, m * P:(m + 1) * P],
                                     lambda h: xs[:, h, k, :], k == 0, k == KT - 1)
                    last.then_inc(S["ffn_up"], 1)

            def ffn_down(it, q, is_last):
                pe.wait_ge(S["ffh_split"], it * SLOTS + (q + 1))
                if is_last:
                    pe.wait_ge(S["wdn_split"], it * (2 * SLOTS) + (2 * q + 2))
                    for m in range(TT):
                        for n in range(2):
                            for k in range(2):
                                last = three(ps[4 + 2 * m + n][:, :],
                                             lambda h: ffs[:, q % 2, h, k * SEQ + m * P:k * SEQ + (m + 1) * P],
                                             lambda h: dns[:, k, h, 512 * n:512 * n + 512], False, k == 1)
                        last.then_inc(S["ffn_sums"], 1)
                    return
                for k in range(2):
                    pe.wait_ge(S["wdn_split"], it * (2 * SLOTS) + (2 * q + k + 1))
                    for m in range(TT):
                        for n in range(2):
                            last = three(ps[4 + 2 * m + n][:, :],
                                         lambda h: ffs[:, q % 2, h, k * SEQ + m * P:k * SEQ + (m + 1) * P],
                                         lambda h: dns[:, k, h, 512 * n:512 * n + 512], False, False)
                last.then_inc(S["ffn_down"], 1)

            turns = FF // 256 // SLOTS
            ffn_up(0, 0, lambda k: pe.wait_ge(S["x_split"], k + 1))
            pe.sem_inc(S["ffn_down"], 1)
            with pe.Fori(0, turns - 1) as it:
                for q in range(SLOTS):
                    ffn_up(it, q + 1)
                    ffn_down(it, q, False)
            for q in range(SLOTS):
                if q < SLOTS - 1:
                    ffn_up(turns - 1, q + 1)
                ffn_down(turns - 1, q, q == SLOTS - 1)

            transposed("x2T", 3)
            for c, name in enumerate(("ga", "gb")):
                o = free(name, 0)
                for k in range(KT):
                    if c == 0:
                        pe.wait_ge(*drained("x2T", k))
                    last = nc.tensor.matmul(o[0:GH, 0:SEQ], wif2[:, k, 4 * c:4 * c + 4], hT[:, k, 0:SEQ],
                                            start=(k == 0), stop=(k == KT - 1))
                last.then_inc(*full(name, 0))
            for t in range(12):
                if t % 4 == 0:
                    arrived("gqkv", t // 4)
                o = free("gqkv", t)
                project_T(o[:, 0:SEQ], slot("gqkv", t // 4, 512), (t % 4) * P, hT, KT, 0, SEQ)\
                    .then_inc(*full("gqkv", t))
            pe.wait_ge(S["decay_rows_ready"], 1)
            o = free("Gc", 0)
            for m in range(TT):
                nc.tensor.transpose(o[:, 4 * m:4 * m + 4], rows[:, 3, m * P:(m + 1) * P], ident[0:GH, 0:GH])
                last = nc.tensor.transpose(o[:, 8 + 4 * m:12 + 4 * m], rows[:, 4, m * P:(m + 1) * P], ident[0:GH, 0:GH])
            last.then_inc(*full("Gc", 0))

            def attention_qk(t0, t1):
                for t in range(t0, t1):
                    if t % 4 == 0:
                        arrived("mqk", t // 4)
                    o = free("mqk", t)
                    project_T(o[:, 0:SEQ], slot("mqk", t // 4, 512), (t % 4) * P, hT, KT, 0, SEQ)\
                        .then_inc(*full("mqk", t))

            attention_qk(0, 5)
            for t in range(4):
                pe.wait_ge(S["gsq_ready"], t + 1)
                o = free("nq", t)
                nc.tensor.matmul(o[:, :], ones[:], gsq[:, 2 * t:2 * t + 2, :].rearrange("p t n -> p (t n)"),
                                 start=True, stop=True).then_inc(*full("nq", t))
            attention_qk(5, 8)
            arrived("mv", 0)

            def attention_values(m):
                o = free("mv", m)
                project_tok(o[:, :], slot("mv", 0, 512), hT, KT, m * P, (m + 1) * P).then_inc(*full("mv", m))

            attention_values(0)
            pe.wait_ge(S["gconv_ready"], 3)
            for m in range(TT):
                o = free("vk", m)
                for h in range(GH):
                    last = nc.tensor.transpose(o[:, h * P:(h + 1) * P], gconv[:, 8 + h, m * P:(m + 1) * P], ident[:])
                last.then_inc(*full("vk", m))
            pe.wait_ge(S["gnorm_ready"], 4)
            for h in range(GH):
                q, kk = gconv[:, h, :], gconv[:, 4 + h, :]
                o = free("gb_", h)
                nc.tensor.matmul(o[:, 0:SEQ], sel[:, h, :], rows[:, 3, 0:SEQ], start=True, stop=True)
                nc.tensor.matmul(o[:, SEQ:2 * SEQ], sel[:, h, :], rows[:, 4, 0:SEQ], start=True, stop=True)\
                    .then_inc(*full("gb_", h))
                for name, r in (("kk", kk), ("qk_", q)):
                    o = free(name, h)
                    nc.tensor.matmul(o[:, 0:SEQ], kk[:, 0:P], r, start=True, stop=True)
                    nc.tensor.matmul(o[:, SEQ:SEQ + P], kk[:, P:SEQ], r[:, P:SEQ], start=True, stop=True)\
                        .then_inc(*full(name, h))

            attention_values(1)

            def scores(h):
                b = MD * (h % 2)
                qh, kh = mq[b:b + MD, h // 2, :], mq[b:b + MD, 4 + h // 2, :]
                o = free("sc", h)
                nc.tensor.matmul(o[:, 0:P], qh[:, 0:P], kh[:, 0:P], start=True, stop=True)
                nc.tensor.matmul(o[:, P:P + SEQ], qh[:, P:SEQ], kh, start=True, stop=True).then_inc(*full("sc", h))

            def probs_T(h):
                pe.wait_ge(S["probs_ready"], h + 1)
                o = free("pT", h)
                for c in range(3):
                    last = nc.tensor.transpose(o[:, c * P:(c + 1) * P], pm[:, h % 2, c * P:(c + 1) * P], ident[:])
                last.then_inc(*full("pT", h))

            def attend(h):
                b = MD * (h % 2)
                pe.wait_ge(*drained("pT", h))
                o = free("av", h)
                w = pTs[:, h % 2, :]
                nc.tensor.matmul(o[b:b + MD, 0:SEQ], mval[:, 0, h * MD:(h + 1) * MD], w[:, 0:SEQ], start=True, stop=False)
                nc.tensor.matmul(o[b:b + MD, P:SEQ], mval[:, 1, h * MD:(h + 1) * MD], w[:, SEQ:SEQ + P],
                                 start=False, stop=True).then_inc(*full("av", h))

            def diag(h, m):
                return aT[:, h, 0:P] if m == 0 else aT[:, h, SEQ:SEQ + P]

            pe.wait_ge(S["aT_ready"], GH)
            pe.wait_ge(*drained("mv", 1))
            def output_gate(o, r, k0, k1):
                for k in range(k0, k1):
                    last = nc.tensor.matmul(o[:, 0:256], hT[:, k, (r // 2) * P:(r // 2 + 1) * P],
                                            slot("gz", 0, 512)[:, k, 256 * (r % 2):256 * (r % 2) + 256],
                                            start=(k == 0), stop=(k == KT - 1))
                return last

            arrived("gz", 0)
            for lv in range(LEVELS):
                for half in range(2):
                    if lv:
                        pe.wait_ge(S["T_ready"], 2 * lv - 1 + half)
                    else:
                        pe.wait_ge(S["T_init"], 1)
                    o = free("X", lv, half)
                    for q in range(4):
                        h, m = 2 * half + q // 2, q % 2
                        last = nc.tensor.matmul(o[:, q * P:(q + 1) * P], diag(h, m), Tm[:, 4 * half + q, :],
                                                start=True, stop=True)
                    last.then_inc(*full("X", lv, half))
                scores(lv)
                if lv:
                    attend(lv - 1)
                if lv < 4:
                    o = free("gz", lv)
                    output_gate(o, lv, 0, 4)
                for half in range(2):
                    pe.wait_ge(*drained("X", lv, half))
                    o = free("Z", lv, half)
                    for q in range(4):
                        g = 4 * half + q
                        last = nc.tensor.matmul(o[:, q * P:(q + 1) * P], Tt[:, g, :], Xb[:, g, :], start=True, stop=True)
                    last.then_inc(*full("Z", lv, half))
                    o = free("ZT", lv, half)
                    for q in range(4):
                        g = 4 * half + q
                        last = nc.tensor.matmul(o[:, q * P:(q + 1) * P], Xb[:, g, :], Tt[:, g, :], start=True, stop=True)
                    last.then_inc(*full("ZT", lv, half))
                if lv < 4:
                    output_gate(bank("gz", lv), lv, 4, KT).then_inc(*full("gz", lv))
                probs_T(lv)
            scores(MH - 1)
            attend(MH - 2)
            probs_T(MH - 1)
            attend(MH - 1)
            pe.wait_ge(S["T_ready"], 2 * LEVELS)
            pe.wait_ge(*drained("vk", 1))
            o = free("U1", 0)
            for h in range(GH):
                last = nc.tensor.matmul(o[:, h * P:(h + 1) * P], Tt[:, 2 * h, :], vb[:, 0, h, :], start=True, stop=True)
            last.then_inc(*full("U1", 0))
            pe.wait_ge(*drained("U1", 0))
            o = free("AU", 0)
            for h in range(GH):
                last = nc.tensor.matmul(o[:, h * P:(h + 1) * P], aT[:, h, P:SEQ], U[:, 0, h, :], start=True, stop=True)
            last.then_inc(*full("AU", 0))
            pe.wait_ge(*drained("AU", 0))
            o = free("U2", 0)
            for h in range(GH):
                last = nc.tensor.matmul(o[:, h * P:(h + 1) * P], Tt[:, 2 * h + 1, :], vb[:, 1, h, :], start=True, stop=True)
            last.then_inc(*full("U2", 0))
            o = free("O", 0)
            for h in range(GH):
                last = nc.tensor.matmul(o[:, h * P:(h + 1) * P], qkT[:, h, 0:P], U[:, 0, h, :], start=True, stop=True)
            last.then_inc(*full("O", 0))
            pe.wait_ge(*drained("U2", 0))
            o = free("O", 1)
            for h in range(GH):
                nc.tensor.matmul(o[:, h * P:(h + 1) * P], qkT[:, h, P:SEQ], U[:, 0, h, :], start=True, stop=False)
                last = nc.tensor.matmul(o[:, h * P:(h + 1) * P], qkT[:, h, SEQ:SEQ + P], U[:, 1, h, :],
                                        start=False, stop=True)
            last.then_inc(*full("O", 1))
            def mixer_out(k, first):
                for t in range(KT // 2):
                    t += 0 if first else KT // 2
                    last = nc.tensor.matmul(bank("wout", k)[:], mix2T[:, t, (k % 2) * P:(k % 2 + 1) * P],
                                            slot("wout", k // 2, 512)[:, t, :], start=(t == 0), stop=(t == KT - 1))
                return last

            pe.wait_ge(*drained("av", MH - 1))
            for k in range(4):
                if k % 2 == 0:
                    arrived("wout", k // 2)
                free("wout", k)
                mixer_out(k, True)
            pe.wait_ge(S["ob_ready"], 1)
            for b in range(2):
                o = free("obT", b)
                for q in range(4):
                    h, m = 2 * b + q // 2, q % 2
                    last = nc.tensor.transpose(o[:, q * P:(q + 1) * P], ob[:, m, h, :], ident[:])
                last.then_inc(*full("obT", b))
            pe.wait_ge(*drained("obT", 1))
            for k in range(4):
                mixer_out(k, False).then_inc(*full("wout", k))
            transposed("x3T", 4)
            for m in range(TT):
                o = free("rt", m)
                project_tok(o[:, 0:NG + NE], wr, hT, KT, m * P, (m + 1) * P,
                            (lambda k: pe.wait_ge(*drained("x3T", k))) if m == 0 else None).then_inc(*full("rt", m))
            pe.wait_ge(S["group_ready"], 1)
            o = free("cum", 0)
            nc.tensor.matmul(o[:, 0:NG], tri[:], fgs[:, 0, :], start=True, stop=True)
            nc.tensor.matmul(o[:, NG:2 * NG], tri[:], fgs[:, 1, :], start=True, stop=False)
            nc.tensor.matmul(o[:, NG:2 * NG], ones[:], fgs[:, 0, :], start=False, stop=True)
            nc.tensor.matmul(o[:, 2 * NG:3 * NG], ones[:], fgs[:, 0, :], start=True, stop=False)
            nc.tensor.matmul(o[:, 2 * NG:3 * NG], ones[:], fgs[:, 1, :], start=False, stop=True)\
                .then_inc(*full("cum", 0))
            def gather(b):
                for k in range(KT):
                    for m in range(TT):
                        last = nc.tensor.matmul(ps[6 + k // 4][:, (k % 4) * CAP:(k % 4 + 1) * CAP],
                                                tokB[:, m, k * P:(k + 1) * P], ptok[:, m, b, :],
                                                start=(m == 0), stop=(m == TT - 1))
                last.then_inc(S["gathered"], 1)

            pe.wait_ge(S["first_slots_ready"], TT)
            gather(0)
            pe.wait_ge(S["ptok_ready"], 1)
            o = free("comb", 0)
            for b in range(BLOCKS):
                for m in range(TT):
                    last = nc.tensor.matmul(o[:, b * EG:(b + 1) * EG], ptok[:, m, b, :], wtok[:, m, :],
                                            start=(m == 0), stop=(m == TT - 1))
            last.then_inc(*full("comb", 0))
            for c in range(BLOCKS // 2):
                o = free("sT", c)
                for q in range(4):
                    last = nc.tensor.transpose(o[:, q * P:(q + 1) * P], ptok[:, q % 2, 2 * c + q // 2, :], ident[:])
                last.then_inc(*full("sT", c))
            pe.wait_ge(*drained("sT", BLOCKS // 2 - 1))
            pe.wait_ge(*drained("comb", 0))

            def gate_up(it, e):
                for k in range(KT):
                    if k % 2 == 0:
                        pe.wait_ge(S["gu_split"], it * (4 * EG) + (4 * e + k // 2 + 1))
                    last = three(ps[e % 2][:], lambda h: xgs[:, h, k, :],
                                 lambda h: gus[:, k // 2, h, :, k % 2, :], k == 0, k == KT - 1)
                    if k % 2 == 1:
                        last.then_inc(S["gu_used"], 1)

            def hidden_T(it, e):
                pe.wait_ge(S["hidden_ready"], it * EG + (e + 1))
                for k in range(2):
                    last = nc.tensor.transpose(ps[2 + e % 2][:, k * CAP:(k + 1) * CAP], hid[:, e % 2, k * P:(k + 1) * P],
                                               ident[:])
                last.then_inc(S["hidT_full"], 1)

            def down(it, e):
                if e == 0:
                    pe.wait_ge(S["yg_ready"], it + 1)
                pe.wait_ge(S["hidT_split"], it * EG + (e + 1))
                for k in range(2):
                    pe.wait_ge(S["dn_split"], it * (2 * EG) + (2 * e + k + 1))
                    for n in range(2):
                        last = three(ps[4 + n][:], lambda h: hidTs[:, e % 2, h, k * CAP:(k + 1) * CAP],
                                     lambda h: dns2[:, k, h, 512 * n:512 * n + 512],
                                     e == 0 and k == 0, e == EG - 1 and k == 1)
                    last.then_inc(S["dn_used"], 1)

            def put_back(m):
                for n in range(2):
                    last = nc.tensor.matmul(ps[6 + n][:], pcur[:, m * P:(m + 1) * P], yg[:, 512 * n:512 * n + 512],
                                            start=True, stop=True)
                last.then_inc(S["put_back"], 1)

            pe.wait_ge(S["turns_ready"], 1)
            turns = pe.value_load(turns_[0:1, 0:1], min_val=NG - 1, max_val=BLOCKS - 1)

            def block_of_tokens(it, is_last):
                pe.wait_ge(S["xg_split"], it + 1)
                for e in range(EG):
                    gate_up(it, e)
                    if e >= 1:
                        hidden_T(it, e - 1)
                    if e >= 2:
                        down(it, e - 2)
                    if e == 1:
                        pe.wait_ge(S["yg_ready"], it + 1)
                        pe.wait_ge(S["pcur_ready"], it + 1)
                        put_back(0)
                    if e == 3:
                        pe.wait_ge(S["added_back"], it * 2 + 2)
                        put_back(1)
                if not is_last:
                    pe.wait_ge(S["added_back"], it * 2 + 3)
                    gather(it + 1)
                hidden_T(it, EG - 1)
                down(it, EG - 2)
                down(it, EG - 1)

            with pe.Fori(0, turns) as it:
                block_of_tokens(it, False)
            block_of_tokens(turns, True)
            pe.wait_ge(S["yg_ready"], turns + 2)
            pe.wait_ge(S["pcur_ready"], turns + 2)
            pe.wait_ge(S["added_back"], turns * 2 + 3)
            put_back(0)
            pe.wait_ge(S["added_back"], turns * 2 + 4)
            put_back(1)

        @block.scalar
        def _(act):
            n_act = [0]

            def link(ins):
                n_act[0] += 1
                ins.then_inc(S["act_chain"], 1)
                act.wait_ge(S["act_chain"], n_act[0])

            A = nc.scalar.activation

            warmed = [0]

            def warm(func):
                warmed[0] += 1
                A(warm_out[:, warmed[0] - 1:warmed[0]], eps6, func)

            def root(out, in_, eps, scale, k):
                if k > 1:
                    warm(ACT.Sqrt)
                act.wait_ge(S["var_ready"], k)
                A(out, in_, ACT.Sqrt, bias=eps, scale=scale).then_inc(S["std_ready"], 1)

            for t in range(TT):
                act.dma_start(tokA[:, t, :], a["x"][0, t * P:(t + 1) * P, :]).then_inc(S["x_loaded"], 16)
            act.dma_start(meta, a["meta_tokens"]).then_inc(S["x_loaded"], 16)
            for c, name in ((0, "s5_lambda_re"), (1, "s5_lambda_im")):
                act.dma_start(lrow[:, c, :], a[name][0].rearrange("(i two) p -> i (two p)", two=2))\
                    .then_inc(S["poles_loaded"], 16)
            act.dma_start(ldt[:], a["s5_log_dt"][0].rearrange("(i two) -> i two", two=2)).then_inc(S["poles_loaded"], 16)
            for c, (bn, cn) in enumerate((("s5_b_re", "s5_c_re"), ("s5_b_im", "s5_c_im"))):
                act.dma_start(braw[:, c, :, :], a[bn][0].rearrange("(i two) p h -> (two p) i h", two=2))\
                    .then_inc(S["bc_loaded"], 16)
                act.dma_start(craw[:, c, :, :], a[cn][0].rearrange("(j g) h n -> (g h) j n", g=8))\
                    .then_inc(S["bc_loaded"], 16)
            act.wait_ge(S["poles_loaded"], 48)
            A(ldt[:], ldt[:], ACT.Exp).then_inc(S["dt_ready"], 1)
            act.wait_ge(S["eps_ready"], 2)
            root(std[:, 0:3], mv3[:, :, 1], eps5, 1.0, 1)
            act.wait_ge(S["zr_ready"], 1)
            A(lrow[:, 7, :], lrow[:, 3, :], ACT.Exp).then_inc(S["er_ready"], 1)
            act.wait_ge(S["angle_ready"], 1)
            A(lrow[:, 8, :], lrow[:, 6, :], ACT.Sin).then_inc(S["sin_ready"], 1)
            A(lrow[:, 9, :], lrow[:, 6, :], ACT.Sin, scale=0.5).then_inc(S["sin_ready"], 1)
            act.wait_ge(*drained("prow", 1))
            for t in range(KT):
                act.wait_ge(*filled("xT", t))
                A(hT[:, t, :], bank("xT", t)[:, 0:LEN], ACT.Identity, bias=pcol[:, 0, 112 + t:113 + t],
                  scale=pcol[:, 0, 104 + t:105 + t]).then_inc(*read("xT", t))
            for t in range(UT):
                act.wait_ge(*filled("u", t))
                A(uTp[:, t, :, :].rearrange("p s n -> p n s"),
                  bank("u", t)[:, 0:LEN].rearrange("p (n s) -> p n s", s=CHUNK), ACT.Identity,
                  bias=pcol[:, 0, 40 + t:41 + t]).then_inc(*read("u", t))
            for c in range(2):
                act.wait_ge(*filled("bT", c))
                A(bTt[:, c, :, :].rearrange("p j n -> p (j n)"), bank("bT", c)[:], ACT.Copy).then_inc(*read("bT", c))
            for c in range(2):
                act.wait_ge(*filled("cT", c))
                A(cTt[:, c, :, :].rearrange("p j n -> p (j n)"), bank("cT", c)[:], ACT.Copy).then_inc(*read("cT", c))
            act.wait_ge(S["h0_ready"], 1)
            for k in range(2 * NST):
                act.wait_ge(*filled("bu", k))
                A(X[:, k % 2, k // 2, :, :].rearrange("p s n -> p (s n)"), bank("bu", k)[:, 0:LEN], ACT.Copy)\
                    .then_inc(*read("bu", k))
            act.wait_ge(S["pads_ready"], 1)
            for t in range(8):
                act.wait_ge(*filled("qk", t))
                A(raw[:, t, 3:3 + LEN], bank("qk", t)[:, 0:LEN], ACT.Identity, bias=pcol[:, 0, 44 + t:45 + t])\
                    .then_inc(*read("qk", t))
            act.wait_ge(S["small_loaded"], SMALL_DMAS * 16)
            for c, name in enumerate(("i", "f")):
                act.wait_ge(*filled(name, 0))
                A(rows[:, c, :], bank(name, 0)[0:HEADS, 0:LEN], ACT.Identity, bias=bif[:, c:c + 1])\
                    .then_inc(*read(name, 0))
            act.wait_ge(*drained("f", 0))
            link(A(rows[:, 2, :], rows[:, 1, :], ACT.Abs))
            link(A(rows[:, 2, :], rows[:, 2, :], ACT.Exp, scale=-1.0))
            A(rows[:, 2, :], rows[:, 2, :], ACT.Ln, bias=1.0).then_inc(S["softplus_ready"], 1)
            act.wait_ge(S["ones_column_ready"], 1)
            for k in range(6):
                n = META if k % 3 == 0 else P
                act.wait_ge(*filled("v", k))
                A(vaug[0:n, k % 3, 2 * (k // 3):2 * (k // 3) + 2, 0:DV],
                  bank("v", k)[0:n, :].rearrange("p (h n) -> p h n", h=2), ACT.Copy).then_inc(*read("v", k))
            for k in range(4):
                act.wait_ge(*filled("o", k))
                A(tokB[:, k % 2, 512 * (k // 2):512 * (k // 2) + 512], bank("o", k)[:], ACT.Copy)\
                    .then_inc(*read("o", k))
            def gates(t0, t1):
                for t in range(t0, t1):
                    act.wait_ge(*filled("g", t))
                    A(gT[:, t, :], bank("g", t)[:, 0:SEQ], ACT.Sigmoid, bias=pcol[:, 0, 52 + t:53 + t])\
                        .then_inc(*read("g", t))

            gates(0, 4)
            act.wait_ge(S["o_biased"], 4)
            A(tokB[:], tokB[:], ACT.Sigmoid).then_inc(S["osig_ready"], 1)
            act.wait_ge(S["conv_ready"], 1)
            sig = rawR[:, 0:8 * LEN]
            A(sig, convR[:], ACT.Sigmoid).then_inc(S["silu_ready"], 1)
            gates(4, 8)
            for t in range(UT):
                act.wait_ge(*drained("y", t))
                A(gelT[:, t, :].rearrange("p (n s) -> p s n", s=CHUNK),
                  yu[:, t, :].rearrange("p (s n) -> p s n", s=CHUNK), ACT.Gelu_apprx_tanh).then_inc(S["gelu_ready"], 1)
            gates(8, 12)
            act.wait_ge(*filled("gm", 0))
            A(em, bank("gm", 0)[:, 12:20], ACT.Exp, scale=-1.0).then_inc(S["em_ready"], 1)
            for t in range(KT):
                act.wait_ge(*filled("z", t))
                if t >= 2:
                    act.wait_ge(*drained("z", t - 2))
                A(zsig[:, t % 2, :], bank("z", t)[:, SEQ:2 * SEQ], ACT.Sigmoid).then_inc(S["zsig_ready"], 1)
            for h in range(HEADS):
                act.wait_ge(S["wlog_ready"], h + 1)
                A(wgt[0:META, h % 2, 0:SEQ], wgt[0:META, h % 2, 0:SEQ], ACT.Exp, scale=-1.0)
                A(wgt[:, h % 2, SEQ:640], wgt[:, h % 2, SEQ:640], ACT.Exp, scale=-1.0).then_inc(S["w_ready"], 1)
            root(std, mvh3[:, :, 1], eps5, 1.0, 2)
            gates(12, 16)
            for t in range(KT):
                act.wait_ge(*filled("oT", t))
                A(omT[:, t, :], bank("oT", t)[:, 0:SEQ], ACT.Copy, scale=pcol[:, 0, 120 + t:121 + t])\
                    .then_inc(*read("oT", t))
            base = CHUNK_AT["ffn", 0]
            first = [loaded_count(base + q) for q in range(SLOTS)]

            def up_hi(it, q):
                s = (base + q) % SLOTS
                act.wait_ge(S[f"slot{s}_loaded"], it * 32 + (first[q % SLOTS] + 32 * (q // SLOTS)))
                for i in range(2):
                    A(ups[:, i, HI, :, :].rearrange("p k n -> p (k n)"), ring[:, s, 1024 * i:1024 * (i + 1)], ACT.Copy)\
                        .then_inc(S["wup_hi"], 1)

            act.wait_ge(S["mix_ready"], KT)
            up_hi(0, 0)
            root(std[:, 0:2], mv3[:, 0:2, 1], eps5, 1.0, 3)
            for t in range(KT):
                act.wait_ge(*filled("h1T", t))
                A(hT[:, t, 0:SEQ], bank("h1T", t)[:, 0:SEQ], ACT.Identity, bias=pcol[:, 1, 56 + t:57 + t],
                  scale=pcol[:, 1, 48 + t:49 + t]).then_inc(*read("h1T", t))
                act.wait_ge(*drained("h1T", t))
                A(xs[:, HI, t, :], hT[:, t, 0:SEQ], ACT.Copy).then_inc(S["x_hi"], 1)

            def relu_and_hi(it, q, more):
                for m in range(2):
                    act.wait_ge(S["ffn_up"], it * (2 * SLOTS) + (2 * q + m + 1))
                    A(ffr[:, q % 2, m * SEQ:(m + 1) * SEQ], ps[2 * (q % 2) + m][:, 0:SEQ], ACT.Relu,
                      bias=pcol[:, 0, bass.ds(it * (2 * SLOTS) + (72 + 2 * q + m), 1)]).then_inc(S["relu_ready"], 1)
                if more:
                    up_hi(it, q + 1)
                act.wait_ge(S["ffh_ready"], it * SLOTS + (q + 1))
                A(ffs[:, q % 2, HI, :], ffh[:, q % 2, :], ACT.Copy).then_inc(S["ffh_hi"], 1)
                act.wait_ge(S["ffn_down"], it * SLOTS + (q + 1))
                for i in range(2):
                    A(dns[:, i, HI, :], ring[:, (base + q) % SLOTS, 2048 + i * D:2048 + (i + 1) * D], ACT.Copy)\
                        .then_inc(S["wdn_hi"], 1)

            turns = FF // 256 // SLOTS
            with act.Fori(0, turns - 1) as it:
                for q in range(SLOTS):
                    relu_and_hi(it, q, True)
            for q in range(SLOTS):
                relu_and_hi(turns - 1, q, q < SLOTS - 1)

            root(std[:, 0:2], mv3[:, 0:2, 1], eps5, 1.0, 4)

            def mean_square(k):
                warm(ACT.Sqrt)
                if k > 1:
                    act.wait_ge(S["res_ready"], k)
                for m in range(TT):
                    if k == 1:
                        act.wait_ge(S["row_tile_ready"], m + 1)
                    A(tokB[:, m, :], tokA[:, m, :], ACT.Square, accum_out=ss[:, m:m + 1]).then_inc(S["act_sq"], 1)
                act.wait_ge(S["act_sq"], TT * k)
                A(std[:, 0:TT], ss[:, 0:TT], ACT.Sqrt, bias=eps6, scale=1.0 / D).then_inc(S["std_ready"], 1)

            def normed_T(name, c0):
                for t in range(KT):
                    act.wait_ge(*filled(name, t))
                    A(hT[:, t, 0:SEQ], bank(name, t)[:, 0:SEQ], ACT.Copy, scale=pcol[:, 1, c0 + t:c0 + t + 1])\
                        .then_inc(*read(name, t))

            mean_square(1)
            normed_T("x2T", 64)
            act.wait_ge(*filled("ga", 0))
            A(rows[:, 0, 0:SEQ], bank("ga", 0)[0:GH, 0:SEQ], ACT.Identity, bias=p4[:, 1:2]).then_inc(*read("ga", 0))
            act.wait_ge(*filled("gb", 0))
            A(rows[:, 4, 0:SEQ], bank("gb", 0)[0:GH, 0:SEQ], ACT.Sigmoid).then_inc(*read("gb", 0))
            act.wait_ge(*drained("ga", 0))
            link(A(rows[:, 2, 0:SEQ], rows[:, 0, 0:SEQ], ACT.Abs))
            link(A(rows[:, 2, 0:SEQ], rows[:, 2, 0:SEQ], ACT.Exp, scale=-1.0))
            A(p4[:, 0:1], p4[:, 0:1], ACT.Exp)
            A(rows[:, 2, 0:SEQ], rows[:, 2, 0:SEQ], ACT.Ln, bias=1.0).then_inc(S["softplus_ready"], 1)
            act.wait_ge(S["pads_ready"], 2)
            for t in range(12):
                act.wait_ge(*filled("gqkv", t))
                A(graw[:, t, 3:3 + SEQ], bank("gqkv", t)[:, 0:SEQ], ACT.Copy).then_inc(*read("gqkv", t))
            def copy_mqk(t0, t1):
                for t in range(t0, t1):
                    act.wait_ge(*filled("mqk", t))
                    A(mq[:, t, :], bank("mqk", t)[:, 0:SEQ], ACT.Copy).then_inc(*read("mqk", t))

            copy_mqk(0, 2)
            for g in range(3):
                act.wait_ge(S["gpre_ready"], g + 1)
                A(gsig[:, 4 * g:4 * g + 4, :], gconv[:, 4 * g:4 * g + 4, :], ACT.Sigmoid).then_inc(S["gsilu_ready"], 1)
            for t in range(4):
                act.wait_ge(S["gconv_ready"], t // 2 + 1)
                A(gsq[:, 2 * t:2 * t + 2, :], gconv[:, 2 * t:2 * t + 2, :], ACT.Square).then_inc(S["gsq_ready"], 1)
            copy_mqk(2, 5)
            for t in range(4):
                act.wait_ge(*filled("nq", t))
                A(gsq[:, 2 * t:2 * t + 2, :].rearrange("p t n -> p (t n)"), bank("nq", t)[:], ACT.Sqrt, bias=eps6)\
                    .then_inc(*read("nq", t))
            copy_mqk(5, 8)
            act.wait_ge(*filled("mv", 0))
            A(mval[:, 0, :], bank("mv", 0)[:], ACT.Copy).then_inc(*read("mv", 0))
            for h in range(GH):
                act.wait_ge(S["dlog_ready"], h + 1)
                A(dec[:, h % 2, 0:384], dec[:, h % 2, 0:384], ACT.Exp).then_inc(S["dec_ready"], 1)
            act.wait_ge(*filled("mv", 1))
            A(mval[:, 1, :], bank("mv", 1)[:], ACT.Copy).then_inc(*read("mv", 1))

            def copy_X(lv, half):
                act.wait_ge(*filled("X", lv, half))
                A(Xb[:, 4 * half:4 * half + 4, :].rearrange("p q n -> p (q n)"), bank("X", lv, half)[:], ACT.Copy)\
                    .then_inc(*read("X", lv, half))

            def softmax(h):
                act.wait_ge(S["logits_ready"], h + 1)
                w = pm[:, h % 2, :]
                A(w[:, 0:P], w[:, 0:P], ACT.Exp, bias=nmax[:, 2 * (h % 2):2 * (h % 2) + 1],
                  accum_out=psum_[:, 2 * (h % 2):2 * (h % 2) + 1])
                A(w[:, P:P + SEQ], w[:, P:P + SEQ], ACT.Exp, bias=nmax[:, 2 * (h % 2) + 1:2 * (h % 2) + 2],
                  accum_out=psum_[:, 2 * (h % 2) + 1:2 * (h % 2) + 2]).then_inc(S["exp_ready"], 1)

            def copy_pT(h):
                act.wait_ge(*filled("pT", h))
                A(pTs[:, h % 2, :], bank("pT", h)[:, 0:384], ACT.Copy).then_inc(*read("pT", h))

            def copy_av(h):
                b = MD * (h % 2)
                act.wait_ge(*filled("av", h))
                A(mix2T[b:b + MD, h // 2, :], bank("av", h)[b:b + MD, 0:SEQ], ACT.Copy).then_inc(*read("av", h))

            for lv in range(LEVELS):
                copy_X(lv, 0)
                copy_X(lv, 1)
                if lv:
                    copy_av(lv - 1)
                softmax(lv)
                if lv < 4:
                    act.wait_ge(*filled("gz", lv))
                    A(gz[:, lv // 2, 256 * (lv % 2):256 * (lv % 2) + 256], bank("gz", lv)[:, 0:256], ACT.Sigmoid)\
                        .then_inc(S["gzsig_ready"], 1)
                copy_pT(lv)
            softmax(MH - 1)
            copy_av(MH - 2)
            copy_pT(MH - 1)
            copy_av(MH - 1)
            act.wait_ge(*filled("U1", 0))
            A(U[:, 0, :, :].rearrange("p h n -> p (h n)"), bank("U1", 0)[:], ACT.Copy).then_inc(*read("U1", 0))
            act.wait_ge(*filled("U2", 0))
            A(U[:, 1, :, :].rearrange("p h n -> p (h n)"), bank("U2", 0)[:], ACT.Copy).then_inc(*read("U2", 0))
            warm(ACT.Sqrt)
            act.wait_ge(S["var_ready"], 5)
            A(std, ss, ACT.Sqrt, bias=eps6, scale=1.0 / GD).then_inc(S["std_ready"], 1)
            for b in range(2):
                act.wait_ge(*filled("obT", b))
                A(mix2T[:, 4 + 2 * b:6 + 2 * b, :].rearrange("p t n -> p (t n)"), bank("obT", b)[:], ACT.Copy,
                  scale=pcol[:, 1, 80:81]).then_inc(*read("obT", b))
            mean_square(2)
            normed_T("x3T", 72)
            warm(ACT.Exp)
            act.wait_ge(S["gmax_ready"], 1)
            for m in range(TT):
                A(gexp[:, m, :], lg2[:, m, 0:NG], ACT.Exp, bias=ngmax[:, m:m + 1], accum_out=gsum[:, m:m + 1])\
                    .then_inc(S["gexp_ready"], 1)
            act.wait_ge(S["e2_ready"], 1)
            A(e2, e2, ACT.Exp).then_inc(S["e2exp_ready"], 1)

            def hi_gate_up(it, e, i):
                s = (base + 2 * e) % SLOTS
                if i == 0:
                    act.wait_ge(S[f"slot{s}_loaded"], it * 128 + (first[2 * (e % 2)] + 32 * (e // 2)))
                act.wait_ge(S["gu_used"], it * (4 * EG) + (4 * e + i + 1))
                A(gus[:, i, HI, :, :, :].rearrange("p c k n -> p c (k n)"),
                  ring[:, s, :].rearrange("p (c i n) -> p i c n", c=2, i=4)[:, i, :, :], ACT.Copy)\
                    .then_inc(S["gu_hi"], 1)

            def hi_down(it, e):
                s = (base + 2 * e + 1) % SLOTS
                act.wait_ge(S[f"down{e % 2}_loaded"], it * (8 * EG) + 16 * (e // 2 + 1))
                for i in range(2):
                    act.wait_ge(S["dn_used"], it * (2 * EG) + (2 * e + i + 1))
                    A(dns2[:, i, HI, :], ring[:, s, i * D:(i + 1) * D], ACT.Copy).then_inc(S["dn_hi"], 1)

            def copy_gathered(it):
                act.wait_ge(S["gathered"], it + 1)
                for k in range(KT):
                    ins = A(xg[:, k, :], ps[6 + k // 4][:, (k % 4) * CAP:(k % 4 + 1) * CAP], ACT.Copy,
                            scale=pcol[:, 1, 72 + k:73 + k])
                ins.then_inc(S["xg_ready"], 1)
                act.wait_ge(S["xg_ready"], it + 1)
                A(xgs[:, HI, :, :], xg, ACT.Copy).then_inc(S["xg_hi"], 1)

            def hi_hidden(it, e):
                act.wait_ge(S["hidT_full"], it * EG + (e + 1))
                A(hidTs[:, e % 2, HI, :], ps[2 + e % 2][:, 0:2 * CAP], ACT.Copy).then_inc(S["hidT_hi"], 1)

            base = CHUNK_AT["gu", 0]
            first = [loaded_count(base + q) for q in range(SLOTS)]
            act.sem_inc(S["gu_used"], 4)
            act.sem_inc(S["dn_used"], 2)
            for i in range(4):
                hi_gate_up(0, 0, i)
            copy_gathered(0)
            for c in range(BLOCKS // 2):
                act.wait_ge(*filled("sT", c))
                A(pslot[:, 2 * c:2 * c + 2, :].rearrange("p b n -> p (b n)"), bank("sT", c)[:], ACT.Copy)\
                    .then_inc(*read("sT", c))
            act.wait_ge(S["turns_ready"], 1)
            turns = act.value_load(turns_[0:1, 0:1], min_val=NG - 1, max_val=BLOCKS - 1)

            def block_of_tokens(it, is_last):
                for e in range(EG):
                    more = not (is_last and e == EG - 1)
                    for i in range(4):
                        if i == 3:
                            act.wait_ge(S["gu_used"], it * (4 * EG) + (4 * e + 8))
                            A(sg[:, e % 2, :], ps[e % 2][:, 0:EF], ACT.Sigmoid).then_inc(S["sg_ready"], 1)
                        if more:
                            hi_gate_up(it, e + 1, i)
                    if e >= 1:
                        hi_hidden(it, e - 1)
                    if e != 1:
                        hi_down(it, max(e - 1, 0))
                if not is_last:
                    copy_gathered(it + 1)
                hi_hidden(it, EG - 1)
                hi_down(it, EG - 1)
                act.wait_ge(S["dn_used"], it * (2 * EG) + (2 * EG + 2))
                A(yg[:, 0:512], ps[4][:], ACT.Copy)
                A(yg[:, 512:D], ps[5][:], ACT.Copy).then_inc(S["yg_ready"], 1)

            with act.Fori(0, turns) as it:
                block_of_tokens(it, False)
            block_of_tokens(turns, True)
            mean_square(3)

        @block.vector
        def _(dve):
            V = nc.vector
            n_dve = [0]

            def step(ins):
                n_dve[0] += 1
                ins.then_inc(S["dve_chain"], 1)

            def settle():
                dve.wait_ge(S["dve_chain"], n_dve[0])

            def link(ins):
                step(ins)
                settle()

            def stt(out, in0, scalar, in1, op0, op1):
                return V.scalar_tensor_tensor(out=out, in0=in0, scalar=scalar, in1=in1, op0=op0, op1=op1)

            def layer_stats(rows_, k):
                for r, (x, n) in enumerate(rows_):
                    for c in range(2):
                        step(V.bn_stats(stats[0:n, 12 * r + 6 * c:12 * r + 6 * c + 6], x[:, 512 * c:512 * c + 512]))
                settle()
                for r, (x, n) in enumerate(rows_):
                    ins = V.bn_aggr(mv3[0:n, r, :], stats[0:n, 12 * r:12 * r + 12])
                    if r == len(rows_) - 1:
                        ins.then_inc(S["var_ready"], 1)
                    else:
                        step(ins)
                dve.wait_ge(S["std_ready"], k)
                settle()
                link(V.reciprocal(rstd[:, 0:3] if len(rows_) == 3 else rstd[:, 0:2],
                                  std[:, 0:3] if len(rows_) == 3 else std[:, 0:2]))

            link(V.memset(mv, 1.0))
            V.memset(eps5, 1e-5).then_inc(S["eps_ready"], 1)
            V.memset(eps6, 1e-6).then_inc(S["eps_ready"], 1)
            dve.wait_ge(S["x_loaded"], 48)
            layer_stats([(tokA[:, 0, :], P), (tokA[:, 1, :], P), (meta, META)], 1)
            for m in range(TT):
                step(V.tensor_scalar(tokA[:, m, :], tokA[:, m, :], mv3[:, m, 0:1], rstd[:, m:m + 1],
                                     ALU.subtract, ALU.mult))
            settle()
            V.tensor_scalar(meta, meta, mv3[0:META, 2, 0:1], rstd[0:META, 2:3], ALU.subtract, ALU.mult)\
                .then_inc(S["xn_ready"], 1)
            for c, n in ((0, P), (1, NROW1)):
                dve.wait_ge(*filled("prow", c))
                V.tensor_copy(pcol[:, c, 0:n], bank("prow", c)[:, 0:n]).then_inc(*read("prow", c))
            L = [lrow[:, c, :] for c in range(16)]
            lre, lim, dt, zr, th, kk, r, er, sn, sh, t1, t2, lbr, lbi, cr, ci = L
            dve.wait_ge(S["dt_ready"], 1)
            V.tensor_tensor(zr.rearrange("p (a b) -> p a b", a=2), lre.rearrange("p (a b) -> p a b", a=2),
                            ldt[:].unsqueeze(2).broadcast_to([NST, 2, STATE]), ALU.mult).then_inc(S["zr_ready"], 1)
            link(V.tensor_tensor(th.rearrange("p (a b) -> p a b", a=2), lim.rearrange("p (a b) -> p a b", a=2),
                                 ldt[:].unsqueeze(2).broadcast_to([NST, 2, STATE]), ALU.mult))
            link(V.tensor_scalar(kk, th, 1.0 / (2.0 * math.pi), ROUND, ALU.mult, ALU.add))
            link(V.tensor_scalar(kk, kk, -ROUND, None, ALU.add))
            link(stt(r, kk, -TWO_PI_HI, th, ALU.mult, ALU.add))
            link(stt(r, kk, -TWO_PI_MID, r, ALU.mult, ALU.add))
            link(stt(r, kk, -TWO_PI_LO, r, ALU.mult, ALU.add))
            V.tensor_scalar(r, r, 3.1415925, -3.1415925, ALU.min, ALU.max).then_inc(S["angle_ready"], 1)
            step(V.tensor_tensor(t1, lre, lre, ALU.mult))
            step(V.tensor_tensor(t2, lim, lim, ALU.mult))
            settle()
            link(V.tensor_tensor(t1, t1, t2, ALU.add))
            link(V.reciprocal(kk, t1))
            dve.wait_ge(S["er_ready"], 1)
            dve.wait_ge(S["sin_ready"], 2)
            link(V.tensor_tensor(sh, sh, sh, ALU.mult))
            step(V.tensor_tensor(lbi, er, sn, ALU.mult))
            link(V.tensor_scalar(sh, sh, -2.0, 1.0, ALU.mult, ALU.add))
            link(V.tensor_tensor(lbr, er, sh, ALU.mult))
            link(V.tensor_scalar(sh, lbr, -1.0, None, ALU.add))
            step(V.tensor_tensor(t1, sh, lre, ALU.mult))
            step(V.tensor_tensor(t2, lbi, lim, ALU.mult))
            step(V.tensor_tensor(sn, lbi, lre, ALU.mult))
            step(V.tensor_tensor(er, sh, lim, ALU.mult))
            settle()
            step(V.tensor_tensor(t1, t1, t2, ALU.add))
            step(V.tensor_tensor(sn, sn, er, ALU.subtract))
            settle()
            step(V.tensor_tensor(cr, t1, kk, ALU.mult))
            settle()
            V.tensor_tensor(ci, sn, kk, ALU.mult).then_inc(S["poles_ready"], 1)
            dve.wait_ge(S["const_ready"], 2)
            dve.wait_ge(S["bc_loaded"], 64)
            for c in range(2):
                sign = 1.0 - 2.0 * c
                step(V.tensor_scalar(cexp[:, c, :, 0:STATE], craw[:, c, :, :], even, sign, ALU.mult, ALU.mult))
                ins = V.tensor_scalar(cexp[:, c, :, STATE:P], craw[:, c, :, :], odd, sign, ALU.mult, ALU.mult)
                if c:
                    ins.then_inc(S["cexp_ready"], 1)
                else:
                    step(ins)
            dve.wait_ge(*filled("lam", 0))
            V.tensor_copy(lamcol, bank("lam", 0)[:, 0:64]).then_inc(*read("lam", 0))
            dve.wait_ge(*drained("lam", 0))
            ar, ai = lamcol[:, 0:16], lamcol[:, 16:32]
            crc = lamcol[:, 32:48].unsqueeze(2).broadcast_to([P, NST, GRP])
            cic = lamcol[:, 48:64].unsqueeze(2).broadcast_to([P, NST, GRP])
            tmp = [scanR[:, 256 * k:256 * k + 256].rearrange("p (i h) -> p i h", i=NST) for k in range(4)]
            step(V.tensor_tensor(tmp[0], crc, braw[:, 0, :, :], ALU.mult))
            step(V.tensor_tensor(tmp[1], cic, braw[:, 1, :, :], ALU.mult))
            step(V.tensor_tensor(tmp[2], crc, braw[:, 1, :, :], ALU.mult))
            step(V.tensor_tensor(tmp[3], cic, braw[:, 0, :, :], ALU.mult))
            settle()
            dve.wait_ge(S["bexp_zero"], 1)
            for g in range(2):
                p0 = g * STATE
                step(V.tensor_tensor(bexp[p0:p0 + STATE, 0, :, g * GRP:(g + 1) * GRP], tmp[0][p0:p0 + STATE],
                                     tmp[1][p0:p0 + STATE], ALU.subtract))
                ins = V.tensor_tensor(bexp[p0:p0 + STATE, 1, :, g * GRP:(g + 1) * GRP], tmp[2][p0:p0 + STATE],
                                      tmp[3][p0:p0 + STATE], ALU.add)
                step(ins) if g == 0 else ins.then_inc(S["bexp_ready"], 1)
            settle()
            arn = ar.unsqueeze(1)
            ain = ai.unsqueeze(1)
            step(V.tensor_copy(PW[:, 0, 0, :], ar))
            step(V.tensor_copy(PW[:, 1, 0, :], ai))
            settle()
            n = 1
            while n < CHUNK:
                hi = [PW[:, c, n - 1:n, :].broadcast_to([P, n, NST]) for c in range(2)]
                lo = [PW[:, c, 0:n, :] for c in range(2)]
                q = [scanR[:, 128 * k:128 * k + n * NST].rearrange("p (s i) -> p s i", i=NST) for k in range(4)]
                step(V.tensor_tensor(q[0], hi[0], lo[0], ALU.mult))
                step(V.tensor_tensor(q[1], hi[1], lo[1], ALU.mult))
                step(V.tensor_tensor(q[2], hi[0], lo[1], ALU.mult))
                step(V.tensor_tensor(q[3], hi[1], lo[0], ALU.mult))
                settle()
                step(V.tensor_tensor(PW[:, 0, n:2 * n, :], q[0], q[1], ALU.subtract))
                step(V.tensor_tensor(PW[:, 1, n:2 * n, :], q[2], q[3], ALU.add))
                settle()
                n *= 2
            dve.wait_ge(*drained("bu", 2 * NST - 1))

            def times(v, s):
                n = NCH - (s is not None)
                src = (ar, ai)[v] if s is None else PW[:, v, s, :]
                return src.unsqueeze(1).unsqueeze(3).broadcast_to([P, 2, NST, n])

            for s in range(1, CHUNK):
                prev, here = X[:, :, :, s - 1, :], X[:, :, :, s, :]
                step(V.tensor_tensor(T1, prev, times(0, None), ALU.mult))
                step(V.tensor_tensor(T2, prev, times(1, None), ALU.mult))
                settle()
                link(V.tensor_tensor(here, here, T1, ALU.add))
                step(V.tensor_tensor(here[:, 0], here[:, 0], T2[:, 1], ALU.subtract))
                step(V.tensor_tensor(here[:, 1], here[:, 1], T2[:, 0], ALU.add))
                settle()
            link(V.tensor_copy(EN, X[:, :, :, CHUNK - 1, :]))
            a16 = [PW[:, v, CHUNK - 1, :].unsqueeze(1).broadcast_to([P, 2, NST]) for v in range(2)]
            for c in range(1, NCH - 1):
                step(V.tensor_tensor(T1[:, :, :, 0], EN[:, :, :, c - 1], a16[0], ALU.mult))
                step(V.tensor_tensor(T2[:, :, :, 0], EN[:, :, :, c - 1], a16[1], ALU.mult))
                settle()
                link(V.tensor_tensor(EN[:, :, :, c], EN[:, :, :, c], T1[:, :, :, 0], ALU.add))
                step(V.tensor_tensor(EN[:, 0, :, c], EN[:, 0, :, c], T2[:, 1, :, 0], ALU.subtract))
                step(V.tensor_tensor(EN[:, 1, :, c], EN[:, 1, :, c], T2[:, 0, :, 0], ALU.add))
                settle()
            prev = EN[:, :, :, 0:NCH - 1]
            for s in range(CHUNK):
                here = X[:, :, :, s, 1:NCH]
                step(V.tensor_tensor(T1[:, :, :, 1:NCH], prev, times(0, s), ALU.mult))
                step(V.tensor_tensor(T2[:, :, :, 1:NCH], prev, times(1, s), ALU.mult))
                settle()
                link(V.tensor_tensor(here, here, T1[:, :, :, 1:NCH], ALU.add))
                step(V.tensor_tensor(here[:, 0], here[:, 0], T2[:, 1, :, 1:NCH], ALU.subtract))
                ins = V.tensor_tensor(here[:, 1], here[:, 1], T2[:, 0, :, 1:NCH], ALU.add)
                ins.then_inc(S["scan_ready"], 1) if s == CHUNK - 1 else step(ins)
                settle()
            dve.wait_ge(S["v_biased"], 6)
            dve.wait_ge(S["o_biased"], 4)
            dve.wait_ge(*drained("qk", 7))
            for tap in range(4):
                for t in range(8):
                    w = pcol[:, 0, 8 * tap + t:8 * tap + t + 1]
                    if tap == 0:
                        ins = V.tensor_scalar(conv[:, t, :], raw[:, t, 0:LEN], w, pcol[:, 0, 32 + t:33 + t],
                                              ALU.mult, ALU.add)
                    else:
                        ins = stt(conv[:, t, :], raw[:, t, tap:tap + LEN], w, conv[:, t, :], ALU.mult, ALU.add)
                    ins.then_inc(S["conv_ready"], 1) if (tap, t) == (3, 7) else step(ins)
                settle()
            dve.wait_ge(S["silu_ready"], 1)
            half = 4 * LEN
            V.tensor_tensor(convR[:, 0:half], convR[:, 0:half], rawR[:, 0:half], ALU.mult).then_inc(S["qk_ready"], 1)
            stt(convR[:, half:2 * half], convR[:, half:2 * half], DK ** -0.5, rawR[:, half:2 * half],
                ALU.mult, ALU.mult).then_inc(S["qk_ready"], 1)
            dve.wait_ge(S["softplus_ready"], 1)
            dve.wait_ge(S["rowone_ready"], 1)
            rowones = rowone[:].broadcast_to([HEADS, LEN])
            link(stt(rows[:, 2, :], rows[:, 1, :], 0.0, rows[:, 2, :], ALU.min, ALU.subtract))
            link(V.tensor_tensor_scan(rows[:, 3, :], rowones, rows[:, 2, :], 0.0, ALU.mult, ALU.add))
            link(V.tensor_tensor(rows[:, 0, :], rows[:, 0, :], rows[:, 3, :], ALU.subtract))
            link(V.tensor_tensor_scan(rows[:, 4, :], rows[:, 0, :], rows[:, 0, :], 0.0, ALU.max, ALU.max))
            V.tensor_tensor(rows[:, 5, :], rows[:, 3, :], rows[:, 4, :], ALU.add).then_inc(S["gate_rows_ready"], 1)
            for t in range(UT):
                dve.wait_ge(*filled("y", t))
                stt(yu[:, t, :].rearrange("p (s n) -> p s n", s=CHUNK), uTp[:, t, :, 1:NCH], pcol[:, 0, 68 + t:69 + t],
                    bank("y", t)[:, 0:SEQ].rearrange("p (s n) -> p s n", s=CHUNK), ALU.mult, ALU.add)\
                    .then_inc(*read("y", t))
            dve.wait_ge(*filled("gm", 0))
            dve.wait_ge(S["em_ready"], 1)
            link(V.tensor_copy(gcol[0:META, 0:4], bank("gm", 0)[0:META, 0:4]))
            V.tensor_copy(gcol[:, 4:12], bank("gm", 0)[:, 4:12]).then_inc(*read("gm", 0))
            dve.wait_ge(*drained("gm", 0))
            for t in range(KT):
                dve.wait_ge(S["zsig_ready"], t + 1)
                V.tensor_tensor(mixT[:, t, :], bank("z", t)[:, 0:SEQ], zsig[:, t % 2, :], ALU.mult)\
                    .then_inc(*read("z", t))
                dve.wait_ge(*drained("z", t))
                step(V.tensor_tensor(mixT[:, t, :], mixT[:, t, :], gT[:, t, :], ALU.mult))
            for h in range(HEADS):
                b = h % 2
                dve.wait_ge(*filled("ms", h))
                M = bank("ms", h)[:, 0:SEQ]
                V.tensor_scalar(wgt[0:META, b, 0:SEQ], M[0:META], gcol[0:META, h:h + 1], 0.0, ALU.subtract, ALU.max)
                V.tensor_scalar(wgt[:, b, SEQ:2 * SEQ], M, gcol[:, 4 + h:5 + h], 0.0, ALU.subtract, ALU.max)
                V.tensor_scalar(wgt[:, b, 2 * SEQ:640], M[:, P:SEQ], gcol[:, 8 + h:9 + h], 0.0, ALU.subtract, ALU.max)\
                    .then_inc(S["wlog_ready"], 1)
                dve.wait_ge(S["w_ready"], h + 1)
                if h >= 2:
                    dve.wait_ge(*filled("h", 2 * (h - 2) + 1))
                V.tensor_tensor(pt[0:META, b, 0:SEQ], wgt[0:META, b, 0:SEQ], bank("ms", h)[0:META, SEQ:2 * SEQ],
                                ALU.mult).then_inc(*read("ms", h))
                dve.wait_ge(*filled("s", h))
                V.tensor_tensor(pt[:, b, SEQ:640], wgt[:, b, SEQ:640], bank("s", h)[:, 0:384], ALU.mult)\
                    .then_inc(*read("s", h))
                dve.wait_ge(*drained("s", h))
                step(V.tensor_tensor(pt[:, b, SEQ:SEQ + P], pt[:, b, SEQ:SEQ + P], tri[:], ALU.mult))
                V.tensor_tensor(pt[:, b, 2 * SEQ:640], pt[:, b, 2 * SEQ:640], tri[:], ALU.mult)\
                    .then_inc(S["pt_ready"], 1)
                settle()
            for k in range(2 * HEADS):
                h, m = k // 2, k % 2
                dve.wait_ge(*filled("h", k))
                o = bank("h", k)
                link(V.tensor_scalar(rden[:, k:k + 1], o[:, DV:DV + 1], -1.0, None, ALU.mult))
                link(stt(den[:, k:k + 1], o[:, DV:DV + 1], em[:, 4 * m + h:4 * m + h + 1], rden[:, k:k + 1],
                         ALU.max, ALU.max))
                link(V.reciprocal(rden[:, k:k + 1], den[:, k:k + 1]))
                V.tensor_scalar(hm[:, m, h * DV:(h + 1) * DV], o[:, 0:DV], rden[:, k:k + 1], None, ALU.mult)\
                    .then_inc(*read("h", k))
                dve.wait_ge(*drained("h", k))
                step(V.bn_stats(bst[:, 6 * k:6 * k + 6], hm[:, m, h * DV:(h + 1) * DV]))
            settle()
            for k in range(2 * HEADS):
                ins = V.bn_aggr(mvh3[:, k, :], bst[:, 6 * k:6 * k + 6])
                ins.then_inc(S["var_ready"], 1) if k == 2 * HEADS - 1 else step(ins)
            dve.wait_ge(S["std_ready"], 2)
            link(V.reciprocal(rstd, std))
            for k in range(2 * HEADS):
                h, m = k // 2, k % 2
                part = hm[:, m, h * DV:(h + 1) * DV]
                step(V.tensor_scalar(part, part, mvh3[:, k, 0:1], rstd[:, k:k + 1], ALU.subtract, ALU.mult))
            settle()
            dve.wait_ge(S["osig_ready"], 1)
            V.tensor_tensor(hm, hm, tokB[:], ALU.mult).then_inc(S["gated_ready"], 1)
            for t in range(KT):
                dve.wait_ge(*filled("ym", t))
                V.tensor_tensor(ymg[:, t % 2, :], bank("ym", t)[:, 0:SEQ], gT[:, 8 + t, :], ALU.mult)\
                    .then_inc(*read("ym", t))
                dve.wait_ge(*drained("ym", t))
                settle()
                V.tensor_tensor(mixT[:, t, :], mixT[:, t, :], ymg[:, t % 2, :], ALU.add).then_inc(S["mix_ready"], 1)
            dve.wait_ge(S["h0_ready"], 1)
            for k in range(4):
                m, n = k % 2, k // 2
                dve.wait_ge(*filled("wo", k))
                part = tokA[:, m, 512 * n:512 * n + 512]
                stt(part, part, ALPHA, bank("wo", k)[:], ALU.mult, ALU.add).then_inc(*read("wo", k))
            for k in range(4):
                dve.wait_ge(*drained("wo", k))

            def normalised(count, k):
                layer_stats([(tokA[:, m, :], P) for m in range(TT)], k)
                for m in range(TT):
                    ins = V.tensor_scalar(tokB[:, m, :], tokA[:, m, :], mv3[:, m, 0:1], rstd[:, m:m + 1],
                                          ALU.subtract, ALU.mult)
                    if m == TT - 1 and count:
                        ins.then_inc(S["xn_ready"], 1)
                    else:
                        step(ins)
                if count:
                    dve.wait_ge(S["xn_ready"], count)
                settle()

            def lo(out_, whole, hi):
                return V.tensor_tensor(out_, whole, hi.bitcast(FP32), ALU.subtract)

            def up_lo(it, q):
                for i in range(2):
                    dve.wait_ge(S["wup_hi"], it * (2 * SLOTS) + (2 * q + i + 1))
                    lo(ups[:, i, LO, :, :].rearrange("p k n -> p (k n)"),
                       ring[:, (base + q) % SLOTS, 1024 * i:1024 * (i + 1)],
                       ups[:, i, HI, :, :].rearrange("p k n -> p (k n)")).then_inc(S["wup_split"], 1)

            base = CHUNK_AT["ffn", 0]
            normalised(2, 3)
            up_lo(0, 0)
            for t in range(KT):
                dve.wait_ge(S["x_hi"], t + 1)
                lo(xs[:, LO, t, :], hT[:, t, 0:SEQ], xs[:, HI, t, :]).then_inc(S["x_split"], 1)

            def square_and_lo(it, q, more):
                for m in range(2):
                    dve.wait_ge(S["relu_ready"], it * (2 * SLOTS) + (2 * q + m + 1))
                    half = ffr[:, q % 2, m * SEQ:(m + 1) * SEQ]
                    V.tensor_tensor(ffh[:, q % 2, m * SEQ:(m + 1) * SEQ], half, half, ALU.mult)\
                        .then_inc(S["ffh_ready"] if m else S["ffh_half_ready"], 1)
                if more:
                    up_lo(it, q + 1)
                dve.wait_ge(S["ffh_hi"], it * SLOTS + (q + 1))
                lo(ffs[:, q % 2, LO, :], ffh[:, q % 2, :], ffs[:, q % 2, HI, :]).then_inc(S["ffh_split"], 1)
                for i in range(2):
                    dve.wait_ge(S["wdn_hi"], it * (2 * SLOTS) + (2 * q + i + 1))
                    lo(dns[:, i, LO, :], ring[:, (base + q) % SLOTS, 2048 + i * D:2048 + (i + 1) * D],
                       dns[:, i, HI, :]).then_inc(S["wdn_split"], 1)

            turns = FF // 256 // SLOTS
            with dve.Fori(0, turns - 1) as it:
                for q in range(SLOTS):
                    square_and_lo(it, q, True)
            for q in range(SLOTS):
                square_and_lo(turns - 1, q, q < SLOTS - 1)
            dve.wait_ge(S["h1_ready"], 1)
            for m in range(TT):
                dve.wait_ge(S["ffn_sums"], m + 1)
                for n in range(2):
                    part = tokA[:, m, 512 * n:512 * n + 512]
                    step(V.tensor_tensor(part, part, ps[4 + 2 * m + n][:], ALU.add))
            settle()
            normalised(0, 4)
            dve.wait_ge(S["bc_rows_loaded"], 96)
            for m in range(TT):
                link(V.tensor_tensor(tokA[:, m, :], tokB[:, m, :], bcL[:, 0, :], ALU.mult))
                V.tensor_tensor(tokA[:, m, :], tokA[:, m, :], bcL[:, 1, :], ALU.add).then_inc(S["row_tile_ready"], 1)
            dve.wait_ge(S["row_tile_ready"], TT)
            dve.sem_inc(S["res_ready"], 1)

            def rms(count, k):
                dve.wait_ge(S["std_ready"], k)
                link(V.reciprocal(rstd[:, 0:2], std[:, 0:2]))
                for m in range(TT):
                    ins = V.tensor_scalar(tokB[:, m, :], tokA[:, m, :], rstd[:, m:m + 1], None, ALU.mult)
                    ins.then_inc(S["xn_ready"], 1) if m and count else step(ins)

            rms(3, 5)
            dve.wait_ge(S["softplus_ready"], 2)
            link(stt(rows[:, 1, 0:SEQ], rows[:, 0, 0:SEQ], 0.0, rows[:, 2, 0:SEQ], ALU.max, ALU.add))
            link(V.tensor_scalar(rows[:, 1, 0:SEQ], rows[:, 1, 0:SEQ], p4[:, 0:1], -1.0, ALU.mult, ALU.mult))
            V.tensor_tensor_scan(rows[:, 3, 0:SEQ], rowone[:].broadcast_to([GH, SEQ]), rows[:, 1, 0:SEQ], 0.0, ALU.mult, ALU.add)\
                .then_inc(S["decay_rows_ready"], 1)
            for g in range(3):
                dve.wait_ge(*drained("gqkv", 4 * g + 3))
                for tap in range(4):
                    for t in range(4 * g, 4 * g + 4):
                        w = pcol[:, 1, 12 * tap + t:12 * tap + t + 1]
                        if tap == 0:
                            ins = V.tensor_scalar(gconv[:, t, :], graw[:, t, 0:SEQ], w, None, ALU.mult)
                        else:
                            ins = stt(gconv[:, t, :], graw[:, t, tap:tap + SEQ], w, gconv[:, t, :], ALU.mult, ALU.add)
                        ins.then_inc(S["gpre_ready"], 1) if (tap, t) == (3, 4 * g + 3) else step(ins)
                    settle()
            dve.wait_ge(*filled("Gc", 0))
            V.tensor_copy(gc, bank("Gc", 0)[:, 0:16]).then_inc(*read("Gc", 0))
            for g in range(3):
                dve.wait_ge(S["gsilu_ready"], g + 1)
                V.tensor_tensor(gconv[:, 4 * g:4 * g + 4, :], gconv[:, 4 * g:4 * g + 4, :], gsig[:, 4 * g:4 * g + 4, :],
                                ALU.mult).then_inc(S["gconv_ready"], 1)
            for t in range(4):
                dve.wait_ge(*drained("nq", t))
                n2 = gsq[:, 2 * t:2 * t + 2, :]
                link(V.reciprocal(n2, n2))
                stt(gconv[:, 2 * t:2 * t + 2, :], gconv[:, 2 * t:2 * t + 2, :], GD ** -0.5 if t < 2 else 1.0, n2,
                    ALU.mult, ALU.mult).then_inc(S["gnorm_ready"], 1)
            dve.wait_ge(*drained("Gc", 0))
            for m in range(TT):
                dve.wait_ge(*filled("vk", m))
                for h in range(GH):
                    ins = V.tensor_scalar(vb[:, m, h, :], bank("vk", m)[:, h * P:(h + 1) * P],
                                          gc[:, 8 + 4 * m + h:9 + 4 * m + h], None, ALU.mult)
                    if h == GH - 1:
                        ins.then_inc(*read("vk", m))
                    else:
                        step(ins)
            for h in range(GH):
                b = h % 2
                dve.wait_ge(*filled("gb_", h))
                G, beta = bank("gb_", h)[:, 0:SEQ], bank("gb_", h)[:, SEQ:2 * SEQ]
                V.tensor_scalar(dec[:, b, 0:SEQ], G, gc[:, h:h + 1], 0.0, ALU.subtract, ALU.min)
                V.tensor_scalar(dec[:, b, SEQ:384], G[:, P:SEQ], gc[:, 4 + h:5 + h], 0.0, ALU.subtract, ALU.min)\
                    .then_inc(S["dlog_ready"], 1)
                dve.wait_ge(S["dec_ready"], h + 1)
                dve.wait_ge(*filled("kk", h))
                V.tensor_tensor(aT[:, h, :], dec[:, b, 0:384], bank("kk", h)[:, 0:384], ALU.mult).then_inc(*read("kk", h))
                dve.wait_ge(*filled("qk_", h))
                V.tensor_tensor(qkT[:, h, :], dec[:, b, 0:384], bank("qk_", h)[:, 0:384], ALU.mult)\
                    .then_inc(*read("qk_", h))
                dve.wait_ge(*drained("kk", h))
                step(V.tensor_tensor(aT[:, h, SEQ:384], aT[:, h, SEQ:384], beta[:, P:SEQ], ALU.mult))
                V.tensor_tensor(aT[:, h, 0:SEQ], aT[:, h, 0:SEQ], beta, ALU.mult).then_inc(*read("gb_", h))
                dve.wait_ge(*drained("gb_", h))
                dve.wait_ge(*drained("qk_", h))
                settle()
                step(V.tensor_tensor(qkT[:, h, 0:P], qkT[:, h, 0:P], tri[:], ALU.mult))
                step(V.tensor_tensor(qkT[:, h, SEQ:384], qkT[:, h, SEQ:384], tri[:], ALU.mult))
                step(V.tensor_tensor(aT[:, h, 0:P], aT[:, h, 0:P], stri[:], ALU.mult))
                settle()
                V.tensor_tensor(aT[:, h, SEQ:384], aT[:, h, SEQ:384], stri[:], ALU.mult).then_inc(S["aT_ready"], 1)

            def logits(h):
                w, o, nm = pm[:, h % 2, :], bank("sc", h), nmax[:, 2 * (h % 2):2 * (h % 2) + 2]
                if h >= 2:
                    dve.wait_ge(*filled("pT", h - 2))
                dve.wait_ge(*filled("sc", h))
                step(stt(w[:, 0:P], o[:, 0:P], MD ** -0.5, negm[:], ALU.mult, ALU.add))
                step(V.tensor_scalar(w[:, P:SEQ], o[:, P:SEQ], MD ** -0.5, None, ALU.mult))
                stt(w[:, SEQ:384], o[:, SEQ:384], MD ** -0.5, negm[:], ALU.mult, ALU.add).then_inc(*read("sc", h))
                settle()
                dve.wait_ge(*drained("sc", h))
                step(V.tensor_reduce(nm[:, 0:1], w[:, 0:P], AX.X, ALU.max, negate=True))
                settle()
                V.tensor_reduce(nm[:, 1:2], w[:, P:384], AX.X, ALU.max, negate=True).then_inc(S["logits_ready"], 1)

            def probs(h):
                w, c = pm[:, h % 2, :], 2 * (h % 2)
                dve.wait_ge(S["exp_ready"], h + 1)
                link(V.reciprocal(prec[:, c:c + 2], psum_[:, c:c + 2]))
                step(V.tensor_scalar(w[:, 0:P], w[:, 0:P], prec[:, c:c + 1], None, ALU.mult))
                settle()
                V.tensor_scalar(w[:, P:384], w[:, P:384], prec[:, c + 1:c + 2], None, ALU.mult)\
                    .then_inc(S["probs_ready"], 1)

            dve.wait_ge(S["masks_ready"], 1)
            for lv in range(LEVELS):
                if 1 <= lv < 5:
                    dve.wait_ge(S["gzsig_ready"], lv)
                    part = gz[:, (lv - 1) // 2, 256 * ((lv - 1) % 2):256 * ((lv - 1) % 2) + 256]
                    V.tensor_tensor(part, part, bank("gz", lv - 1)[:, 0:256], ALU.mult).then_inc(*read("gz", lv - 1))
                logits(lv)
                for half in range(2):
                    m4 = lvl[:, lv, :].unsqueeze(1).broadcast_to([P, 4, P])
                    for name, M in (("Z", Tm), ("ZT", Tt)):
                        part = M[:, 4 * half:4 * half + 4, :]
                        dve.wait_ge(*filled(name, lv, half))
                        V.tensor_tensor(Zm[:, 0:4, :] if name == "Z" else Zm[:, 4:8, :],
                                        bank(name, lv, half)[:].rearrange("p (q n) -> p q n", q=4), m4, ALU.mult)\
                            .then_inc(*read(name, lv, half))
                    dve.wait_ge(*drained("Z", lv, half))
                    dve.wait_ge(*drained("ZT", lv, half))
                    step(V.tensor_tensor(Tm[:, 4 * half:4 * half + 4, :], Tm[:, 4 * half:4 * half + 4, :],
                                         Zm[:, 0:4, :], ALU.subtract))
                    settle()
                    V.tensor_tensor(Tt[:, 4 * half:4 * half + 4, :], Tt[:, 4 * half:4 * half + 4, :],
                                    Zm[:, 4:8, :], ALU.subtract).then_inc(S["T_ready"], 1)
                    if half == 0:
                        probs(lv)
                    dve.wait_ge(S["T_ready"], 2 * lv + half + 1)
            logits(MH - 1)
            probs(MH - 1)
            dve.wait_ge(*filled("AU", 0))
            V.tensor_tensor(vb[:, 1, :, :].rearrange("p h n -> p (h n)"), vb[:, 1, :, :].rearrange("p h n -> p (h n)"),
                            bank("AU", 0)[:], ALU.subtract).then_inc(*read("AU", 0))
            for m in range(TT):
                dve.wait_ge(*filled("O", m))
                V.tensor_copy(ob[:, m, :, :].rearrange("p h n -> p (h n)"), bank("O", m)[:]).then_inc(*read("O", m))
                dve.wait_ge(*drained("O", m))
                link(V.tensor_tensor(Zm[:, 0:4, :], ob[:, m, :, :], ob[:, m, :, :], ALU.mult))
                ins = V.tensor_reduce(ss[:, 4 * m:4 * m + 4], Zm[:, 0:4, :], AX.X, ALU.add)
                ins.then_inc(S["var_ready"], 1) if m else link(ins)
            dve.wait_ge(S["std_ready"], 6)
            link(V.reciprocal(rstd, std))
            for m in range(TT):
                link(V.tensor_tensor(ob[:, m, :, :], ob[:, m, :, :],
                                     rstd[:, 4 * m:4 * m + 4].unsqueeze(2).broadcast_to([P, GH, GD]), ALU.mult))
                ins = V.tensor_tensor(ob[:, m, :, :].rearrange("p h n -> p (h n)"),
                                      ob[:, m, :, :].rearrange("p h n -> p (h n)"), gz[:, m, :], ALU.mult)
                ins.then_inc(S["ob_ready"], 1) if m else step(ins)
            for k in range(4):
                m, n = k % 2, k // 2
                dve.wait_ge(*filled("wout", k))
                part = tokA[:, m, 512 * n:512 * n + 512]
                V.tensor_tensor(part, part, bank("wout", k)[:], ALU.add).then_inc(*read("wout", k))
            for k in range(4):
                dve.wait_ge(*drained("wout", k))
            link(V.memset(gsum, 0.0))
            dve.sem_inc(S["res_ready"], 1)
            rms(4, 7)
            def spread(x, n):
                return x.unsqueeze(2).broadcast_to([P, TT, n])

            def first_max(out, x, top, n):
                eq, cum = req[:, 0:TT * n], rcum[:, 0:TT * n]
                keep = rkeep[:, 0:TT * NG] if n == NG else rkeep[:, TT * NG:TT * (NG + EG)]
                link(V.tensor_tensor(eq.rearrange("p (m n) -> p m n", m=TT), x, spread(top, n), ALU.is_equal))
                link(V.tensor_tensor_scan(cum, keep, eq, 0.0, ALU.mult, ALU.add))
                link(stt(out.rearrange("p m n -> p (m n)"), cum, 1.0, eq, ALU.is_equal, ALU.mult))

            for m in range(TT):
                dve.wait_ge(*filled("rt", m))
                V.tensor_copy(lg2[:, m, :], bank("rt", m)[:, 0:NG + NE]).then_inc(*read("rt", m))
            for m in range(TT):
                dve.wait_ge(*drained("rt", m))
            V.tensor_reduce(ngmax, lg2[:, :, 0:NG], AX.X, ALU.max, negate=True).then_inc(S["gmax_ready"], 1)
            link(V.tensor_reduce(top1, lg2[:, :, 0:NG], AX.X, ALU.max))
            first_max(fgs[:], lg2[:, :, 0:NG], top1, NG)
            for m in range(TT):
                step(V.tensor_tensor(rmul[:, m, :, :], lg2[:, m, NG:NG + NE].rearrange("p (g e) -> p g e", g=NG),
                                     fgs[:, m, :].unsqueeze(2).broadcast_to([P, NG, EG]), ALU.mult))
            settle()
            link(V.tensor_reduce(rig[:], rmul[:].rearrange("p m g e -> p m e g"), AX.X, ALU.add))
            link(V.tensor_reduce(top1, rig[:], AX.X, ALU.max))
            first_max(f1, rig[:], top1, EG)
            link(stt(rig[:], f1, 2.0 * NEG, rig[:], ALU.mult, ALU.add))
            link(V.tensor_reduce(top2, rig[:], AX.X, ALU.max))
            first_max(f2, rig[:], top2, EG)
            V.tensor_tensor(e2, top2, top1, ALU.subtract).then_inc(S["e2_ready"], 1)
            dve.wait_ge(S["gexp_ready"], TT)
            dve.wait_ge(S["e2exp_ready"], 1)
            link(stt(w0, e2, 1.0, gsum, ALU.add, ALU.mult))
            link(V.reciprocal(w0, w0))
            link(V.tensor_tensor(f2, f2, spread(e2, EG), ALU.mult))
            link(V.tensor_tensor(f1, f1, f2, ALU.add))
            V.tensor_tensor(wtok[:], f1, spread(w0, EG), ALU.mult).then_inc(S["group_ready"], 1)
            dve.wait_ge(*filled("cum", 0))
            o = bank("cum", 0)
            ranked = rmul[:, 0, 0:2, 0:NG]
            link(V.tensor_tensor(ranked, fgs[:], o[:, 0:TT * NG].rearrange("p (m g) -> p m g", m=TT), ALU.mult))
            link(V.tensor_reduce(rank[:, 0:TT], ranked, AX.X, ALU.add))
            link(V.tensor_scalar(rank[:, 0:TT], rank[:, 0:TT], -1.0, None, ALU.add))
            step(V.tensor_scalar(rank[:, TT:2 * TT], rank[:, 0:TT], -float(CAP), None, ALU.add))
            V.tensor_reduce(count[:, 0:1], o[:, 2 * NG:3 * NG], AX.X, ALU.max).then_inc(*read("cum", 0))
            dve.wait_ge(*drained("cum", 0))
            settle()
            link(V.tensor_scalar(count[:, 1:2], count[:, 0:1], CAP + 0.5, float(NG), ALU.is_gt, ALU.mult))
            V.tensor_scalar(turns_[:], count[0:1, 1:2], float(NG - 1), None, ALU.add).then_inc(S["turns_ready"], 1)
            dve.wait_ge(S["iota_ready"], 1)
            base = CHUNK_AT["gu", 0]

            def lo_gate_up(it, e, i):
                dve.wait_ge(S["gu_hi"], it * (4 * EG) + (4 * e + i + 1))
                lo(gus[:, i, LO, :, :, :].rearrange("p c k n -> p c (k n)"),
                   ring[:, (base + 2 * e) % SLOTS, :].rearrange("p (c i n) -> p i c n", c=2, i=4)[:, i, :, :],
                   gus[:, i, HI, :, :, :].rearrange("p c k n -> p c (k n)")).then_inc(S["gu_split"], 1)

            def lo_down(it, e):
                for i in range(2):
                    dve.wait_ge(S["dn_hi"], it * (2 * EG) + (2 * e + i + 1))
                    lo(dns2[:, i, LO, :], ring[:, (base + 2 * e + 1) % SLOTS, i * D:(i + 1) * D], dns2[:, i, HI, :])\
                        .then_inc(S["dn_split"], 1)

            def lo_gathered(it):
                dve.wait_ge(S["xg_hi"], it + 1)
                lo(xgs[:, LO, :, :], xg, xgs[:, HI, :, :]).then_inc(S["xg_split"], 1)

            def lo_hidden(it, e):
                dve.wait_ge(S["hidT_hi"], it * EG + (e + 1))
                lo(hidTs[:, e % 2, LO, :], ps[2 + e % 2][:, 0:2 * CAP], hidTs[:, e % 2, HI, :])\
                    .then_inc(S["hidT_split"], 1)

            def slots_of(m, b):
                r, g = b // NG, b % NG
                return V.tensor_scalar(ptok[:, m, b, :], iota, rank[:, TT * r + m:TT * r + m + 1],
                                       fgs[:, m, g:g + 1], ALU.is_equal, ALU.mult)

            for m in range(TT):
                slots_of(m, 0).then_inc(S["first_slots_ready"], 1)
            for i in range(4):
                lo_gate_up(0, 0, i)
            for m in range(TT):
                for b in range(1, BLOCKS):
                    step(slots_of(m, b))
            settle()
            V.memset(ptok[:, :, BLOCKS, :], 0.0).then_inc(S["ptok_ready"], 1)
            lo_gathered(0)
            dve.wait_ge(*filled("comb", 0))
            V.tensor_copy(wslot, bank("comb", 0)[:, 0:BLOCKS * EG]).then_inc(*read("comb", 0))
            dve.wait_ge(*drained("comb", 0))

            def add_back(m, at):
                dve.wait_ge(S["put_back"], at + (m + 1))
                for n in range(2):
                    part = tokA[:, m, 512 * n:512 * n + 512]
                    ins = V.tensor_tensor(part, part, ps[6 + n][:], ALU.add)
                    ins.then_inc(S["added_back"] if n else S["half_added_back"], 1)

            dve.wait_ge(*drained("sT", BLOCKS // 2 - 1))
            dve.sem_inc(S["added_back"], 1)
            turns = dve.value_load(turns_[0:1, 0:1], min_val=NG - 1, max_val=BLOCKS - 1)

            def block_of_tokens(it, is_last):
                for e in range(EG):
                    o, q = ps[e % 2], e % 2
                    more = not (is_last and e == EG - 1)
                    for i in range(4):
                        if i == 3:
                            dve.wait_ge(S["sg_ready"], it * EG + (e + 1))
                            V.tensor_tensor(sg[:, q, :], sg[:, q, :], o[:, 0:EF], ALU.mult).then_inc(S["silu_gate"], 1)
                            dve.wait_ge(S["silu_gate"], it * EG + (e + 1))
                            stt(hid[:, q, :], o[:, EF:2 * EF], wslot[:, bass.ds(it * EG + e, 1)], sg[:, q, :],
                                ALU.mult, ALU.mult).then_inc(S["hidden_ready"], 1)
                        if more:
                            lo_gate_up(it, e + 1, i)
                    if e >= 1:
                        lo_hidden(it, e - 1)
                    if e == 2:
                        add_back(0, it * 2)
                    if e == 4:
                        add_back(1, it * 2)
                    if e != 1:
                        lo_down(it, max(e - 1, 0))
                V.tensor_copy(pcur, pslot[:, bass.ds(it, 1), :].rearrange("p b n -> p (b n)"))\
                    .then_inc(S["pcur_ready"], 1)
                if not is_last:
                    lo_gathered(it + 1)
                lo_hidden(it, EG - 1)
                lo_down(it, EG - 1)

            with dve.Fori(0, turns) as it:
                block_of_tokens(it, False)
            block_of_tokens(turns, True)
            for m in range(TT):
                add_back(m, turns * 2 + 2)
            dve.wait_ge(S["added_back"], turns * 2 + 5)
            dve.sem_inc(S["res_ready"], 1)
            rms(0, 8)
            settle()
            dve.wait_ge(S["bc_rows_loaded"], 112)
            for m in range(TT):
                V.tensor_tensor(tokB[:, m, :], tokB[:, m, :], bcL[:, 0, :], ALU.mult).then_inc(S["out_ready"], 1)

        @block.gpsimd
        def _(pool):
            G = nc.gpsimd
            n_pool = [0]

            def link(ins):
                n_pool[0] += 1
                ins.then_inc(S["pool_chain"], 1)
                pool.wait_ge(S["pool_chain"], n_pool[0])

            b_in = a["b_in"][0]
            link(G.memset(ident[:], 0.0))
            G.affine_select(out=ident[:], in_=ident[:], compare_op=ALU.not_equal, fill=1.0, base=0,
                            pattern=[[-1, P]], channel_multiplier=1).then_inc(S["const_ready"], 1)
            link(G.memset(parity, 1.0))
            link(G.affine_select(out=parity, in_=parity, compare_op=ALU.is_ge, fill=0.0, base=-GRP,
                                 pattern=[[-2 * GRP, 4]], channel_multiplier=1))
            link(G.affine_select(out=parity, in_=parity, compare_op=ALU.is_ge, fill=0.0, base=2 * GRP - 1,
                                 pattern=[[2 * GRP, 4]], channel_multiplier=-1))
            link(G.tensor_tensor(parity[:, 0:2], parity[:, 0:2], parity[:, 2:4], ALU.add))
            link(G.tensor_tensor(odd, parity[:, 0:1], parity[:, 1:2], ALU.add))
            G.tensor_scalar(even, odd, -1.0, 1.0, ALU.mult, ALU.add).then_inc(S["const_ready"], 1)
            G.memset(bexp, 0.0).then_inc(S["bexp_zero"], 1)
            pool.dma_start(wif[:], a["w_in"][0, :, C_I:C_G].rearrange("(k p) n -> p k n", p=P),
                           allow_slow_non_contiguous=True).then_inc(S["small_loaded"], 16)
            pool.dma_start(wif2[:], a["w_in_2"][0, :, C2_GA:C2_GA + 8].rearrange("(k p) n -> p k n", p=P),
                           allow_slow_non_contiguous=True).then_inc(S["small_loaded"], 16)
            pool.dma_start(bif[:], b_in[C_I:C_G].rearrange("(c h) -> h c", c=2),
                           allow_slow_non_contiguous=True).then_inc(S["small_loaded"], 16)
            pool.dma_start(wr[:, :, 0:NG], a["w_group_2"][0].rearrange("(k p) n -> p k n", p=P),
                           allow_slow_non_contiguous=True).then_inc(S["small_loaded"], 16)
            pool.dma_start(wr[:, :, NG:NG + NE], a["w_router_2"][0].rearrange("(k p) n -> p k n", p=P),
                           allow_slow_non_contiguous=True).then_inc(S["small_loaded"], 16)
            pool.dma_start(p4[:, 0:1], a["A_log_2"][0].rearrange("(h a) -> h a", a=1),
                           allow_slow_non_contiguous=True).then_inc(S["small_loaded"], 16)
            pool.dma_start(p4[:, 1:2], a["dt_bias_2"][0].rearrange("(h a) -> h a", a=1),
                           allow_slow_non_contiguous=True).then_inc(S["small_loaded"], 16)
            for c, v in enumerate((a["ln0_g"], a["ln0_b"])):
                pool.dma_start(bc0[:, c, :], v.partition_broadcast(P)).then_inc(S["bc_rows_loaded"], 16)
            pool.dma_start(convR[:, 0:2 * D], b_in[C_V:C_I].partition_broadcast(P))\
                .then_inc(S["bcvo_loaded"], 16)
            G.memset(rowone[:], 1.0).then_inc(S["rowone_ready"], 1)
            G.memset(raw[:, :, 0:3], 0.0).then_inc(S["pads_ready"], 1)
            link(G.memset(sel[:], 1.0))
            link(G.affine_select(out=sel[:], in_=sel[:], compare_op=ALU.is_equal, fill=0.0, base=0,
                                 pattern=[[-1, HEADS], [0, P]], channel_multiplier=1))
            for m, base, op, fill in ((tri, 0, ALU.is_ge, 0.0), (stri, 0, ALU.is_gt, 0.0)):
                link(G.memset(m[:], 1.0))
                link(G.affine_select(out=m[:], in_=m[:], compare_op=op, fill=fill, base=base,
                                     pattern=[[1, P]], channel_multiplier=-1))
            link(G.memset(negm[:], 0.0))
            link(G.affine_select(out=negm[:], in_=negm[:], compare_op=ALU.is_ge, fill=NEG, base=0,
                                 pattern=[[-1, P]], channel_multiplier=1))
            link(G.memset(ones[:], 1.0))
            link(G.memset(rkeep[:], 1.0))
            for n, at in ((NG, 0), (EG, TT * NG)):
                link(G.memset(rkeep[:, at:at + TT * n].rearrange("p (m n) -> p m n", m=TT)[:, :, 0:1], 0.0))
            pool.wait_ge(*drained("xT", KT - 1))
            G.memset(vaug[:, :, :, DV:DV + 1], 1.0).then_inc(S["ones_column_ready"], 1)
            pool.wait_ge(S["bc_rows_loaded"], 32)
            for m in range(TT):
                link(G.tensor_tensor(tokA[:, m, :], tokA[:, m, :], bc0[:, 0, :], ALU.mult))
                link(G.tensor_tensor(tokA[:, m, :], tokA[:, m, :], bc0[:, 1, :], ALU.add))
            pool.sem_inc(S["h0_ready"], 1)
            for lv in range(LEVELS + 1):
                s = 1 << lv
                nb = P // s
                m = blk[:].rearrange("p (b n) -> p b n", n=s)
                link(G.memset(blk[:], 1.0))
                link(G.affine_select(out=m, in_=m, compare_op=ALU.is_ge, fill=0.0, base=0,
                                     pattern=[[-s, nb], [0, s]], channel_multiplier=1))
                link(G.affine_select(out=m, in_=m, compare_op=ALU.is_ge, fill=0.0, base=s - 1,
                                     pattern=[[s, nb], [0, s]], channel_multiplier=-1))
                if lv < LEVELS:
                    link(G.tensor_scalar(lvl[:, lv, :], blk[:], -1.0, None, ALU.mult))
                if lv:
                    link(G.tensor_tensor(lvl[:, lv - 1, :], lvl[:, lv - 1, :], blk[:], ALU.add))
            pool.sem_inc(S["masks_ready"], 1)
            pool.wait_ge(S["bcvo_loaded"], 16)
            for k in range(6):
                n = META if k % 3 == 0 else P
                c = k // 3
                pool.wait_ge(*drained("v", k))
                part = vaug[0:n, k % 3, 2 * c:2 * c + 2, 0:DV]
                G.tensor_tensor(part, part, bcvo[0:n, 0, 512 * c:512 * c + 512].rearrange("p (h n) -> p h n", h=2),
                                ALU.add).then_inc(S["v_biased"], 1)
            for k in range(4):
                c = k // 2
                pool.wait_ge(*drained("o", k))
                part = tokB[:, k % 2, 512 * c:512 * c + 512]
                G.tensor_tensor(part, part, bcvo[:, 1, 512 * c:512 * c + 512], ALU.add).then_inc(S["o_biased"], 1)
            pool.wait_ge(S["gated_ready"], 1)
            G.memset(zeros, 0.0).then_inc(S["zeros_ready"], 1)
            for c, v in enumerate((a["ln1_g"][0], a["ln1_b"][0])):
                pool.dma_start(bcL[:, c, :], v.partition_broadcast(P)).then_inc(S["bc_rows_loaded"], 16)
            pool.wait_ge(S["bc_rows_loaded"], 64)
            pool.wait_ge(S["xn_ready"], 2)
            for m in range(TT):
                link(G.tensor_tensor(tokA[:, m, :], tokB[:, m, :], bcL[:, 0, :], ALU.mult))
                link(G.tensor_tensor(tokA[:, m, :], tokA[:, m, :], bcL[:, 1, :], ALU.add))
                link(G.tensor_scalar(tokA[:, m, :], tokA[:, m, :], ALPHA, None, ALU.mult))
            pool.sem_inc(S["h1_ready"], 1)
            for c, v in enumerate((a["ln2_g"][0], a["ln2_b"][0])):
                pool.dma_start(bcL[:, c, :], v.partition_broadcast(P)).then_inc(S["bc_rows_loaded"], 16)
            pool.wait_ge(S["xn_ready"], 3)
            G.memset(graw[:, :, 0:3], 0.0).then_inc(S["pads_ready"], 1)
            link(G.tensor_copy(Tm, ident[:].unsqueeze(1).broadcast_to([P, 8, P])))
            G.tensor_copy(Tt, ident[:].unsqueeze(1).broadcast_to([P, 8, P])).then_inc(S["T_init"], 1)
            wd = a["w_down_2"][0].rearrange("g e (k p) n -> (g e) p k n", p=P)

            def load_down(e, q):
                s = CHUNK_AT["dn", q] % SLOTS
                pool.dma_start(ring[:, s, 0:2048].rearrange("p (k n) -> p k n", n=D),
                               wd[bass.ds(e, 1)].squeeze(0)).then_inc(S[f"down{q}_loaded"], 16)

            for q, tenant in ((0, ("gz", 0)), (1, ("wout", 1))):
                assert (CHUNK_AT[tenant] - CHUNK_AT["dn", q]) % SLOTS == 0
                pool.wait_ge(*filled(tenant[0], 3))
                load_down(q, q)
            pool.wait_ge(S["xn_ready"], 4)
            G.iota(iota, pattern=[[1, CAP]], base=0, channel_multiplier=0, allow_small_or_imprecise_dtypes=True)\
                .then_inc(S["iota_ready"], 1)
            G.memset(yg, 0.0).then_inc(S["yg_ready"], 1)
            G.memset(pcur, 0.0).then_inc(S["pcur_ready"], 1)
            pool.dma_start(bcL[:, 0, :], a["final_norm_2"].partition_broadcast(P)).then_inc(S["bc_rows_loaded"], 16)
            pool.wait_ge(S["turns_ready"], 1)
            turns = pool.value_load(turns_[0:1, 0:1], min_val=NG - 1, max_val=BLOCKS - 1)
            with pool.Fori(1, turns * (EG // 2) + EG // 2) as it:
                pair = it % (NE // 2)
                for q in range(2):
                    pool.wait_ge(S["dn_split"], it * 4 + 2 * (q - 1))
                    load_down(pair * 2 + q, q)


_INS = ["x", "meta_tokens", "ln0_g", "ln0_b", "w_in", "b_in", "qk_conv_w", "qk_conv_b", "s5_lambda_re",
        "s5_lambda_im", "s5_log_dt", "s5_b_re", "s5_b_im", "s5_c_re", "s5_c_im", "s5_d", "s5_w_glu", "m_norm_g",
        "m_w_out", "w_o", "ln1_g", "ln1_b", "w_up", "b_up", "w_down", "ln2_g", "ln2_b", "attn_norm_2", "w_in_2",
        "conv_w_2", "A_log_2", "dt_bias_2", "gdn_norm_2", "w_out_2", "ffn_norm_2", "w_group_2", "w_router_2",
        "w_gate_2", "w_up_2", "w_down_2", "final_norm_2"]


def kernel(**inputs):
    import numpy as np
    import concourse.bacc as bacc
    from concourse.bass_utils import run_bass_kernel_spmd

    nc = bacc.Bacc("TRN2", target_bir_lowering=False, num_devices=1)
    arrays, args = {}, {}
    for name in _INS:
        v = np.ascontiguousarray(inputs[name])
        arrays[f"in_{name}"] = v
        args[name] = nc.dram_tensor(f"in_{name}", v.shape, mybir.dt.from_np(v.dtype), kind="ExternalInput").ap()
    args["out"] = nc.dram_tensor("out", (1, SEQ, D), FP32, kind="ExternalOutput").ap()
    build(nc, args)
    r = run_bass_kernel_spmd(nc, [arrays], core_ids=[0])
    return r.results[0]["out"]
```
